# Optimizing a Trainium2 kernel written in Bass

```python
import jax, jax.numpy as jnp
from jax import lax
import numpy as np
import math
import jax
import jax.numpy as jnp

D_MODEL = 1024
BATCH = 1
SEQ = 512
DEPTH = 2

N_MIXERS = 2
N_POOL_LAYERS = (DEPTH + 1) // 2
N_MLA_LAYERS = DEPTH // 2

POOL_WINDOWS = (2, 4, 8, 16)
N_POOL_GROUPS = len(POOL_WINDOWS)
POOL_GROUP = D_MODEL // N_POOL_GROUPS

N_HEADS = D_MODEL // 128
QK_NOPE_DIM = 128
QK_ROPE_DIM = 64
V_HEAD_DIM = 128
Q_LORA_RANK = 3 * D_MODEL // 8
KV_LORA_RANK = D_MODEL // 8
QK_HEAD_DIM = QK_NOPE_DIM + QK_ROPE_DIM
ROPE_THETA = 10000.0
Q_BLOCK = 128

D_FF = ((8 * D_MODEL // 3 + 255) // 256) * 256

RMS_EPS = 1e-6


def rms_norm(x, g):
    xf = x.astype(jnp.float32)
    y = xf * lax.rsqrt(jnp.mean(xf * xf, axis=-1, keepdims=True) + RMS_EPS)
    return (y * g.astype(jnp.float32)).astype(x.dtype)

def pool_mixer(h, w, scale):
    B, S, D = h.shape
    hf = h.astype(jnp.float32).reshape(B, S, N_POOL_GROUPS, POOL_GROUP)
    cs = jnp.cumsum(hf, axis=1)
    n_avail = jnp.arange(1, S + 1, dtype=jnp.float32)
    outs = []
    for g, win in enumerate(POOL_WINDOWS):
        c = cs[:, :, g]
        lag = jnp.pad(c[:, :-win], ((0, 0), (win, 0), (0, 0)))
        mean = (c - lag) / jnp.minimum(n_avail, float(win))[:, None]
        outs.append(mean - hf[:, :, g])
    p = jnp.stack(outs, axis=2).astype(h.dtype)
    y = jnp.einsum('bsgc,gcd->bsgd', p, w).reshape(B, S, D)
    return y * scale

def rope_tables(positions):
    inv = 1.0 / (ROPE_THETA ** (jnp.arange(0, QK_ROPE_DIM, 2, dtype=jnp.float32) / QK_ROPE_DIM))
    ang = positions.astype(jnp.float32)[..., None] * inv
    return jnp.cos(ang), jnp.sin(ang)

def apply_rope(x, cos, sin):
    xf = x.astype(jnp.float32)
    half = QK_ROPE_DIM // 2
    x1, x2 = xf[..., :half], xf[..., half:]
    return jnp.concatenate([x1 * cos - x2 * sin, x2 * cos + x1 * sin], axis=-1).astype(x.dtype)

def causal_attention(q, k, v):
    B, S, H, Dq = q.shape
    nb = S // Q_BLOCK
    qb = q.reshape(B, nb, Q_BLOCK, H, Dq).transpose(1, 0, 2, 3, 4)
    key_pos = jnp.arange(S)
    sm_scale = Dq ** -0.5

    def one_block(args):
        blk, qi = args
        s = jnp.einsum('bqhd,bkhd->bhqk', qi, k).astype(jnp.float32) * sm_scale
        q_pos = blk * Q_BLOCK + jnp.arange(Q_BLOCK)
        mask = key_pos[None, :] <= q_pos[:, None]
        s = jnp.where(mask, s, -jnp.inf)
        p = jax.nn.softmax(s, axis=-1).astype(v.dtype)
        return jnp.einsum('bhqk,bkhd->bqhd', p, v)

    o = lax.map(one_block, (jnp.arange(nb), qb))
    return o.transpose(1, 0, 2, 3, 4).reshape(B, S, H, v.shape[-1])

def mla(h, cos, sin, w_down, q_norm, w_uq, kv_norm, w_ukv, w_o):
    B, S, _ = h.shape
    d = h @ w_down
    cq = rms_norm(d[..., :Q_LORA_RANK], q_norm)
    ckv = rms_norm(d[..., Q_LORA_RANK:Q_LORA_RANK + KV_LORA_RANK], kv_norm)
    k_rope = apply_rope(d[..., Q_LORA_RANK + KV_LORA_RANK:], cos, sin)
    q = (cq @ w_uq).reshape(B, S, N_HEADS, QK_HEAD_DIM)
    q_rope = apply_rope(q[..., QK_NOPE_DIM:], cos[:, :, None], sin[:, :, None])
    q = jnp.concatenate([q[..., :QK_NOPE_DIM], q_rope], axis=-1)
    kv = (ckv @ w_ukv).reshape(B, S, N_HEADS, QK_NOPE_DIM + V_HEAD_DIM)
    k = jnp.concatenate(
        [kv[..., :QK_NOPE_DIM],
         jnp.broadcast_to(k_rope[:, :, None, :], (B, S, N_HEADS, QK_ROPE_DIM))], axis=-1)
    v = kv[..., QK_NOPE_DIM:]
    o = causal_attention(q, k, v)
    return o.reshape(B, S, N_HEADS * V_HEAD_DIM) @ w_o

def swiglu(h, w_gate, w_up, w_down):
    return (jax.nn.silu(h @ w_gate) * (h @ w_up)) @ w_down

def first_inputs(seed: int = 0) -> dict:
    key = jax.random.key(seed)
    ks = jax.random.split(key, 16)
    f32 = jnp.float32

    def nrm(k, shape, fan_in):
        return jax.random.normal(k, shape, f32) * (fan_in ** -0.5)

    def gain(k, shape):
        return 1.0 + 0.02 * jax.random.normal(k, shape, f32)

    x = jax.random.normal(ks[0], (BATCH, SEQ, D_MODEL), f32)
    positions = jnp.broadcast_to(jnp.arange(SEQ, dtype=jnp.int32)[None, :], (BATCH, SEQ))
    return {
        "x": x,
        "positions": positions,
        "norm_mix": gain(ks[1], (DEPTH, D_MODEL)),
        "norm_ffn": gain(ks[2], (DEPTH, D_MODEL)),
        "norm_final": gain(ks[3], (D_MODEL,)),
        "pool_w": nrm(ks[4], (N_POOL_LAYERS, N_POOL_GROUPS, POOL_GROUP, POOL_GROUP), POOL_GROUP),
        "pool_scale": gain(ks[5], (N_POOL_LAYERS, D_MODEL)),
        "mla_w_down": nrm(ks[6], (N_MLA_LAYERS, D_MODEL, Q_LORA_RANK + KV_LORA_RANK + QK_ROPE_DIM), D_MODEL),
        "mla_q_norm": gain(ks[7], (N_MLA_LAYERS, Q_LORA_RANK)),
        "mla_w_uq": nrm(ks[8], (N_MLA_LAYERS, Q_LORA_RANK, N_HEADS * QK_HEAD_DIM), Q_LORA_RANK),
        "mla_kv_norm": gain(ks[9], (N_MLA_LAYERS, KV_LORA_RANK)),
        "mla_w_ukv": nrm(ks[10], (N_MLA_LAYERS, KV_LORA_RANK, N_HEADS * (QK_NOPE_DIM + V_HEAD_DIM)), KV_LORA_RANK),
        "mla_w_o": nrm(ks[11], (N_MLA_LAYERS, N_HEADS * V_HEAD_DIM, D_MODEL), N_HEADS * V_HEAD_DIM),
        "ffn_w_gate": nrm(ks[12], (DEPTH, D_MODEL, D_FF), D_MODEL),
        "ffn_w_up": nrm(ks[13], (DEPTH, D_MODEL, D_FF), D_MODEL),
        "ffn_w_down": nrm(ks[14], (DEPTH, D_FF, D_MODEL), D_FF),
    }

def first_block(x, positions, norm_mix, norm_ffn, norm_final, pool_w, pool_scale,
              mla_w_down, mla_q_norm, mla_w_uq, mla_kv_norm, mla_w_ukv, mla_w_o,
              ffn_w_gate, ffn_w_up, ffn_w_down):
    cos, sin = rope_tables(positions)
    for i in range(DEPTH):
        h = rms_norm(x, norm_mix[i])
        j = i // N_MIXERS
        if i % N_MIXERS == 0:
            x = x + pool_mixer(h, pool_w[j], pool_scale[j])
        else:
            x = x + mla(h, cos, sin, mla_w_down[j], mla_q_norm[j], mla_w_uq[j],
                        mla_kv_norm[j], mla_w_ukv[j], mla_w_o[j])
        h = rms_norm(x, norm_ffn[i])
        x = x + swiglu(h, ffn_w_gate[i], ffn_w_up[i], ffn_w_down[i])
    return rms_norm(x, norm_final)


DEPTH_2 = 1

N_MIXERS_2 = 4
QBLOCK = 128
NORM_EPS = 1e-6
NEG_BIG = -1e30
F32 = jnp.float32
DA_HEADS = 8
DA_HEAD_DIM = 64
DA_IN_WIDTH = 3 * DA_HEADS * 2 * DA_HEAD_DIM
NSA_HEADS = 16
NSA_KV_GROUPS = 2
NSA_HEAD_DIM = 64
NSA_QBLOCK = 64
CMP_BLOCK = 32
CMP_STRIDE = 16
CMP_HIDDEN = 256
SEL_BLOCK = 64
N_SELECT = 8
WINDOW = 512
NSA_IN_WIDTH = NSA_HEADS * NSA_HEAD_DIM + 6 * NSA_KV_GROUPS * NSA_HEAD_DIM + 3 * NSA_HEADS
GDN_HEADS = 8
GDN_HEAD_DIM = 128
GDN_CHUNK = 64
GDN_IN_WIDTH = 4 * GDN_HEADS * GDN_HEAD_DIM + 2 * GDN_HEADS
CONV_WIDTH = 4
LRU_WIDTH = D_MODEL
LRU_BLOCKS = 4
LRU_C = 8.0
N_GROUPS = 4
EXPERTS_PER_GROUP = 4
N_EXPERTS = N_GROUPS * EXPERTS_PER_GROUP
TOP_K_IN_GROUP = 2
D_EXPERT = 512


def rmsnorm(x, gain):
    xf = x.astype(F32)
    y = xf * lax.rsqrt(jnp.mean(xf * xf, -1, keepdims=True) + NORM_EPS)
    return (y * gain.astype(F32)).astype(x.dtype)

def l2norm(x):
    xf = x.astype(F32)
    return xf * lax.rsqrt(jnp.sum(xf * xf, -1, keepdims=True) + NORM_EPS)

def alibi_slopes(n):
    return jnp.asarray(2.0 ** (-8.0 * np.arange(1, n + 1) / n), dtype=F32)

def causal_depthwise_conv(x, w):
    k = w.shape[0]
    xp = jnp.pad(x, ((0, 0), (k - 1, 0), (0, 0)))
    return lax.conv_general_dilated(xp, w[:, None, :].astype(x.dtype), window_strides=(1,), padding='VALID',
                                    dimension_numbers=('NWC', 'WIO', 'NWC'), feature_group_count=x.shape[-1])

def diff_attention(x, w_in, q_gain, k_gain, lq1, lk1, lq2, lk2, subln, w_out, lambda_init):
    B, T, _ = x.shape
    H, dh = DA_HEADS, DA_HEAD_DIM
    q, k, v = jnp.split(x @ w_in, [2 * H * dh, 4 * H * dh], axis=-1)
    q = rmsnorm(q.reshape(B, T, H, 2, dh), q_gain) * (dh ** -0.5)
    k = rmsnorm(k.reshape(B, T, H, 2, dh), k_gain)
    v = v.reshape(B, T, H, 2 * dh)
    lam = (jnp.exp(jnp.sum(lq1.astype(F32) * lk1.astype(F32)))
           - jnp.exp(jnp.sum(lq2.astype(F32) * lk2.astype(F32))) + lambda_init)
    slopes = alibi_slopes(H)
    outs = []
    for s in range(0, T, QBLOCK):
        e = s + QBLOCK
        sc = jnp.einsum('bqhcd,bkhcd->bhcqk', q[:, s:e], k[:, :e]).astype(F32)
        dist = (jnp.arange(s, e)[:, None] - jnp.arange(e)[None, :]).astype(F32)
        sc = jnp.where(dist >= 0, sc - slopes[:, None, None, None] * dist, -jnp.inf)
        p = jax.nn.softmax(sc, axis=-1)
        pd = p[:, :, 0] - lam * p[:, :, 1]
        outs.append(jnp.einsum('bhqk,bkhe->bqhe', pd.astype(v.dtype), v[:, :e]))
    o = rmsnorm(jnp.concatenate(outs, axis=1), subln) * (1.0 - lambda_init)
    return o.reshape(B, T, H * 2 * dh) @ w_out

def nsa_attention(x, w_in, q_gain, k_gains, cmp_pos, cmp_w1, cmp_w2, w_out):
    B, T, _ = x.shape
    H, G, dh = NSA_HEADS, NSA_KV_GROUPS, NSA_HEAD_DIM
    P = H // G
    kvw = G * dh
    cuts = np.cumsum([H * dh] + [kvw] * 6).tolist()
    q, kc, vc, ks, vs, kw, vw, gl = jnp.split(x @ w_in, cuts, axis=-1)
    q = (rmsnorm(q.reshape(B, T, H, dh), q_gain) * (dh ** -0.5)).reshape(B, T, G, P, dh)
    gates = jax.nn.sigmoid(gl.reshape(B, T, G, P, 3))
    n_cmp = (T - CMP_BLOCK) // CMP_STRIDE + 1
    cidx = np.arange(n_cmp)[:, None] * CMP_STRIDE + np.arange(CMP_BLOCK)[None, :]

    def compress(t, c):
        tb = t.reshape(B, T, G, dh)[:, cidx] + cmp_pos[c][:, None, :]
        tb = tb.transpose(0, 1, 3, 2, 4).reshape(B, n_cmp, G, CMP_BLOCK * dh)
        return jax.nn.silu(tb @ cmp_w1[c]) @ cmp_w2[c]

    kcmp = rmsnorm(compress(kc, 0), k_gains[0])
    vcmp = compress(vc, 1)
    cmp_end = jnp.asarray(cidx[:, -1])
    n_sel = T // SEL_BLOCK
    k_top = min(N_SELECT, n_sel)

    def to_blocks(t):
        return t.reshape(B, n_sel, SEL_BLOCK, G, dh).transpose(0, 3, 1, 2, 4)

    ksb = to_blocks(rmsnorm(ks.reshape(B, T, G, dh), k_gains[1]))
    vsb = to_blocks(vs)
    cs = np.arange(n_cmp) * CMP_STRIDE
    ss0 = np.arange(n_sel) * SEL_BLOCK
    overlap = jnp.asarray(((cs[:, None] < ss0[None, :] + SEL_BLOCK)
                           & (cs[:, None] + CMP_BLOCK > ss0[None, :])).astype(np.float32))
    kwin = rmsnorm(kw.reshape(B, T, G, dh), k_gains[2])
    vwin = vw.reshape(B, T, G, dh)
    slopes = alibi_slopes(H).reshape(G, P)
    gather = jax.vmap(jax.vmap(lambda blocks, idx: blocks[idx]))
    blk_ids = jnp.arange(n_sel)
    outs = []
    for s in range(0, T, NSA_QBLOCK):
        e = s + NSA_QBLOCK
        qb = q[:, s:e]
        tpos = jnp.arange(s, e)
        dist_c = (tpos[:, None] - cmp_end[None, :]).astype(F32)
        valid_c = dist_c >= 0
        sc = jnp.einsum('bqgpd,bcgd->bgpqc', qb, kcmp).astype(F32) - slopes[:, :, None, None] * dist_c
        p_c = jax.nn.softmax(jnp.where(valid_c, sc, NEG_BIG), -1) * valid_c
        o_cmp = jnp.einsum('bgpqc,bcgd->bqgpd', p_c.astype(vcmp.dtype), vcmp)
        imp = jnp.einsum('bgpqc,cn->bgqn', p_c, overlap)
        qblk = tpos // SEL_BLOCK
        forced = (blk_ids[None, :] == 0) | (blk_ids[None, :] == qblk[:, None])
        future = blk_ids[None, :] > qblk[:, None]
        score = jnp.where(forced, 1e4, jnp.where(future, -1.0, imp))
        _, sel = lax.top_k(score, k_top)
        kg = gather(ksb, sel)
        vg = gather(vsb, sel)
        dist_s = (tpos[None, None, :, None, None]
                  - (sel[..., None] * SEL_BLOCK + jnp.arange(SEL_BLOCK))).astype(F32)
        ssc = (jnp.einsum('bqgpd,bgqksd->bgpqks', qb, kg).astype(F32)
               - slopes[None, :, :, None, None, None] * dist_s[:, :, None])
        ssc = jnp.where(dist_s[:, :, None] >= 0, ssc, -jnp.inf)
        p_s = jax.nn.softmax(ssc.reshape(B, G, P, NSA_QBLOCK, k_top * SEL_BLOCK), -1)
        o_sel = jnp.einsum('bgpqn,bgqnd->bqgpd', p_s.astype(vg.dtype),
                           vg.reshape(B, G, NSA_QBLOCK, k_top * SEL_BLOCK, dh))
        ws = max(0, s - WINDOW + 1)
        dist_w = (tpos[:, None] - jnp.arange(ws, e)[None, :]).astype(F32)
        valid_w = (dist_w >= 0) & (dist_w < WINDOW)
        swc = jnp.einsum('bqgpd,bkgd->bgpqk', qb, kwin[:, ws:e]).astype(F32) - slopes[:, :, None, None] * dist_w
        p_w = jax.nn.softmax(jnp.where(valid_w, swc, -jnp.inf), -1)
        o_win = jnp.einsum('bgpqk,bkgd->bqgpd', p_w.astype(vwin.dtype), vwin[:, ws:e])
        gb = gates[:, s:e]
        outs.append(gb[..., 0:1] * o_cmp + gb[..., 1:2] * o_sel + gb[..., 2:3] * o_win)
    o = jnp.concatenate(outs, axis=1).reshape(B, T, H * dh)
    return o @ w_out

def gated_deltanet(x, w_in, conv_w, a_log, dt_bias, out_gain, w_out):
    B, T, _ = x.shape
    H, dk = GDN_HEADS, GDN_HEAD_DIM
    C = GDN_CHUNK
    n = T // C
    W = H * dk
    qkv, z, b, a = jnp.split(x @ w_in, [3 * W, 4 * W, 4 * W + H], axis=-1)
    qkv = jax.nn.silu(causal_depthwise_conv(qkv, conv_w))
    q, k, v = jnp.split(qkv, 3, axis=-1)
    q = l2norm(q.reshape(B, T, H, dk)) * (dk ** -0.5)
    k = l2norm(k.reshape(B, T, H, dk))
    v = v.reshape(B, T, H, dk).astype(F32)
    beta = jax.nn.sigmoid(b.astype(F32))
    g = -jnp.exp(a_log.astype(F32)) * jax.nn.softplus(a.astype(F32) + dt_bias.astype(F32))

    def chunks(t):
        return jnp.moveaxis(t.reshape(B, n, C, H, *t.shape[3:]), 3, 1)

    q, k, v, beta, g = chunks(q), chunks(k), chunks(v), chunks(beta), chunks(g)
    gc = jnp.cumsum(g, axis=-1)
    tril = jnp.tril(jnp.ones((C, C), bool))
    decay = jnp.exp(jnp.where(tril, gc[..., :, None] - gc[..., None, :], -jnp.inf))
    kb = k * beta[..., None]
    lmat = jnp.einsum('bhnid,bhnjd->bhnij', kb, k) * decay * jnp.tril(jnp.ones((C, C), F32), -1)
    ia = lmat + jnp.eye(C, dtype=F32)
    u = lax.linalg.triangular_solve(ia, v * beta[..., None], left_side=True, lower=True, unit_diagonal=True)
    w = lax.linalg.triangular_solve(ia, kb * jnp.exp(gc)[..., None], left_side=True, lower=True, unit_diagonal=True)
    aqk = jnp.einsum('bhnid,bhnjd->bhnij', q, k) * decay

    def step(S, inp):
        qc, kc, uc, wc, gcc, aq = inp
        v_new = uc - jnp.einsum('bhck,bhkv->bhcv', wc, S)
        o = (jnp.einsum('bhck,bhkv->bhcv', qc * jnp.exp(gcc)[..., None], S)
             + jnp.einsum('bhij,bhjv->bhiv', aq, v_new))
        glast = gcc[..., -1:]
        S = S * jnp.exp(glast)[..., None] + jnp.einsum('bhck,bhcv->bhkv', kc * jnp.exp(glast - gcc)[..., None], v_new)
        return S, o

    xs = (jnp.moveaxis(q, 2, 0), jnp.moveaxis(k, 2, 0), jnp.moveaxis(u, 2, 0),
          jnp.moveaxis(w, 2, 0), jnp.moveaxis(gc, 2, 0), jnp.moveaxis(aqk, 2, 0))
    _, o = lax.scan(step, jnp.zeros((B, H, dk, dk), F32), xs)
    o = o.transpose(1, 0, 3, 2, 4).reshape(B, T, H, dk)
    o = rmsnorm(o, out_gain) * jax.nn.silu(z.reshape(B, T, H, dk).astype(F32))
    return o.astype(x.dtype).reshape(B, T, W) @ w_out

def rg_lru_block(x, w_in, conv_w, conv_b, w_a, b_a, w_x, b_x, lam, w_out):
    B, T, _ = x.shape
    gate, rec = jnp.split(x @ w_in, 2, axis=-1)
    gate = jax.nn.gelu(gate, approximate=True)
    xr = causal_depthwise_conv(rec, conv_w) + conv_b
    xb = xr.reshape(B, T, LRU_BLOCKS, -1)
    r = jax.nn.sigmoid((jnp.einsum('btnc,ncd->btnd', xb, w_a).reshape(B, T, -1) + b_a).astype(F32))
    i = jax.nn.sigmoid((jnp.einsum('btnc,ncd->btnd', xb, w_x).reshape(B, T, -1) + b_x).astype(F32))
    log_a = -LRU_C * r * jax.nn.softplus(-lam.astype(F32))
    a = jnp.exp(log_a)
    bterm = jnp.sqrt(1.0 - jnp.exp(2.0 * log_a)) * (i * xr.astype(F32))
    _, h = lax.associative_scan(lambda c1, c2: (c1[0] * c2[0], c2[0] * c1[1] + c2[1]), (a, bterm), axis=1)
    return (h.astype(x.dtype) * gate) @ w_out

def hier_moe(x, w_group, b_group, w_router, b_router, w_gate, w_up, w_down):
    B, T, D = x.shape
    n_tok = B * T
    xt = x.reshape(n_tok, D)
    logit_g = (xt @ w_group + b_group).astype(F32)
    prob_g = jax.nn.softmax(logit_g, -1)
    g_sel = jnp.argmax(logit_g, -1)
    gate_g = jnp.take_along_axis(prob_g, g_sel[:, None], -1)
    logit_e = (xt @ w_router + b_router).astype(F32).reshape(n_tok, N_GROUPS, EXPERTS_PER_GROUP)
    logit_e = jnp.take_along_axis(logit_e, g_sel[:, None, None], 1)[:, 0]
    top_v, top_i = lax.top_k(jax.nn.softmax(logit_e, -1), TOP_K_IN_GROUP)
    top_v = top_v / jnp.sum(top_v, -1, keepdims=True)
    w_in_group = jnp.sum(jax.nn.one_hot(top_i, EXPERTS_PER_GROUP, dtype=F32) * top_v[..., None], 1) * gate_g
    combine = jax.nn.one_hot(g_sel, N_GROUPS, dtype=F32)[:, :, None] * w_in_group[:, None, :]
    y = jnp.zeros_like(xt)
    for g in range(N_GROUPS):
        e = slice(g * EXPERTS_PER_GROUP, (g + 1) * EXPERTS_PER_GROUP)
        h = jax.nn.silu(jnp.einsum('nd,edf->nef', xt, w_gate[e])) * jnp.einsum('nd,edf->nef', xt, w_up[e])
        h = h * combine[:, g, :, None].astype(h.dtype)
        y = y + jnp.einsum('nef,efd->nd', h, w_down[e])
    return y.reshape(B, T, D)

def second_inputs(seed: int = 0) -> dict:
    key = jax.random.key(seed)
    keys = iter(jax.random.split(key, 48))

    def normal(shape, scale):
        return jax.random.normal(next(keys), shape, F32) * scale

    def gain(shape):
        return 1.0 + normal(shape, 0.02)

    def uniform(shape, lo, hi):
        return jax.random.uniform(next(keys), shape, F32, minval=lo, maxval=hi)

    nA, nB, nC, nD = [len(range(m, DEPTH_2, N_MIXERS_2)) for m in range(N_MIXERS_2)]
    D = D_MODEL
    rs = (2 * DEPTH_2) ** -0.5
    x = normal((BATCH, SEQ, D), 1.0)
    norm_mix = gain((DEPTH_2, D))
    norm_ffn = gain((DEPTH_2, D))
    da_w_in = normal((nA, D, DA_IN_WIDTH), D ** -0.5)
    da_q_norm = gain((nA, DA_HEAD_DIM))
    da_k_norm = gain((nA, DA_HEAD_DIM))
    da_lambda_q1 = normal((nA, DA_HEAD_DIM), 0.1)
    da_lambda_k1 = normal((nA, DA_HEAD_DIM), 0.1)
    da_lambda_q2 = normal((nA, DA_HEAD_DIM), 0.1)
    da_lambda_k2 = normal((nA, DA_HEAD_DIM), 0.1)
    da_subln = gain((nA, 2 * DA_HEAD_DIM))
    da_w_out = normal((nA, DA_HEADS * 2 * DA_HEAD_DIM, D), (DA_HEADS * 2 * DA_HEAD_DIM) ** -0.5 * rs)
    nsa_w_in = normal((nB, D, NSA_IN_WIDTH), D ** -0.5)
    nsa_q_norm = gain((nB, NSA_HEAD_DIM))
    nsa_k_norm = gain((nB, 3, NSA_HEAD_DIM))
    nsa_cmp_pos = normal((nB, 2, CMP_BLOCK, NSA_HEAD_DIM), 0.1)
    nsa_cmp_w1 = normal((nB, 2, CMP_BLOCK * NSA_HEAD_DIM, CMP_HIDDEN), (CMP_BLOCK * NSA_HEAD_DIM) ** -0.5)
    nsa_cmp_w2 = normal((nB, 2, CMP_HIDDEN, NSA_HEAD_DIM), CMP_HIDDEN ** -0.5)
    nsa_w_out = normal((nB, NSA_HEADS * NSA_HEAD_DIM, D), (NSA_HEADS * NSA_HEAD_DIM) ** -0.5 * rs)
    gdn_w_in = normal((nC, D, GDN_IN_WIDTH), D ** -0.5)
    gdn_conv_w = normal((nC, CONV_WIDTH, 3 * GDN_HEADS * GDN_HEAD_DIM), CONV_WIDTH ** -0.5)
    gdn_a_log = jnp.log(uniform((nC, GDN_HEADS), 1.0, 16.0))
    dt = jnp.exp(uniform((nC, GDN_HEADS), math.log(1e-3), math.log(0.1)))
    gdn_dt_bias = dt + jnp.log(-jnp.expm1(-dt))
    gdn_out_norm = gain((nC, GDN_HEAD_DIM))
    gdn_w_out = normal((nC, GDN_HEADS * GDN_HEAD_DIM, D), (GDN_HEADS * GDN_HEAD_DIM) ** -0.5 * rs)
    bw = LRU_WIDTH // LRU_BLOCKS
    lru_w_in = normal((nD, D, 2 * LRU_WIDTH), D ** -0.5)
    lru_conv_w = normal((nD, CONV_WIDTH, LRU_WIDTH), CONV_WIDTH ** -0.5)
    lru_conv_b = normal((nD, LRU_WIDTH), 0.1)
    lru_w_a = normal((nD, LRU_BLOCKS, bw, bw), bw ** -0.5)
    lru_b_a = normal((nD, LRU_WIDTH), 0.1)
    lru_w_x = normal((nD, LRU_BLOCKS, bw, bw), bw ** -0.5)
    lru_b_x = normal((nD, LRU_WIDTH), 0.1)
    a_c = uniform((nD, LRU_WIDTH), 0.9, 0.999)
    a0 = a_c ** (1.0 / LRU_C)
    lru_lambda = jnp.log(a0) - jnp.log1p(-a0)
    lru_w_out = normal((nD, LRU_WIDTH, D), LRU_WIDTH ** -0.5 * rs)
    moe_w_group = normal((DEPTH_2, D, N_GROUPS), D ** -0.5)
    moe_b_group = normal((DEPTH_2, N_GROUPS), 0.01)
    moe_w_router = normal((DEPTH_2, D, N_EXPERTS), D ** -0.5)
    moe_b_router = normal((DEPTH_2, N_EXPERTS), 0.01)
    moe_w_gate = normal((DEPTH_2, N_EXPERTS, D, D_EXPERT), D ** -0.5)
    moe_w_up = normal((DEPTH_2, N_EXPERTS, D, D_EXPERT), D ** -0.5)
    moe_w_down = normal((DEPTH_2, N_EXPERTS, D_EXPERT, D), D_EXPERT ** -0.5 * rs)
    return {'x': x, 'norm_mix': norm_mix, 'norm_ffn': norm_ffn,
            'da_w_in': da_w_in, 'da_q_norm': da_q_norm, 'da_k_norm': da_k_norm,
            'da_lambda_q1': da_lambda_q1, 'da_lambda_k1': da_lambda_k1,
            'da_lambda_q2': da_lambda_q2, 'da_lambda_k2': da_lambda_k2,
            'da_subln': da_subln, 'da_w_out': da_w_out,
            'nsa_w_in': nsa_w_in, 'nsa_q_norm': nsa_q_norm, 'nsa_k_norm': nsa_k_norm,
            'nsa_cmp_pos': nsa_cmp_pos, 'nsa_cmp_w1': nsa_cmp_w1, 'nsa_cmp_w2': nsa_cmp_w2,
            'nsa_w_out': nsa_w_out,
            'gdn_w_in': gdn_w_in, 'gdn_conv_w': gdn_conv_w, 'gdn_a_log': gdn_a_log,
            'gdn_dt_bias': gdn_dt_bias, 'gdn_out_norm': gdn_out_norm, 'gdn_w_out': gdn_w_out,
            'lru_w_in': lru_w_in, 'lru_conv_w': lru_conv_w, 'lru_conv_b': lru_conv_b,
            'lru_w_a': lru_w_a, 'lru_b_a': lru_b_a, 'lru_w_x': lru_w_x, 'lru_b_x': lru_b_x,
            'lru_lambda': lru_lambda, 'lru_w_out': lru_w_out,
            'moe_w_group': moe_w_group, 'moe_b_group': moe_b_group,
            'moe_w_router': moe_w_router, 'moe_b_router': moe_b_router,
            'moe_w_gate': moe_w_gate, 'moe_w_up': moe_w_up, 'moe_w_down': moe_w_down}

def second_block(x, norm_mix, norm_ffn,
              da_w_in, da_q_norm, da_k_norm, da_lambda_q1, da_lambda_k1, da_lambda_q2, da_lambda_k2,
              da_subln, da_w_out,
              nsa_w_in, nsa_q_norm, nsa_k_norm, nsa_cmp_pos, nsa_cmp_w1, nsa_cmp_w2, nsa_w_out,
              gdn_w_in, gdn_conv_w, gdn_a_log, gdn_dt_bias, gdn_out_norm, gdn_w_out,
              lru_w_in, lru_conv_w, lru_conv_b, lru_w_a, lru_b_a, lru_w_x, lru_b_x, lru_lambda, lru_w_out,
              moe_w_group, moe_b_group, moe_w_router, moe_b_router, moe_w_gate, moe_w_up, moe_w_down):
    for i in range(DEPTH_2):
        m, j = i % N_MIXERS_2, i // N_MIXERS_2
        h = rmsnorm(x, norm_mix[i])
        if m == 0:
            y = diff_attention(h, da_w_in[j], da_q_norm[j], da_k_norm[j], da_lambda_q1[j], da_lambda_k1[j],
                               da_lambda_q2[j], da_lambda_k2[j], da_subln[j], da_w_out[j],
                               0.8 - 0.6 * math.exp(-0.3 * i))
        elif m == 1:
            y = nsa_attention(h, nsa_w_in[j], nsa_q_norm[j], nsa_k_norm[j], nsa_cmp_pos[j],
                              nsa_cmp_w1[j], nsa_cmp_w2[j], nsa_w_out[j])
        elif m == 2:
            y = gated_deltanet(h, gdn_w_in[j], gdn_conv_w[j], gdn_a_log[j], gdn_dt_bias[j],
                               gdn_out_norm[j], gdn_w_out[j])
        else:
            y = rg_lru_block(h, lru_w_in[j], lru_conv_w[j], lru_conv_b[j], lru_w_a[j], lru_b_a[j],
                             lru_w_x[j], lru_b_x[j], lru_lambda[j], lru_w_out[j])
        x = x + y
        x = x + hier_moe(rmsnorm(x, norm_ffn[i]), moe_w_group[i], moe_b_group[i], moe_w_router[i],
                         moe_b_router[i], moe_w_gate[i], moe_w_up[i], moe_w_down[i])
    return x


def setup_inputs(seed=0):
    out = dict(first_inputs(seed))
    for name, value in second_inputs(seed + 1).items():
        if name != "x":
            out[name + "_2"] = value
    return out


def reference(
    x, positions, norm_mix, norm_ffn, norm_final, pool_w, pool_scale, mla_w_down, mla_q_norm,
    mla_w_uq, mla_kv_norm, mla_w_ukv, mla_w_o, ffn_w_gate, ffn_w_up, ffn_w_down, norm_mix_2,
    norm_ffn_2, da_w_in_2, da_q_norm_2, da_k_norm_2, da_lambda_q1_2, da_lambda_k1_2,
    da_lambda_q2_2, da_lambda_k2_2, da_subln_2, da_w_out_2, nsa_w_in_2, nsa_q_norm_2,
    nsa_k_norm_2, nsa_cmp_pos_2, nsa_cmp_w1_2, nsa_cmp_w2_2, nsa_w_out_2, gdn_w_in_2,
    gdn_conv_w_2, gdn_a_log_2, gdn_dt_bias_2, gdn_out_norm_2, gdn_w_out_2, lru_w_in_2,
    lru_conv_w_2, lru_conv_b_2, lru_w_a_2, lru_b_a_2, lru_w_x_2, lru_b_x_2, lru_lambda_2,
    lru_w_out_2, moe_w_group_2, moe_b_group_2, moe_w_router_2, moe_b_router_2, moe_w_gate_2,
    moe_w_up_2, moe_w_down_2,
):
    x = first_block(
        x, positions, norm_mix, norm_ffn, norm_final, pool_w, pool_scale, mla_w_down,
        mla_q_norm, mla_w_uq, mla_kv_norm, mla_w_ukv, mla_w_o, ffn_w_gate, ffn_w_up, ffn_w_down,
    )
    return second_block(
        x, norm_mix_2, norm_ffn_2, da_w_in_2, da_q_norm_2, da_k_norm_2, da_lambda_q1_2,
        da_lambda_k1_2, da_lambda_q2_2, da_lambda_k2_2, da_subln_2, da_w_out_2, nsa_w_in_2,
        nsa_q_norm_2, nsa_k_norm_2, nsa_cmp_pos_2, nsa_cmp_w1_2, nsa_cmp_w2_2, nsa_w_out_2,
        gdn_w_in_2, gdn_conv_w_2, gdn_a_log_2, gdn_dt_bias_2, gdn_out_norm_2, gdn_w_out_2,
        lru_w_in_2, lru_conv_w_2, lru_conv_b_2, lru_w_a_2, lru_b_a_2, lru_w_x_2, lru_b_x_2,
        lru_lambda_2, lru_w_out_2, moe_w_group_2, moe_b_group_2, moe_w_router_2, moe_b_router_2,
        moe_w_gate_2, moe_w_up_2, moe_w_down_2,
    )


_drawn_inputs = setup_inputs


def setup_inputs(seed=0):
    import zlib

    import numpy as np

    out = dict(_drawn_inputs(seed))
    spreads = {}
    factors = {'mla_q_norm': 8.0,
     'mla_kv_norm': 6.359,
     'norm_ffn_2': 3.616,
     'da_q_norm_2': 3.797,
     'da_k_norm_2': 3.41,
     'da_subln_2': 3.66,
     'moe_b_group_2': 4.746,
     'moe_b_router_2': 7.007}
    for name, (base, spread) in spreads.items():
        noise = np.random.default_rng([zlib.crc32(name.encode()), seed]).standard_normal(out[name].shape)
        drawn = base * np.exp(spread * noise) if base else spread * noise
        out[name] = jnp.asarray(drawn.astype(out[name].dtype))
    for name, factor in factors.items():
        out[name] = (out[name] * factor).astype(out[name].dtype)
    return out
```

```python
from contextlib import ExitStack

import numpy as np
import concourse.bass as bass
from concourse import mybir

F32 = mybir.dt.float32
F32R = mybir.dt.float32r
I32 = mybir.dt.int32
U32 = mybir.dt.uint32
ALU = mybir.AluOpType
ACT = mybir.ActivationFunctionType
AX_X = mybir.AxisListType.X

P = 128
S = 512
T = S // P
D = 1024
C = D // P
F = 2816
FC = F // P
EPS = 1e-6
UNIT = 2048
SLOTS = 2
POOL_WINDOWS = (2, 4, 8, 16)
H = 8
ROPE = 64
Q_LORA = 384
KV_LORA = 128
MLA_SCALE = 192.0 ** -0.5
ROPE_THETA = 10000.0
NEG = -1e30
LAMBDA_INIT = 0.2
G = 4
E = 16
DE = 512
EU = 6
ESLOTS = 3
ROUNDS = S // P

U_POOL = 0
U_FFN0 = 1
FFN_UNITS = 3 * FC // 2
U_MLA = U_FFN0 + FFN_UNITS
U_MLA_OUT = U_MLA + 7
U_FFN1 = U_MLA + 11
U_DA = U_FFN1 + FFN_UNITS
U_DA_OUT = U_DA + 12
U_END = U_DA + 16

CONST_COLS = {}
_at = 0
for _name, _width in (("ident", P), ("causal", P), ("alibi", S), ("before", P), ("iota", P),
                      ("inv_freq", ROPE // 2), ("token1", T), ("priority", G)):
    CONST_COLS[_name] = (_at, _width)
    _at += _width
CONST_WIDTH = _at
BAND_WIDTH = 4 * (P + P + 16)

GAIN_COLS = {}
_at = 0
for _name, _width in (("mix0", C), ("ffn0", C), ("mix1", C), ("ffn1", C), ("mix2", C), ("moe", C),
                      ("q_lora", 3), ("kv_lora", 1), ("da_q", 1), ("da_k", 1), ("da_sub", 1)):
    GAIN_COLS[_name] = (_at, _width)
    _at += _width
GAIN_WIDTH = _at


def constants():
    p = np.arange(P)
    out = np.zeros((P, CONST_WIDTH), np.float32)

    def put(name, value):
        a, w = CONST_COLS[name]
        out[:, a:a + w] = value

    put("ident", np.eye(P))
    put("causal", np.where(p[None, :] <= p[:, None], 0.0, NEG))
    dist = p[:, None] + (S - P) - np.arange(S)[None, :]
    put("alibi", np.where(dist >= 0, -dist, NEG))
    put("before", p[:, None] < p[None, :])
    put("iota", np.broadcast_to(p[None, :], (P, P)))
    inv = np.float32(1.0) / np.float32(ROPE_THETA) ** (np.arange(0, ROPE, 2, dtype=np.float32) / np.float32(ROPE))
    put("inv_freq", inv[None, :])
    put("token1", p[:, None] + P * np.arange(T)[None, :] + 1)
    put("priority", (G - np.arange(G))[None, :])
    band = np.zeros((P, BAND_WIDTH), np.float32)
    for g, win in enumerate(POOL_WINDOWS):
        t, s = p[:, None], p[None, :]
        inside = (s - win < t) & (t <= s)
        first = np.where(inside, 1.0 / np.minimum(s + 1, win), 0.0) - (s == t)
        rest = np.where(inside, 1.0 / win, 0.0) - (s == t)
        s = np.arange(16)[None, :]
        prev = np.where(s + P - win < t, 1.0 / win, 0.0)
        band[:, g * P:(g + 1) * P] = first
        band[:, (4 + g) * P:(5 + g) * P] = rest
        band[:, 8 * P + 16 * g:8 * P + 16 * (g + 1)] = prev
    return out, band


def build_program(nc, stream, experts, x, positions, gains, rows, lams, router, consts, band, out, scratch, stop=99):
    ctx = ExitStack()
    with ctx:
        def sb(name, shape, dt=F32, where=None):
            return (where or ctx).enter_context(nc.sbuf_tensor(name, shape, dt))

        stage_sems = []

        def lasting(name):
            return nc.alloc_semaphore(name)

        def sem(name):
            stage_sems.append(nc.alloc_semaphore(name))
            return stage_sems[-1]

        def recycle():
            nc.clear_and_free_semaphores(list(stage_sems))
            stage_sems.clear()
            nc.all_engine_barrier()

        PS = ctx.enter_context(nc.psum_tensor("PS", [P, 8, 512], F32))
        X = sb("X", [P, T, D])
        cst = sb("cst", [P, CONST_WIDTH])
        gain = sb("gain", [P, GAIN_WIDTH])
        identr = sb("identr", [P, P], F32R)
        causalr = sb("causalr", [P, P], F32R)
        rstd = sb("rstd", [P, 8])
        AH = sb("AH", [P, C, S], F32R)
        AL = sb("AL", [P, C, S], F32R)
        wctx = ctx.enter_context(ExitStack())
        raw = sb("raw", [P, SLOTS, UNIT], where=wctx)
        WH = sb("WH", [P, SLOTS, UNIT], F32R, where=wctx)
        WL = sb("WL", [P, SLOTS, UNIT], F32R, where=wctx)

        def const(name):
            a, w = CONST_COLS[name]
            return cst[:, a:a + w]

        def gain_col(name, c=0):
            a, _ = GAIN_COLS[name]
            return gain[:, a + c:a + c + 1]

        ident = const("ident")

        unit_landed = [lasting(f"unit_landed{k}") for k in range(SLOTS)]
        unit_hi = lasting("unit_hi")
        unit_lo = lasting("unit_lo")
        unit_used = lasting("unit_used")

        def load_unit(sp, u, turn=0):
            v = u + SLOTS * turn
            if u >= SLOTS:
                sp.wait_ge(unit_lo, v - SLOTS + 1)
            src = stream[u, :, :] if isinstance(turn, int) else stream[bass.ds(v, 1), :, :].rearrange("a p n -> p (a n)")
            sp.dma_start(raw[:, u % SLOTS, :], src).then_inc(unit_landed[u % SLOTS], 16)

        def split_hi(act, u, turn=0):
            act.wait_ge(unit_landed[u % SLOTS], 16 * (u // SLOTS + 1) + 16 * turn)
            if u >= SLOTS:
                act.wait_ge(unit_used, u - SLOTS + 1 + SLOTS * turn)
            act.activation(WH[:, u % SLOTS, :], raw[:, u % SLOTS, :], ACT.Copy).then_inc(unit_hi, 1)

        def split_lo(dve, u, turn=0):
            dve.wait_ge(unit_hi, u + 1 + SLOTS * turn)
            dve.tensor_tensor(WL[:, u % SLOTS, :], raw[:, u % SLOTS, :], WH[:, u % SLOTS, :].bitcast(F32),
                              ALU.subtract).then_inc(unit_lo, 1)

        def product(pe, acc, lhs_hi, lhs_lo, rhs_hi, rhs_lo, start, stop):
            pe.matmul(acc, lhs_lo, rhs_hi, start=start, stop=False)
            pe.matmul(acc, lhs_hi, rhs_lo, start=False, stop=False)
            return pe.matmul(acc, lhs_hi, rhs_hi, start=False, stop=stop)

        def setup():
            arrived = sem("inputs_arrived")
            with nc.Block() as block:
                @block.sync
                def _(sp):
                    for u in range(SLOTS):
                        load_unit(sp, u)

                @block.scalar
                def _(act):
                    act.dma_start(X[:, :, :], x.rearrange("(t p) d -> p t d", p=P)).then_inc(arrived, 16)
                    act.dma_start(cst[:, :], consts[:, :]).then_inc(arrived, 16)
                    act.dma_start(gain[:, :], gains[:, :]).then_inc(arrived, 16)

                copied = sem("constants_copied")

                @block.vector
                def _(dve):
                    dve.wait_ge(arrived, 48)
                    dve.tensor_copy(identr[:, :], ident).then_inc(copied, 1)
                    dve.tensor_copy(causalr[:, :], const("causal")).then_inc(copied, 1)
                    a = GAIN_COLS["da_q"][0]
                    dve.tensor_scalar(gain[:, a:a + 1], gain[:, a:a + 1], 0.125, None, ALU.mult).then_inc(copied, 1)
                    a = GAIN_COLS["da_sub"][0]
                    dve.tensor_scalar(gain[:, a:a + 1], gain[:, a:a + 1], 1.0 - LAMBDA_INIT, None,
                                      ALU.mult).then_inc(copied, 1)

        def normalize(tag, xs, gain_name=None, split=(), prefetch=None):
            squared_a = sem(tag + "squared_act")
            squared_v = sem(tag + "squared_dve")
            meaned = sem(tag + "meaned")
            rooted = sem(tag + "rooted")
            inverted = sem(tag + "inverted")
            scaled = sem(tag + "scaled")
            turned = sem(tag + "turned")
            hi = sem(tag + "hi")
            lo = sem(tag + "lo")
            with ExitStack() as tmp, nc.Block() as block:
                junk = sb(tag + "junk", [P, 2, D], where=tmp)

                if prefetch:
                    @block.sync
                    def _(sp):
                        prefetch(sp)

                @block.scalar
                def _(act):
                    for t in range(2):
                        act.activation(junk[:, t, :], X[:, t, :], ACT.Square,
                                       accum_out=rstd[:, t:t + 1]).then_inc(squared_a, 1)
                    act.wait_ge(meaned, 1)
                    act.activation(rstd[:, 4:8], rstd[:, 0:4], ACT.Sqrt).then_inc(rooted, 1)
                    for u in split:
                        split_hi(act, u)
                    if gain_name:
                        for c in range(C):
                            act.wait_ge(turned, c + 1)
                            act.activation(AH[:, c, :], PS[:, c, :], ACT.Copy,
                                           scale=gain_col(gain_name, c)).then_inc(hi, 1)

                @block.vector
                def _(dve):
                    for t in range(2, 4):
                        dve.tensor_tensor_reduce(xs[:, t, :], X[:, t, :], X[:, t, :], 1.0, 0.0, ALU.mult, ALU.add,
                                                 rstd[:, t:t + 1]).then_inc(squared_v, 1)
                    dve.wait_ge(squared_a, 2)
                    dve.wait_ge(squared_v, 2)
                    dve.tensor_scalar(rstd[:, 0:4], rstd[:, 0:4], 1.0 / D, EPS, ALU.mult, ALU.add).then_inc(meaned, 1)
                    dve.wait_ge(rooted, 1)
                    dve.reciprocal(rstd[:, 0:4], rstd[:, 4:8]).then_inc(inverted, 1)
                    dve.wait_ge(inverted, 1)
                    for t in range(T):
                        dve.tensor_scalar(xs[:, t, :], X[:, t, :], rstd[:, t:t + 1], None,
                                          ALU.mult).then_inc(scaled, 1)
                    for u in split:
                        split_lo(dve, u)
                    if gain_name:
                        for c in range(C):
                            dve.wait_ge(hi, c + 1)
                            dve.scalar_tensor_tensor(AL[:, c, :], PS[:, c, :], gain_col(gain_name, c),
                                                     AH[:, c, :].bitcast(F32), ALU.mult,
                                                     ALU.subtract).then_inc(lo, 1)

                @block.tensor
                def _(pe):
                    if gain_name:
                        for t in range(T):
                            pe.wait_ge(scaled, t + 1)
                            for c in range(C):
                                mm = pe.transpose(PS[:, c, t * P:(t + 1) * P], xs[:, t, c * P:(c + 1) * P], ident)
                                if t == T - 1:
                                    mm.then_inc(turned, 1)

        def pool_stage(xs, bands, scale_row, rows_in):
            rows_here = sem("pool_rows_here")
            pooled = sem("pooled")
            hi = sem("pooled_hi")
            lo = sem("pooled_lo")
            mixed = sem("pool_mixed")
            weighed = sem("pool_weighed")
            with nc.Block() as block:
                @block.sync
                def _(sp):
                    sp.dma_start(bands[:, :], band[:, :]).then_inc(rows_here, 16)
                    sp.dma_start(scale_row[:, :], rows_in).then_inc(rows_here, 16)
                    load_unit(sp, 2)

                @block.tensor
                def _(pe):
                    pe.wait_ge(rows_here, 32)
                    for c in range(C):
                        g = c // 2
                        for t in range(T):
                            here = bands[:, (g if t == 0 else 4 + g) * P:(g + 1 if t == 0 else 5 + g) * P]
                            mm = pe.matmul(PS[:, c, t * P:(t + 1) * P], xs[:, t, c * P:(c + 1) * P], here,
                                           start=True, stop=(t == 0))
                            if t:
                                mm = pe.matmul(PS[:, c, t * P:t * P + 16], xs[:, t - 1, c * P:(c + 1) * P],
                                               bands[:, 8 * P + 16 * g:8 * P + 16 * (g + 1)], start=False, stop=True)
                        mm.then_inc(pooled, 1)
                    pe.wait_ge(unit_lo, U_POOL + 1)
                    pe.wait_ge(lo, C)
                    for t in range(T):
                        for g in range(4):
                            for k in range(2):
                                c = 2 * g + k
                                w = slice(c * 256, (c + 1) * 256)
                                mm = product(pe, PS[:, 2 * t + g // 2, (g % 2) * 256:(g % 2 + 1) * 256],
                                             AH[:, c, t * P:(t + 1) * P], AL[:, c, t * P:(t + 1) * P],
                                             WH[:, 0, w], WL[:, 0, w], k == 0, k == 1)
                        mm.then_inc(mixed, 1)
                    pe.wait_ge(mixed, T)
                    pe.sem_inc(unit_used, 1)

                @block.scalar
                def _(act):
                    for c in range(C):
                        act.wait_ge(pooled, c + 1)
                        act.activation(AH[:, c, :], PS[:, c, :], ACT.Copy,
                                       scale=gain_col("mix0", c)).then_inc(hi, 1)

                @block.vector
                def _(dve):
                    for c in range(C):
                        dve.wait_ge(hi, c + 1)
                        dve.scalar_tensor_tensor(AL[:, c, :], PS[:, c, :], gain_col("mix0", c),
                                                 AH[:, c, :].bitcast(F32), ALU.mult, ALU.subtract).then_inc(lo, 1)
                    dve.wait_ge(rows_here, 32)
                    for t in range(T):
                        dve.wait_ge(mixed, t + 1)
                        dve.tensor_tensor(xs[:, t, :], PS[:, 2 * t:2 * t + 2, :].rearrange("p a n -> p (a n)"),
                                          scale_row[:, :], ALU.mult).then_inc(weighed, 1)
                        dve.wait_ge(weighed, 2 * t + 1)
                        dve.tensor_tensor(X[:, t, :], X[:, t, :], xs[:, t, :], ALU.add).then_inc(weighed, 1)

        def project_pe(pe, u0, n, lhs_hi, lhs_lo, done):
            for d in range(n):
                u = u0 + d
                pe.wait_ge(unit_lo, u + 1)
                for t in range(T):
                    for f in range(2):
                        for half in range(2):
                            w = slice(f * D + half * 512, f * D + half * 512 + 512)
                            j = 2 * d + f
                            mm = product(pe, PS[:, 2 * t + half, :], lhs_hi[:, j, t * P:(t + 1) * P],
                                         lhs_lo[:, j, t * P:(t + 1) * P], WH[:, u % SLOTS, w], WL[:, u % SLOTS, w],
                                         j == 0, j == 2 * n - 1)
                    if d == n - 1:
                        mm.then_inc(done, 1)
                if d == n - 1:
                    pe.wait_ge(done, T)
                    pe.sem_inc(unit_used, 1)
                else:
                    mm.then_inc(unit_used, 1)

        def project_add(dve, done, added):
            for t in range(T):
                dve.wait_ge(done, t + 1)
                dve.tensor_tensor(X[:, t, :], X[:, t, :], PS[:, 2 * t:2 * t + 2, :].rearrange("p a n -> p (a n)"),
                                  ALU.add).then_inc(added, 1)

        def swiglu(tag, u0):
            n = FC // 2
            gate_made = sem(tag + "gate_made")
            up_made = sem(tag + "up_made")
            gate_free = sem(tag + "gate_free")
            up_free = sem(tag + "up_free")
            h_hi = sem(tag + "h_hi")
            h_lo = sem(tag + "h_lo")
            down_made = sem(tag + "down_made")
            added = sem(tag + "added")
            with ExitStack() as tmp, nc.Block() as block:
                FH = sb(tag + "FH", [P, FC, S], F32R, tmp)
                FL = sb(tag + "FL", [P, FC, S], F32R, tmp)
                silu = sb(tag + "silu", [P, 2, S], F32, tmp)

                @block.sync
                def _(sp):
                    with nc.sync.Fori(0, n) as i:
                        for k in range(2):
                            load_unit(sp, u0 + 2 + k, i)
                    for u in range(u0 + 2 * n + 2, u0 + FFN_UNITS + 2):
                        load_unit(sp, u)

                @block.tensor
                def _(pe):
                    with nc.tensor.Fori(0, n) as i:
                        for part, made, free in ((0, gate_made, gate_free), (1, up_made, up_free)):
                            slot = (u0 + part) % SLOTS
                            pe.wait_ge(unit_lo, u0 + part + 1 + 2 * i)
                            for k in range(2):
                                pe.wait_ge(free, 2 * i + k + 1)
                                for c in range(C):
                                    w = slice(c * 256 + k * P, c * 256 + k * P + P)
                                    mm = product(pe, PS[:, 2 * part + k, :], WH[:, slot, w], WL[:, slot, w],
                                                 AH[:, c, :], AL[:, c, :], c == 0, c == C - 1)
                                mm.then_inc(made, 1)
                            pe.wait_ge(made, 2 * i + 2)
                            pe.sem_inc(unit_used, 1)
                    pe.wait_ge(h_lo, FC + 1)
                    project_pe(pe, u0 + 2 * n, n, FH, FL, down_made)

                @block.scalar
                def _(act):
                    act.sem_inc(gate_free, 2)
                    with nc.scalar.Fori(0, n) as i:
                        for k in range(2):
                            act.wait_ge(gate_made, 2 * i + k + 1)
                            act.wait_ge(h_lo, 2 * i + 1)
                            act.activation(silu[:, k, :], PS[:, k, :], ACT.Silu).then_inc(gate_free, 1)
                        split_hi(act, u0 + 2, i)
                        for k in range(2):
                            act.wait_ge(up_free, 2 * i + k + 3)
                            act.activation(FH[:, bass.ds(2 * i + k, 1), :].rearrange("p a s -> p (a s)"),
                                           silu[:, k, :], ACT.Copy).then_inc(h_hi, 1)
                        split_hi(act, u0 + 3, i)
                    for u in range(u0 + 2 * n + 2, u0 + FFN_UNITS):
                        split_hi(act, u)

                @block.vector
                def _(dve):
                    dve.sem_inc(up_free, 2)
                    dve.sem_inc(h_lo, 1)
                    with nc.vector.Fori(0, n) as i:
                        split_lo(dve, u0 + 2, i)
                        for k in range(2):
                            dve.wait_ge(gate_free, 2 * i + k + 3)
                            dve.wait_ge(up_made, 2 * i + k + 1)
                            dve.tensor_tensor(silu[:, k, :], silu[:, k, :], PS[:, 2 + k, :],
                                              ALU.mult).then_inc(up_free, 1)
                        for k in range(2):
                            dve.wait_ge(h_hi, 2 * i + k + 1)
                            j = bass.ds(2 * i + k, 1)
                            dve.tensor_tensor(FL[:, j, :].rearrange("p a s -> p (a s)"), silu[:, k, :],
                                              FH[:, j, :].rearrange("p a s -> p (a s)").bitcast(F32),
                                              ALU.subtract).then_inc(h_lo, 1)
                        split_lo(dve, u0 + 3, i)
                    for u in range(u0 + 2 * n + 2, u0 + FFN_UNITS):
                        split_lo(dve, u)
                    project_add(dve, down_made, added)


        def mla_down(CTH, CTL, KR, rot):
            rope_in = sem("rope_in")
            angle = sem("angle")
            sines = sem("sines")
            main_made = sem("mla_main_made")
            rope_made = sem("mla_rope_made")
            squared = sem("mla_squared")
            meaned = sem("mla_meaned")
            rooted = sem("mla_rooted")
            inverted = sem("mla_inverted")
            scaled = sem("mla_scaled")
            kr_copied = sem("mla_kr_copied")
            rotated = sem("mla_kr_rotated")
            turned = sem("mla_turned")
            hi = sem("mla_ct_hi")
            lo = sem("mla_ct_lo")
            kr_out = sem("mla_kr_out")
            two_pi = 2.0 * np.pi
            c1 = 6.28125
            c2 = float(np.float32(int((two_pi - c1) * 2 ** 21) / 2 ** 21))
            c3 = float(two_pi - c1 - c2)
            magic = 1.5 * 2.0 ** 23
            edge = 3.1415925
            with ExitStack() as tmp, nc.Block() as block:
                dn = sb("mla_dn", [P, T, 512], where=tmp)
                kr = sb("mla_kr", [P, T, 2, 32], where=tmp)
                krot = sb("mla_krot", [P, T, 2, 2, 32], where=tmp)
                krm = sb("mla_krm", [P, 2, T, 2, 32], where=tmp)
                pos = sb("rope_pos", [P, T], I32, tmp)
                posf = sb("rope_posf", [P, T], where=tmp)
                ang = sb("rope_ang", [P, 2, T, 32], where=tmp)
                turns = sb("rope_turns", [P, 2, T, 32], where=tmp)
                sc = sb("mla_sc", [P, 16], where=tmp)

                @block.sync
                def _(sp):
                    sp.dma_start(pos[:, :], positions[:, :]).then_inc(rope_in, 16)
                    for u in range(U_MLA + 2, U_MLA + 5):
                        load_unit(sp, u)

                @block.tensor
                def _(pe):
                    for part in range(2):
                        u = U_MLA + part
                        pe.wait_ge(unit_lo, u + 1)
                        for t in range(T):
                            for k in range(4):
                                c = 4 * part + k
                                w = slice(k * 512, (k + 1) * 512)
                                mm = product(pe, PS[:, t, :], AH[:, c, t * P:(t + 1) * P], AL[:, c, t * P:(t + 1) * P],
                                             WH[:, u % SLOTS, w], WL[:, u % SLOTS, w], c == 0, c == C - 1)
                            if part:
                                mm.then_inc(main_made, 1)
                        if part:
                            pe.wait_ge(main_made, T)
                            pe.sem_inc(unit_used, 1)
                        else:
                            mm.then_inc(unit_used, 1)
                    u = U_MLA + 2
                    pe.wait_ge(unit_lo, u + 1)
                    for t in range(T):
                        for c in range(C):
                            w = slice(c * ROPE, (c + 1) * ROPE)
                            mm = product(pe, PS[:, 4 + t, 0:ROPE], AH[:, c, t * P:(t + 1) * P],
                                         AL[:, c, t * P:(t + 1) * P], WH[:, u % SLOTS, w], WL[:, u % SLOTS, w],
                                         c == 0, c == C - 1)
                    mm.then_inc(rope_made, 1)
                    pe.wait_ge(rope_made, 1)
                    pe.sem_inc(unit_used, 1)
                    pe.wait_ge(kr_copied, 1)
                    for t in range(T):
                        pe.wait_ge(scaled, 2 * (t + 1))
                        for c in range(4):
                            mm = pe.transpose(PS[:, 4 + c, t * P:(t + 1) * P], dn[:, t, c * P:(c + 1) * P], ident)
                            if t == T - 1:
                                mm.then_inc(turned, 1)
                    pe.wait_ge(rotated, 1)
                    for t in range(T):
                        mm = pe.transpose(PS[:, 0, t * P:(t + 1) * P],
                                          krot[:, t, :, :, :].rearrange("p a b n -> p (a b n)"), ident)
                    mm.then_inc(turned, 1)

                @block.scalar
                def _(act):
                    split_hi(act, U_MLA + 2)
                    act.wait_ge(angle, 14)
                    act.activation(rot[:, :, :, :], ang[:, :, :, :], ACT.Sin).then_inc(sines, 1)
                    for t in range(T):
                        act.wait_ge(main_made, t + 1)
                        act.activation(dn[:, t, 0:Q_LORA], PS[:, t, 0:Q_LORA], ACT.Square,
                                       accum_out=sc[:, t:t + 1]).then_inc(squared, 1)
                        act.activation(dn[:, t, Q_LORA:512], PS[:, t, Q_LORA:512], ACT.Square,
                                       accum_out=sc[:, 4 + t:5 + t]).then_inc(squared, 1)
                    act.wait_ge(meaned, 2)
                    act.activation(sc[:, 8:16], sc[:, 0:8], ACT.Sqrt).then_inc(rooted, 1)
                    act.wait_ge(rope_made, 1)
                    act.activation(kr[:, :, :, :].rearrange("p t a n -> p t (a n)"), PS[:, 4:8, 0:ROPE],
                                   ACT.Copy).then_inc(kr_copied, 1)
                    split_hi(act, U_MLA + 3)
                    split_hi(act, U_MLA + 4)
                    for c in range(4):
                        act.wait_ge(turned, c + 1)
                        act.activation(CTH[:, c, :], PS[:, 4 + c, :], ACT.Copy,
                                       scale=gain_col("q_lora", c)).then_inc(hi, 1)
                    act.wait_ge(turned, 5)
                    act.activation(KR[:, :], PS[:, 0, :], ACT.Copy).then_inc(kr_out, 1)

                @block.vector
                def _(dve):
                    split_lo(dve, U_MLA + 2)
                    dve.wait_ge(rope_in, 16)
                    dve.tensor_copy(posf[:, :], pos[:, :]).then_inc(angle, 1)
                    dve.wait_ge(angle, 1)
                    for w in range(2):
                        for t in range(T):
                            ins = dve.tensor_scalar(ang[:, w, t, :], const("inv_freq"), posf[:, t:t + 1], None, ALU.mult)
                    ins.then_inc(angle, 1)
                    dve.wait_ge(angle, 2)
                    for w, quarter in ((0, 0.0), (1, 0.25)):
                        dve.tensor_scalar(turns[:, w, :, :], ang[:, w, :, :], 1.0 / two_pi, quarter, ALU.mult,
                                          ALU.add).then_inc(angle, 1)
                    dve.wait_ge(angle, 4)
                    dve.tensor_scalar(turns[:, :, :, :], turns[:, :, :, :], magic, None, ALU.add).then_inc(angle, 1)
                    dve.wait_ge(angle, 5)
                    dve.tensor_scalar(turns[:, :, :, :], turns[:, :, :, :], magic, None, ALU.subtract).then_inc(angle, 1)
                    dve.wait_ge(angle, 6)
                    flat = "p a t n -> p (a t n)"
                    for n, part in enumerate((c1, c2, c3)):
                        dve.scalar_tensor_tensor(ang[:, :, :, :].rearrange(flat), turns[:, :, :, :].rearrange(flat),
                                                 -part, ang[:, :, :, :].rearrange(flat), ALU.mult,
                                                 ALU.add).then_inc(angle, 1)
                        dve.wait_ge(angle, 7 + n)
                    dve.tensor_scalar(ang[:, 1, :, :], ang[:, 1, :, :], 0.5 * np.pi, None, ALU.add).then_inc(angle, 1)
                    dve.wait_ge(angle, 10)
                    dve.tensor_scalar(ang[:, :, :, :], ang[:, :, :, :], edge, None, ALU.min).then_inc(angle, 1)
                    dve.wait_ge(angle, 11)
                    dve.tensor_scalar(ang[:, :, :, :], ang[:, :, :, :], -edge, None, ALU.max).then_inc(angle, 3)
                    dve.wait_ge(squared, 2 * T)
                    dve.tensor_scalar(sc[:, 0:4], sc[:, 0:4], 1.0 / Q_LORA, EPS, ALU.mult, ALU.add).then_inc(meaned, 1)
                    dve.tensor_scalar(sc[:, 4:8], sc[:, 4:8], 1.0 / KV_LORA, EPS, ALU.mult, ALU.add).then_inc(meaned, 1)
                    dve.wait_ge(rooted, 1)
                    dve.reciprocal(sc[:, 0:8], sc[:, 8:16]).then_inc(inverted, 1)
                    dve.wait_ge(inverted, 1)
                    for t in range(T):
                        dve.tensor_scalar(dn[:, t, 0:Q_LORA], PS[:, t, 0:Q_LORA], sc[:, t:t + 1], None,
                                          ALU.mult).then_inc(scaled, 1)
                        dve.tensor_scalar(dn[:, t, Q_LORA:512], PS[:, t, Q_LORA:512], sc[:, 4 + t:5 + t], None,
                                          ALU.mult).then_inc(scaled, 1)
                    dve.wait_ge(kr_copied, 1)
                    dve.wait_ge(sines, 1)
                    for w in range(2):
                        for a in range(2):
                            ins = dve.tensor_tensor(krm[:, w, :, a, :], kr[:, :, a, :], rot[:, w, :, :], ALU.mult)
                    ins.then_inc(scaled, 1)
                    dve.wait_ge(scaled, 2 * T + 1)
                    for twice in range(2):
                        dve.tensor_tensor(krot[:, :, twice, 0, :], krm[:, 1, :, 0, :], krm[:, 0, :, 1, :], ALU.subtract)
                        ins = dve.tensor_tensor(krot[:, :, twice, 1, :], krm[:, 1, :, 1, :], krm[:, 0, :, 0, :], ALU.add)
                    ins.then_inc(rotated, 1)
                    split_lo(dve, U_MLA + 3)
                    split_lo(dve, U_MLA + 4)
                    for c in range(4):
                        dve.wait_ge(hi, c + 1)
                        dve.scalar_tensor_tensor(CTL[:, c, :], PS[:, 4 + c, :], gain_col("q_lora", c),
                                                 CTH[:, c, :].bitcast(F32), ALU.mult, ALU.subtract).then_inc(lo, 1)

        def mla_up(CTH, CTL, rot, QN, QR, KN, V):
            made = sem("mla_up_made")
            emptied = [sem("mla_up_emptied_act"), sem("mla_up_emptied_dve")]
            rotated = sem("mla_q_rotated")
            n_plain = 4 + 8 + 8 + 8
            with ExitStack() as tmp, nc.Block() as block:
                qr = sb("mla_qr", [P, T, 512], where=tmp)
                qrot = sb("mla_qrot", [P, T, H, 2, 32], where=tmp)
                qrm = sb("mla_qrm", [P, 2, 2, 512], where=tmp)

                def home(n):
                    if n < 4:
                        return qr[:, n, :], 1.0
                    if n < 12:
                        return QN[:, n - 4, :], MLA_SCALE
                    if n < 20:
                        return KN[:, n - 12, :], 1.0
                    if n < 28:
                        return V[:, (n - 20) // 2, (n % 2) * 512:(n % 2 + 1) * 512], 1.0
                    return QR[:, n - 28, :], MLA_SCALE

                @block.sync
                def _(sp):
                    for u in range(U_MLA + 5, U_MLA + 9):
                        load_unit(sp, u)

                @block.tensor
                def _(pe):
                    for n in range(n_plain + 4):
                        if n >= 8:
                            pe.wait_ge(emptied[n % 2], (n - 8) // 2 + 1)
                        acc = PS[:, n % 8, :]
                        u = U_MLA + (3 if n < 4 else 4 if n < 8 else 5 if n < 12 else 6)
                        if n in (0, 4, 8, 12):
                            pe.wait_ge(unit_lo, u + 1)
                        wh, wl = WH[:, u % SLOTS, :], WL[:, u % SLOTS, :]
                        if n < 4:
                            for c in range(3):
                                w = slice(c * 512, (c + 1) * 512)
                                mm = product(pe, acc, CTH[:, c, n * P:(n + 1) * P], CTL[:, c, n * P:(n + 1) * P],
                                             wh[:, w], wl[:, w], c == 0, c == 2)
                        elif n < 12:
                            for c in range(3):
                                w = slice(c * 512 + (n % 4) * P, c * 512 + (n % 4) * P + P)
                                mm = product(pe, acc, wh[:, w], wl[:, w], CTH[:, c, :], CTL[:, c, :], c == 0, c == 2)
                        elif n < 20:
                            w = slice((n - 12) * P, (n - 11) * P)
                            mm = product(pe, acc, wh[:, w], wl[:, w], CTH[:, 3, :], CTL[:, 3, :], True, True)
                        elif n < 28:
                            t = (n - 20) // 2
                            w = slice(D + (n % 2) * 512, D + (n % 2) * 512 + 512)
                            mm = product(pe, acc, CTH[:, 3, t * P:(t + 1) * P], CTL[:, 3, t * P:(t + 1) * P],
                                         wh[:, w], wl[:, w], True, True)
                        else:
                            for t in range(T):
                                pe.wait_ge(rotated, 4 * (t + 1))
                                src = qrot[:, t, 2 * (n - 28):2 * (n - 28) + 2, :, :]
                                mm = pe.transpose(PS[:, n % 8, t * P:(t + 1) * P],
                                                  src.rearrange("p h a n -> p (h a n)"), ident)
                        mm.then_inc(made, 1)
                        if n in (3, 7, 11, 27):
                            pe.wait_ge(made, n + 1)
                            pe.sem_inc(unit_used, 1)

                @block.scalar
                def _(act):
                    for n in range(0, n_plain + 4, 2):
                        act.wait_ge(made, n + 1)
                        dst, scale = home(n)
                        act.activation(dst, PS[:, n % 8, :], ACT.Copy, scale=scale).then_inc(emptied[0], 1)
                        if n in (4, 8, 12):
                            split_hi(act, U_MLA + 5 + (n - 4) // 4)

                @block.vector
                def _(dve):
                    for n in range(1, n_plain + 4, 2):
                        dve.wait_ge(made, n + 1)
                        dst, scale = home(n)
                        dve.tensor_scalar(dst, PS[:, n % 8, :], scale, None, ALU.mult).then_inc(emptied[1], 1)
                        if n in (5, 9, 13):
                            split_lo(dve, U_MLA + 5 + (n - 5) // 4)
                        if n in (5, 7, 9, 11):
                            t = (n - 5) // 2
                            dve.wait_ge(emptied[0], t // 2 + 1)
                            dve.wait_ge(emptied[1], t // 2 + 1)
                            if t >= 2:
                                dve.wait_ge(rotated, 4 * (t - 1))
                            for w in range(2):
                                dve.tensor_tensor(qrm[:, t % 2, w, :].rearrange("p (a n) -> p a n", n=32),
                                                  qr[:, t, :].rearrange("p (a n) -> p a n", n=32),
                                                  rot[:, w, t:t + 1, :].broadcast_to([P, 2 * H, 32]),
                                                  ALU.mult).then_inc(rotated, 1)
                            dve.wait_ge(rotated, 4 * t + 2)
                            by_sin, by_cos = (qrm[:, t % 2, w, :].rearrange("p (h a n) -> p h a n", a=2, n=32)
                                              for w in range(2))
                            dve.tensor_tensor(qrot[:, t, :, 0, :], by_cos[:, :, 0, :], by_sin[:, :, 1, :],
                                              ALU.subtract).then_inc(rotated, 1)
                            dve.tensor_tensor(qrot[:, t, :, 1, :], by_cos[:, :, 1, :], by_sin[:, :, 0, :],
                                              ALU.add).then_inc(rotated, 1)

        def attend(tag, maps, scores, V, O, units, prepare=None):
            scored = sem(tag + "scored")
            maxed = sem(tag + "maxed")
            exped = sem(tag + "exped")
            factored = sem(tag + "factored")
            combined = sem(tag + "combined")
            turned = sem(tag + "turned")
            copied = sem(tag + "copied")
            weighed = sem(tag + "weighed")
            emptied = sem(tag + "emptied")
            ready = sem(tag + "ready")
            N = H * T
            ahead = 4 // maps
            with ExitStack() as tmp, nc.Block() as block:
                probs = sb(tag + "probs", [P, 2, maps, S], where=tmp)
                mixed = sb(tag + "mixed", [P, 2, S], where=tmp) if maps == 2 else None
                turned_probs = sb(tag + "turned_probs", [P, 2, S], where=tmp)
                neg_max = sb(tag + "neg_max", [P, N * maps], where=tmp)
                total = sb(tag + "total", [P, N * maps], where=tmp)
                factor = sb(tag + "factor", [P, N * maps], where=tmp)
                neg_lambda, extra = prepare(tmp, block, ready) if prepare else (None, 0)

                @block.tensor
                def _(pe):
                    for i in range(N + 3):
                        if i < N:
                            h, q = divmod(i, T)
                            if i >= ahead:
                                pe.wait_ge(exped, maps * (i - ahead + 1))
                            if i == 0 and extra:
                                pe.wait_ge(ready, extra)
                            for m in range(maps):
                                scores(pe, h, q, m, PS[:, maps * (i % ahead) + m, 0:(q + 1) * P]).then_inc(scored, 1)
                        j = i - 2
                        if 0 <= j < N:
                            q = j % T
                            pe.wait_ge(combined if maps == 2 else exped, j + 1)
                            if j >= 2:
                                pe.wait_ge(copied, j - 1)
                            src = mixed[:, j % 2, :] if maps == 2 else probs[:, j % 2, 0, :]
                            for k in range(q + 1):
                                mm = pe.transpose(PS[:, 4 + j % 2, k * P:(k + 1) * P], src[:, k * P:(k + 1) * P], ident)
                            mm.then_inc(turned, 1)
                        j = i - 3
                        if 0 <= j < N:
                            h, q = divmod(j, T)
                            pe.wait_ge(copied, j + 1)
                            if j >= 2:
                                pe.wait_ge(emptied, j - 1)
                            for k in range(q + 1):
                                mm = pe.matmul(PS[:, 6 + j % 2, 0:P], turned_probs[:, j % 2, k * P:(k + 1) * P],
                                               V[:, k, h * P:(h + 1) * P], start=(k == 0), stop=(k == q))
                            mm.then_inc(weighed, 1)

                @block.scalar
                def _(act):
                    for i in range(N + 2):
                        if i < N:
                            w = (i % T + 1) * P
                            for m in range(maps):
                                n = maps * i + m
                                act.wait_ge(maxed, n + 1)
                                if i >= 2:
                                    act.wait_ge(combined if maps == 2 else turned, i - 1)
                                act.activation(probs[:, i % 2, m, 0:w], PS[:, maps * (i % ahead) + m, 0:w], ACT.Exp,
                                               bias=neg_max[:, n:n + 1],
                                               accum_out=total[:, n:n + 1]).then_inc(exped, 1)
                        j = i - 2
                        if 0 <= j < N:
                            w = (j % T + 1) * P
                            act.wait_ge(turned, j + 1)
                            if j >= 2:
                                act.wait_ge(weighed, j - 1)
                            act.activation(turned_probs[:, j % 2, 0:w], PS[:, 4 + j % 2, 0:w],
                                           ACT.Copy).then_inc(copied, 1)
                        if i == 1:
                            for u in units:
                                split_hi(act, u)

                @block.vector
                def _(dve):
                    for i in range(N + 3):
                        if i < N:
                            w = (i % T + 1) * P
                            for m in range(maps):
                                n = maps * i + m
                                dve.wait_ge(scored, n + 1)
                                dve.tensor_reduce(neg_max[:, n:n + 1], PS[:, maps * (i % ahead) + m, 0:w], AX_X,
                                                  ALU.max, negate=True).then_inc(maxed, 1)
                        j = i - 1
                        if 0 <= j < N:
                            n = maps * j
                            w = (j % T + 1) * P
                            dve.wait_ge(exped, maps * (j + 1))
                            dve.reciprocal(factor[:, n:n + maps], total[:, n:n + maps]).then_inc(factored, 1)
                            if maps == 2:
                                dve.wait_ge(factored, 2 * j + 1)
                                dve.scalar_tensor_tensor(factor[:, n + 1:n + 2], total[:, n:n + 1], neg_lambda,
                                                         factor[:, n + 1:n + 2], ALU.mult,
                                                         ALU.mult).then_inc(factored, 1)
                                dve.wait_ge(factored, 2 * j + 2)
                                if j >= 2:
                                    dve.wait_ge(turned, j - 1)
                                dve.scalar_tensor_tensor(mixed[:, j % 2, 0:w], probs[:, j % 2, 1, 0:w],
                                                         factor[:, n + 1:n + 2], probs[:, j % 2, 0, 0:w], ALU.mult,
                                                         ALU.add).then_inc(combined, 1)
                        j = i - 3
                        if 0 <= j < N:
                            h, q = divmod(j, T)
                            n = maps * j
                            dve.wait_ge(weighed, j + 1)
                            dve.wait_ge(factored, maps * (j + 1))
                            dve.tensor_scalar(O[:, q, h * P:(h + 1) * P], PS[:, 6 + j % 2, 0:P], factor[:, n:n + 1],
                                              None, ALU.mult).then_inc(emptied, 1)
                        if i == 1:
                            for u in units:
                                split_lo(dve, u)

        def attention_out(tag, O, u0, column, last_load, normed=False):
            turned = sem(tag + "turned")
            hi = sem(tag + "hi")
            lo = sem(tag + "lo")
            made = sem(tag + "made")
            added = sem(tag + "added")
            squared = sem(tag + "squared")
            summed = sem(tag + "summed")
            rooted = sem(tag + "rooted")
            normal = sem(tag + "normal")
            with ExitStack() as tmp, nc.Block() as block:
                square = sb(tag + "square", [P, 2, D], where=tmp) if normed else None
                stat = sb(tag + "stat", [P, T, 2 * H], where=tmp) if normed else None

                @block.sync
                def _(sp):
                    for u in range(u0 + 2, last_load):
                        load_unit(sp, u)

                @block.tensor
                def _(pe):
                    for t in range(T):
                        if normed:
                            pe.wait_ge(normal, t + 1)
                        for c in range(C):
                            mm = pe.transpose(PS[:, c, t * P:(t + 1) * P], O[:, t, c * P:(c + 1) * P], ident)
                            if t == T - 1:
                                mm.then_inc(turned, 1)
                    pe.wait_ge(lo, C)
                    project_pe(pe, u0, 4, AH, AL, made)

                @block.scalar
                def _(act):
                    if normed:
                        for t in range(T):
                            if t >= 2:
                                act.wait_ge(summed, t - 1)
                            act.activation(square[:, t % 2, :], O[:, t, :], ACT.Square).then_inc(squared, 1)
                        act.wait_ge(summed, T + 1)
                        act.activation(stat[:, :, H:2 * H], stat[:, :, 0:H], ACT.Sqrt).then_inc(rooted, 1)
                    for c in range(C):
                        act.wait_ge(turned, c + 1)
                        scale = column if column is not None else 1.0
                        act.activation(AH[:, c, :], PS[:, c, :], ACT.Copy, scale=scale).then_inc(hi, 1)
                    for u in range(u0 + 2, u0 + 4):
                        split_hi(act, u)

                @block.vector
                def _(dve):
                    if normed:
                        for t in range(T):
                            dve.wait_ge(squared, t + 1)
                            dve.tensor_reduce(stat[:, t, 0:H], square[:, t % 2, :].rearrange("p (h d) -> p h d", h=H),
                                              AX_X, ALU.add).then_inc(summed, 1)
                        dve.wait_ge(summed, T)
                        dve.tensor_scalar(stat[:, :, 0:H], stat[:, :, 0:H], 1.0 / P, EPS, ALU.mult,
                                          ALU.add).then_inc(summed, 1)
                        dve.wait_ge(rooted, 1)
                        dve.reciprocal(stat[:, :, 0:H], stat[:, :, H:2 * H]).then_inc(rooted, 1)
                        dve.wait_ge(rooted, 2)
                        for t in range(T):
                            o = O[:, t, :].rearrange("p (h d) -> p h d", h=H)
                            dve.tensor_tensor(o, o, stat[:, t, 0:H].unsqueeze(2).broadcast_to([P, H, P]),
                                              ALU.mult).then_inc(normal, 1)
                    for c in range(C):
                        dve.wait_ge(hi, c + 1)
                        scale = column if column is not None else 1.0
                        dve.scalar_tensor_tensor(AL[:, c, :], PS[:, c, :], scale, AH[:, c, :].bitcast(F32),
                                                 ALU.mult, ALU.subtract).then_inc(lo, 1)
                    for u in range(u0 + 2, u0 + 4):
                        split_lo(dve, u)
                    project_add(dve, made, added)

        def final_norm():
            with ExitStack() as tmp:
                xs = sb("final_xs", [P, T, D], where=tmp)
                row = sb("final_row", [P, D], where=tmp)
                row_here = sem("final_row_here")
                gained = sem("final_gained")
                normalize("nf", xs)
                with nc.Block() as block:
                    @block.scalar
                    def _(act):
                        act.dma_start(row[:, :], rows[1:2, :].broadcast_to([P, D])).then_inc(row_here, 16)

                    @block.vector
                    def _(dve):
                        dve.wait_ge(row_here, 16)
                        for t in range(T):
                            dve.tensor_tensor(X[:, t, :], xs[:, t, :], row[:, :], ALU.mult).then_inc(gained, 1)

        def da_in(QK, V):
            made = sem("da_made")
            squared = sem("da_squared")
            emptied = sem("da_emptied")
            summed = sem("da_summed")
            rooted = sem("da_rooted")
            normal = sem("da_normal")
            with ExitStack() as tmp, nc.Block() as block:
                square = sb("da_square", [P, 2, 512], where=tmp)
                stat = sb("da_stat", [P, T, 32], where=tmp)
                root = sb("da_root", [P, T, 32], where=tmp)

                @block.sync
                def _(sp):
                    for u in range(U_DA + 2, U_DA_OUT + 2):
                        load_unit(sp, u)

                @block.tensor
                def _(pe):
                    for b in range(6):
                        for part in range(2):
                            u = U_DA + 2 * b + part
                            pe.wait_ge(unit_lo, u + 1)
                            for t in range(T):
                                bank = 4 * (b % 2) + t
                                if b >= 2 and part == 0:
                                    pe.wait_ge(emptied, 4 * (b - 2) + t + 1)
                                for k in range(4):
                                    c = 4 * part + k
                                    w = slice(k * 512, (k + 1) * 512)
                                    mm = product(pe, PS[:, bank, :], AH[:, c, t * P:(t + 1) * P],
                                                 AL[:, c, t * P:(t + 1) * P], WH[:, u % SLOTS, w], WL[:, u % SLOTS, w],
                                                 c == 0, c == C - 1)
                                if part:
                                    mm.then_inc(made, 1)
                            if part:
                                pe.wait_ge(made, 4 * (b + 1))
                                pe.sem_inc(unit_used, 1)
                            else:
                                mm.then_inc(unit_used, 1)

                @block.scalar
                def _(act):
                    for b in range(6):
                        if b < 5:
                            split_hi(act, U_DA + 2 * b + 2)
                        for t in range(T):
                            bank = 4 * (b % 2) + t
                            n = 4 * b + t
                            act.wait_ge(made, n + 1)
                            if b < 4:
                                if n >= 2:
                                    act.wait_ge(summed, n - 1)
                                act.activation(square[:, n % 2, :], PS[:, bank, :], ACT.Square).then_inc(squared, 1)
                                act.activation(QK[:, t, b * 512:(b + 1) * 512], PS[:, bank, :],
                                               ACT.Copy).then_inc(emptied, 1)
                            else:
                                act.activation(V[:, t, (b - 4) * 512:(b - 3) * 512], PS[:, bank, :],
                                               ACT.Copy).then_inc(emptied, 1)
                        if b < 5:
                            split_hi(act, U_DA + 2 * b + 3)
                        if b == 3:
                            act.wait_ge(summed, 17)
                            act.activation(root[:, :, :], stat[:, :, :], ACT.Sqrt).then_inc(rooted, 1)

                @block.vector
                def _(dve):
                    for b in range(6):
                        if b < 5:
                            split_lo(dve, U_DA + 2 * b + 2)
                        if b < 4:
                            for t in range(T):
                                n = 4 * b + t
                                dve.wait_ge(squared, n + 1)
                                dve.tensor_reduce(stat[:, t, 8 * b:8 * b + 8],
                                                  square[:, n % 2, :].rearrange("p (g d) -> p g d", d=64), AX_X,
                                                  ALU.add).then_inc(summed, 1)
                        if b == 3:
                            dve.wait_ge(summed, 16)
                            dve.tensor_scalar(stat[:, :, :], stat[:, :, :], 1.0 / 64, EPS, ALU.mult,
                                              ALU.add).then_inc(summed, 1)
                        if b < 5:
                            split_lo(dve, U_DA + 2 * b + 3)
                        if b == 3:
                            dve.wait_ge(rooted, 1)
                            dve.reciprocal(stat[:, :, :], root[:, :, :]).then_inc(rooted, 1)
                            dve.wait_ge(rooted, 2)
                            dve.wait_ge(emptied, 16)
                        if b >= 4:
                            for t in range(2 * (b - 4), 2 * (b - 4) + 2):
                                qk = QK[:, t, :].rearrange("p (g d) -> p g d", d=64)
                                dve.tensor_tensor(qk, qk, stat[:, t, :].unsqueeze(2).broadcast_to([P, 32, 64]),
                                                  ALU.mult).then_inc(normal, 1)

        def da_turn(QK, QT, KT):
            turned = sem("da_turned")
            emptied = [sem("da_emptied_act"), sem("da_emptied_dve")]
            with nc.Block() as block:
                def home(n):
                    return (QT[:, n, :], gain_col("da_q")) if n < 8 else (KT[:, n - 8, :], gain_col("da_k"))

                @block.tensor
                def _(pe):
                    for n in range(16):
                        if n >= 8:
                            pe.wait_ge(emptied[n % 2], (n - 8) // 2 + 1)
                        for t in range(T):
                            mm = pe.transpose(PS[:, n % 8, t * P:(t + 1) * P], QK[:, t, n * P:(n + 1) * P], ident)
                        mm.then_inc(turned, 1)

                @block.scalar
                def _(act):
                    for n in range(0, 16, 2):
                        act.wait_ge(turned, n + 1)
                        dst, scale = home(n)
                        act.activation(dst, PS[:, n % 8, :], ACT.Copy, scale=scale).then_inc(emptied[0], 1)

                @block.vector
                def _(dve):
                    for n in range(1, 16, 2):
                        dve.wait_ge(turned, n + 1)
                        dst, scale = home(n)
                        dve.tensor_scalar(dst, PS[:, n % 8, :], scale, None, ALU.mult).then_inc(emptied[1], 1)

        def route(xs, place, weight, code, counts):
            here = sem("router_here")
            logits_made = sem("logits_made")
            step = sem("route_step")
            exped = sem("route_exped")
            selected = sem("route_selected")
            ranked = sem("route_ranked")
            gained = sem("moe_gained")
            hi = sem("moe_rows_hi")
            lo = sem("moe_rows_lo")
            with ExitStack() as tmp, nc.Block() as block:
                wr = sb("wr", [P, C, 20], where=tmp)
                bias = sb("router_bias", [P, 20], where=tmp)
                row = sb("moe_gain_row", [P, D], where=tmp)
                ones = sb("ones", [P, P], where=tmp)
                L = sb("logits", [P, T, 20], where=tmp)
                small = sb("route_small", [P, 12, T, 1], where=tmp)
                four = sb("route_four", [P, 8, T, G], where=tmp)
                wide = sb("route_wide", [P, 6, T, G, G], where=tmp)
                rank = sb("route_rank", [P, T + 1, E], where=tmp)

                @block.sync
                def _(sp):
                    sp.dma_start(wr[:, :, :].rearrange("p c n -> p (c n)"), router[0:P, :]).then_inc(here, 16)
                    sp.dma_start(bias[:, :], router[P:P + 1, 0:20].broadcast_to([P, 20])).then_inc(here, 16)
                    sp.dma_start(row[:, :], rows[2:3, :].broadcast_to([P, D])).then_inc(here, 16)

                @block.tensor
                def _(pe):
                    pe.wait_ge(here, 48)
                    for t in range(T):
                        for n in range(2 * C):
                            lhs = (AL, AH)[n % 2][:, n // 2, t * P:(t + 1) * P].bitcast(F32)
                            mm = pe.matmul(PS[:, 0, t * 32:t * 32 + 20], lhs, wr[:, n // 2, :], start=(n == 0),
                                           stop=(n == 2 * C - 1))
                    mm.then_inc(logits_made, 1)
                    pe.wait_ge(selected, 1)
                    for t in range(T + 1):
                        for k in range(min(t, T - 1) + 1):
                            lhs = const("before") if k == t else ones[:, :]
                            mm = pe.matmul(PS[:, 1, t * E:(t + 1) * E], lhs,
                                           wide[:, 4, k, :, :].rearrange("p g e -> p (g e)"), start=(k == 0),
                                           stop=(k == min(t, T - 1)))
                    mm.then_inc(ranked, 1)

                @block.scalar
                def _(act):
                    act.wait_ge(step, 4)
                    act.activation(four[:, 1, :, :], four[:, 0, :, :], ACT.Exp).then_inc(exped, 1)
                    act.wait_ge(step, 13)
                    act.activation(four[:, 4, :, :], four[:, 3, :, :], ACT.Exp).then_inc(exped, 1)
                    act.wait_ge(logits_made, 1)
                    for t in range(T):
                        act.wait_ge(gained, t + 1)
                        act.activation(AH[:, 2 * t:2 * t + 2, :].rearrange("p a n -> p (a n)"), xs[:, t, :],
                                       ACT.Copy).then_inc(hi, 1)

                @block.vector
                def _(dve):
                    n = [0]

                    def then(ins):
                        ins.then_inc(step, 1)
                        n[0] += 1
                        dve.wait_ge(step, n[0])

                    def s(k):
                        return small[:, k, :, :]

                    def s4(k):
                        return small[:, k, :, :].broadcast_to([P, T, G])

                    def first_of_equal(out, values, most):
                        then(dve.tensor_tensor(out, values, most, ALU.is_equal))
                        then(dve.tensor_tensor(out, out, const("priority").unsqueeze(1).broadcast_to([P, T, G]),
                                               ALU.mult))
                        then(dve.tensor_reduce(s(11), out, AX_X, ALU.max))
                        then(dve.tensor_tensor(out, out, s4(11), ALU.is_equal))

                    then(dve.memset(ones[:, :], 1.0))
                    dve.wait_ge(logits_made, 1)
                    then(dve.tensor_tensor(L[:, :, :], PS[:, 0, 0:T * 32].rearrange("p (t n) -> p t n", n=32)[:, :, 0:20],
                                           bias[:, :].unsqueeze(1).broadcast_to([P, T, 20]), ALU.add))
                    then(dve.tensor_reduce(s(0), L[:, :, 0:G], AX_X, ALU.max))
                    then(dve.tensor_tensor(four[:, 0, :, :], L[:, :, 0:G], s4(0), ALU.subtract))
                    first_of_equal(four[:, 2, :, :], L[:, :, 0:G], s4(0))
                    for t in range(T):
                        ins = dve.tensor_tensor(wide[:, 0, t, :, :], L[:, t, G:G + E].rearrange("p (g e) -> p g e", e=G),
                                                four[:, 2, t, :].unsqueeze(2).broadcast_to([P, G, G]), ALU.mult)
                    then(ins)
                    for t in range(T):
                        ins = dve.tensor_reduce(four[:, 3, t, :], wide[:, 0, t, :, :].rearrange("p g e -> p e g"),
                                                AX_X, ALU.add)
                    then(ins)
                    then(dve.tensor_reduce(s(1), four[:, 3, :, :], AX_X, ALU.max))
                    then(dve.tensor_tensor(four[:, 3, :, :], four[:, 3, :, :], s4(1), ALU.subtract))
                    dve.wait_ge(exped, 1)
                    then(dve.tensor_reduce(s(2), four[:, 1, :, :], AX_X, ALU.add))
                    assert n[0] == 13
                    then(dve.reciprocal(s(3), s(2)))
                    dve.wait_ge(exped, 2)
                    then(dve.tensor_reduce(s(4), four[:, 4, :, :], AX_X, ALU.add))
                    then(dve.reciprocal(s(5), s(4)))
                    then(dve.tensor_tensor(four[:, 4, :, :], four[:, 4, :, :], s4(5), ALU.mult))
                    then(dve.tensor_reduce(s(6), four[:, 4, :, :], AX_X, ALU.max))
                    first_of_equal(four[:, 5, :, :], four[:, 4, :, :], s4(6))
                    then(dve.tensor_scalar(four[:, 6, :, :], four[:, 5, :, :], -2.0, None, ALU.mult))
                    then(dve.tensor_tensor(four[:, 4, :, :], four[:, 4, :, :], four[:, 6, :, :], ALU.add))
                    then(dve.tensor_reduce(s(7), four[:, 4, :, :], AX_X, ALU.max))
                    first_of_equal(four[:, 6, :, :], four[:, 4, :, :], s4(7))
                    for k in range(2):
                        for t in range(T):
                            ins = dve.tensor_tensor(wide[:, 2 + k, t, :, :],
                                                    four[:, 2, t, :].unsqueeze(2).broadcast_to([P, G, G]),
                                                    four[:, 5 + k, t, :].unsqueeze(1).broadcast_to([P, G, G]), ALU.mult)
                    then(ins)
                    dve.tensor_tensor(wide[:, 4, :, :, :].rearrange("p t g e -> p (t g e)"),
                                      wide[:, 2, :, :, :].rearrange("p t g e -> p (t g e)"),
                                      wide[:, 3, :, :, :].rearrange("p t g e -> p (t g e)"),
                                      ALU.add).then_inc(selected, 1)
                    then(dve.tensor_tensor(s(8), s(6), s(7), ALU.add))
                    then(dve.reciprocal(s(9), s(8)))
                    then(dve.tensor_tensor(s(9), s(9), s(3), ALU.mult))
                    dve.tensor_tensor(weight[:, 0, :], small[:, 6, :, 0], small[:, 9, :, 0], ALU.mult)
                    then(dve.tensor_tensor(weight[:, 1, :], small[:, 7, :, 0], small[:, 9, :, 0], ALU.mult))
                    dve.wait_ge(ranked, 1)
                    then(dve.tensor_copy(rank[:, :, :], PS[:, 1, 0:(T + 1) * E].rearrange("p (t e) -> p t e", e=E)))
                    dve.wait_ge(selected, 1)
                    chosen = wide[:, 4, :, :, :].rearrange("p t g e -> p t (g e)")
                    for r in range(ROUNDS):
                        ins = dve.scalar_tensor_tensor(place[:, :, r * E:(r + 1) * E], rank[:, 0:T, :], 1.0 - P * r,
                                                       chosen, ALU.add, ALU.mult)
                    then(ins)
                    then(dve.tensor_scalar(place[:, :, :], place[:, :, :], -1.0, None, ALU.add))
                    acc = wide[:, 0, :, :, :].rearrange("p t g e -> p t (g e)")
                    then(dve.tensor_tensor(acc, chosen, const("token1").unsqueeze(2).broadcast_to([P, T, E]), ALU.mult))
                    second = wide[:, 3, :, :, :].rearrange("p t g e -> p t (g e)")
                    for r in range(ROUNDS):
                        ins = dve.scalar_tensor_tensor(code[:, :, r * E:(r + 1) * E], second, float(S), acc, ALU.mult,
                                                       ALU.add)
                    then(ins)
                    then(dve.tensor_reduce(small[:, 0, 0, :], rank[:, T, :], AX_X, ALU.max))
                    for r in range(1, ROUNDS):
                        ins = dve.tensor_scalar(small[:, r, 0, :], small[:, 0, 0, :], float(P * r), None, ALU.is_gt)
                    then(ins)
                    then(dve.tensor_tensor(small[:, 1, 0, :], small[:, 1, 0, :], small[:, 2, 0, :], ALU.add))
                    then(dve.tensor_tensor(small[:, 1, 0, :], small[:, 1, 0, :], small[:, 3, 0, :], ALU.add))
                    then(dve.tensor_scalar(small[:, 2, 0, :], small[:, 1, 0, :], float(E), float(E - 1), ALU.mult,
                                           ALU.add))
                    then(dve.tensor_copy(counts[:, 0:1], small[:, 2, 0, :]))
                    dve.wait_ge(here, 48)
                    for t in range(T):
                        dve.tensor_tensor(xs[:, t, :], xs[:, t, :], row[:, :], ALU.mult).then_inc(gained, 1)
                    for t in range(T):
                        dve.wait_ge(hi, t + 1)
                        dve.tensor_tensor(AL[:, 2 * t:2 * t + 2, :].rearrange("p a n -> p (a n)"), xs[:, t, :],
                                          AH[:, 2 * t:2 * t + 2, :].rearrange("p a n -> p (a n)").bitcast(F32),
                                          ALU.subtract).then_inc(lo, 1)

        def moe_prefetch(eraw, landed):
            def issue(sp):
                for j in range(EU):
                    sp.dma_start(eraw[:, j, :], experts[0, j, :, :]).then_inc(landed[j], 16)
            return issue

        def run_experts(eraw, landed, place, code, counts):
            unit_hi = sem("expert_unit_hi")
            unit_lo = sem("expert_unit_lo")
            unit_used = sem("expert_unit_used")
            dispatch_made = sem("dispatch_made")
            gathered = sem("gathered")
            gathered_hi = sem("gathered_hi")
            gathered_lo = sem("gathered_lo")
            silued = sem("expert_silued")
            h_made = sem("expert_h_made")
            h_turned = sem("expert_h_turned")
            h_hi = sem("expert_h_hi")
            h_lo = sem("expert_h_lo")
            y_act = sem("expert_y_act")
            y_dve = sem("expert_y_dve")
            stored = sem("expert_stored")
            index_found = sem("index_found")
            index_step = sem("index_step")
            index_ready = sem("index_ready")
            store_allowed = sem("store_allowed")
            y_free = sem("expert_y_free")
            with ExitStack() as tmp, nc.Block() as block:
                WEH = sb("WEH", [P, ESLOTS, UNIT], F32R, tmp)
                WEL = sb("WEL", [P, ESLOTS, UNIT], F32R, tmp)
                dispatch = sb("dispatch", [P, T, P], F32R, tmp)
                GH = sb("GH", [P, C, P], F32R, tmp)
                GL = sb("GL", [P, C, P], F32R, tmp)
                h = sb("expert_h", [P, DE], where=tmp)
                HH = sb("HH", [P, DE // P, P], F32R, tmp)
                HL = sb("HL", [P, DE // P, P], F32R, tmp)
                y = sb("expert_y", [P, D], where=tmp)
                absent = sb("absent", [P, 1], where=tmp)
                index_next = sb("index_next", [P, 1], U32, tmp)
                index = sb("index", [P, 1], U32, tmp)
                rows_hi = AH[:, :, :].rearrange("p (t a) n -> p t (a n)", t=T)
                rows_lo = AL[:, :, :].rearrange("p (t a) n -> p t (a n)", t=T)

                @block.sync
                def _(sp):
                    final = sp.value_load(counts[0:1, 0:1], min_val=E - 1, max_val=E * ROUNDS - 1)
                    with nc.sync.Fori(0, final) as n:
                        following = (n + 1) % E
                        for j in range(EU):
                            sp.wait_ge(unit_lo, EU * n + j + 7)
                            sp.dma_start(eraw[:, j, :],
                                         experts[bass.ds(following, 1), j, :, :].rearrange("a p n -> p (a n)")
                                         ).then_inc(landed[j], 16)

                def gather(pe, n, a):
                    if a == 0:
                        pe.wait_ge(dispatch_made, n + 1)
                        pe.wait_ge(index_step, 2 * n + 1)
                        for t in range(T):
                            col = code[:, t, n:n + 1] if isinstance(n, int) else code[:, t, bass.ds(n, 1)]
                            mm = pe.matmul(PS[:, 7, 0:1], dispatch[:, t, :].bitcast(F32), col, start=(t == 0),
                                           stop=(t == T - 1))
                        mm.then_inc(index_found, 1)
                    for c in range(4 * a, 4 * a + 4):
                        for t in range(T):
                            for half in (rows_lo, rows_hi):
                                mm = pe.matmul(PS[:, 2 + a, (c % 4) * P:(c % 4 + 1) * P], half[:, t, c * P:(c + 1) * P],
                                               dispatch[:, t, :], start=(t == 0 and half is rows_lo),
                                               stop=(t == T - 1 and half is rows_hi))
                    mm.then_inc(gathered, 1)

                @block.tensor
                def _(pe):
                    final = pe.value_load(counts[0:1, 0:1], min_val=E - 1, max_val=E * ROUNDS - 1)

                    def turn(n, last):
                        pe.wait_ge(gathered_lo, 2 * n + 2)
                        for part, acc in ((0, PS[:, 0, :]), (1, PS[:, 1, :])):
                            pe.wait_ge(silued if part == 0 else h_made, n + 1)
                            for c in range(C):
                                j = 2 * part + c // 4
                                w = slice((c % 4) * DE, (c % 4 + 1) * DE)
                                if c % 4 == 0:
                                    pe.wait_ge(unit_lo, EU * n + j + 7)
                                mm = product(pe, acc, GH[:, c, :], GL[:, c, :], WEH[:, j % ESLOTS, w],
                                             WEL[:, j % ESLOTS, w], c == 0, c == C - 1)
                                if c % 4 == 3:
                                    mm.then_inc(unit_used, 1)
                        if not last:
                            gather(pe, n + 1, 0)
                        pe.wait_ge(h_made, n + 2)
                        for k in range(DE // P):
                            mm = pe.transpose(PS[:, 4, k * P:(k + 1) * P], h[:, k * P:(k + 1) * P], ident)
                        mm.then_inc(h_turned, 1)
                        if not last:
                            gather(pe, n + 1, 1)
                        pe.wait_ge(h_lo, n + 1)
                        pe.wait_ge(y_act, n + 1)
                        pe.wait_ge(y_dve, n + 1)
                        for k in range(DE // P):
                            j = 4 + k // 2
                            if k % 2 == 0:
                                pe.wait_ge(unit_lo, EU * n + j + 7)
                            for half in range(2):
                                w = slice((k % 2) * D + half * 512, (k % 2) * D + half * 512 + 512)
                                mm = product(pe, PS[:, 5 + half, :], HH[:, k, :], HL[:, k, :], WEH[:, j % ESLOTS, w],
                                             WEL[:, j % ESLOTS, w], k == 0, k == DE // P - 1)
                            if k % 2:
                                mm.then_inc(unit_used, 1)

                    gather(pe, 0, 0)
                    gather(pe, 0, 1)
                    with nc.tensor.Fori(0, final) as n:
                        turn(n, False)
                    turn(final, True)

                @block.scalar
                def _(act):
                    final = act.value_load(counts[0:1, 0:1], min_val=E - 1, max_val=E * ROUNDS - 1)

                    def hi(n, j):
                        act.wait_ge(landed[j], 16 * n + 16)
                        act.wait_ge(unit_used, EU * n + j + 1)
                        act.activation(WEH[:, j % ESLOTS, :], eraw[:, j, :], ACT.Copy).then_inc(unit_hi, 1)

                    def gathered_out(n, a):
                        act.wait_ge(gathered, 2 * n + a + 1)
                        act.activation(GH[:, 4 * a:4 * a + 4, :], PS[:, 2 + a, :].rearrange("p (c s) -> p c s", s=P),
                                       ACT.Copy).then_inc(gathered_hi, 1)

                    def turn(n, last):
                        hi(n, 3)
                        act.wait_ge(unit_used, EU * n + 5)
                        act.wait_ge(h_turned, n + 1)
                        act.activation(h[:, :], PS[:, 0, :], ACT.Silu).then_inc(silued, 1)
                        hi(n, 4)
                        hi(n, 5)
                        if not last:
                            hi(n + 1, 0)
                            gathered_out(n + 1, 0)
                        act.wait_ge(h_turned, n + 2)
                        act.wait_ge(unit_used, EU * n + 3)
                        act.activation(HH[:, :, :], PS[:, 4, :].rearrange("p (k s) -> p k s", s=P),
                                       ACT.Copy).then_inc(h_hi, 1)
                        if not last:
                            gathered_out(n + 1, 1)
                            hi(n + 1, 1)
                            hi(n + 1, 2)
                        act.wait_ge(unit_used, EU * n + 9)
                        act.wait_ge(y_free, n + 1)
                        act.activation(y[:, 0:512], PS[:, 5, :], ACT.Copy).then_inc(y_act, 1)

                    for j in range(3):
                        hi(0, j)
                    gathered_out(0, 0)
                    gathered_out(0, 1)
                    with nc.scalar.Fori(0, final) as n:
                        turn(n, False)
                    turn(final, True)

                @block.vector
                def _(dve):
                    final = dve.value_load(counts[0:1, 0:1], min_val=E - 1, max_val=E * ROUNDS - 1)

                    def lo(n, j):
                        dve.wait_ge(unit_hi, EU * n + j + 1)
                        dve.tensor_tensor(WEL[:, j % ESLOTS, :], eraw[:, j, :], WEH[:, j % ESLOTS, :].bitcast(F32),
                                          ALU.subtract).then_inc(unit_lo, 1)

                    def build_dispatch(n):
                        for t in range(T):
                            col = place[:, t, n:n + 1] if isinstance(n, int) else place[:, t, bass.ds(n, 1)]
                            ins = dve.tensor_scalar(dispatch[:, t, :], const("iota"), col, None, ALU.is_equal)
                        ins.then_inc(dispatch_made, 1)

                    def gathered_out(n, a):
                        dve.wait_ge(gathered_hi, 2 * n + a + 1)
                        dve.tensor_tensor(GL[:, 4 * a:4 * a + 4, :], PS[:, 2 + a, :].rearrange("p (c s) -> p c s", s=P),
                                          GH[:, 4 * a:4 * a + 4, :].bitcast(F32), ALU.subtract).then_inc(gathered_lo, 1)

                    def find_index(n):
                        dve.wait_ge(index_found, n + 1)
                        dve.tensor_scalar(absent[:, :], PS[:, 7, 0:1], 0.0, 2.0 * S + 1.0, ALU.is_equal,
                                          ALU.mult).then_inc(index_step, 1)
                        dve.wait_ge(index_step, 2 * n + 2)
                        dve.wait_ge(index_ready, n + 1)
                        dve.scalar_tensor_tensor(index_next[:, :], PS[:, 7, 0:1], -1.0, absent[:, :], ALU.add,
                                                 ALU.add).then_inc(index_step, 1)

                    def turn(n, last):
                        if not last:
                            dve.wait_ge(gathered, 2 * n + 2)
                            build_dispatch(n + 1)
                        lo(n, 3)
                        lo(n, 4)
                        dve.wait_ge(index_step, 2 * n + 3)
                        dve.wait_ge(y_free, n + 1)
                        dve.tensor_copy(index[:, :], index_next[:, :]).then_inc(index_ready, 1)
                        dve.wait_ge(silued, n + 2)
                        dve.wait_ge(unit_used, EU * n + 7)
                        dve.tensor_tensor(h[:, :], h[:, :], PS[:, 1, :], ALU.mult).then_inc(h_made, 1)
                        lo(n, 5)
                        if not last:
                            gathered_out(n + 1, 0)
                        dve.wait_ge(h_hi, n + 1)
                        dve.tensor_tensor(HL[:, :, :], PS[:, 4, :].rearrange("p (k s) -> p k s", s=P),
                                          HH[:, :, :].bitcast(F32), ALU.subtract).then_inc(h_lo, 1)
                        if not last:
                            lo(n + 1, 0)
                            find_index(n + 1)
                            gathered_out(n + 1, 1)
                            lo(n + 1, 1)
                        dve.wait_ge(unit_used, EU * n + 9)
                        dve.wait_ge(y_free, n + 1)
                        dve.tensor_copy(y[:, 512:1024], PS[:, 6, :]).then_inc(y_dve, 1)
                        if not last:
                            lo(n + 1, 2)

                    dve.sem_inc(unit_lo, 6)
                    build_dispatch(0)
                    for j in range(3):
                        lo(0, j)
                    find_index(0)
                    gathered_out(0, 0)
                    gathered_out(0, 1)
                    with nc.vector.Fori(0, final) as n:
                        turn(n, False)
                    turn(final, True)

                @block.gpsimd
                def _(pool):
                    pool.sem_inc(unit_used, 3)
                    for one_turn_back in (y_free, silued, h_made, h_turned, y_act, y_dve, index_step, index_ready):
                        pool.sem_inc(one_turn_back, 1)
                    final = pool.value_load(counts[0:1, 0:1], min_val=E - 1, max_val=E * ROUNDS - 1)
                    bound = pool.to_reg(2 * S - 1)
                    with nc.gpsimd.Fori(0, final + 1) as n:
                        pool.wait_ge(index_ready, n + 2)
                        pool.wait_ge(y_act, n + 2)
                        pool.wait_ge(y_dve, n + 2)
                        pool.sem_inc(store_allowed, 1)
                        pool.indirect_dma_start(scratch[:, :], bass.IndirectOffsetOnAxis(index[:, 0:1], 0), y[:, :],
                                                None, bounds_check=bound, oob_is_err=False).then_inc(stored, 16)
                        pool.wait_ge(stored, 16 * n + 16)
                        pool.sem_inc(y_free, 1)

        def combine(weight):
            fetched = [sem(f"fetched{n}") for n in range(2 * T)]
            summed = sem("summed")
            out_stored = sem("out_stored")
            with ExitStack() as tmp, nc.Block() as block:
                got = sb("got", [P, T, 2, D], where=tmp)

                @block.vector
                def _(dve):
                    for t in range(T):
                        for k in range(2):
                            dve.wait_ge(fetched[2 * t + k], 16)
                            if k:
                                dve.wait_ge(summed, 2 * t + 1)
                            dve.scalar_tensor_tensor(X[:, t, :], got[:, t, k, :], weight[:, k, t:t + 1], X[:, t, :],
                                                     ALU.mult, ALU.add).then_inc(summed, 1)

                @block.sync
                def _(sp):
                    for t in range(T):
                        for k in range(2):
                            sp.dma_start(got[:, t, k, :], scratch[k * S + t * P:k * S + (t + 1) * P, :]
                                         ).then_inc(fetched[2 * t + k], 16)
                    for t in range(T):
                        sp.wait_ge(summed, 2 * t + 2)
                        sp.dma_start(out[t * P:(t + 1) * P, :], X[:, t, :]).then_inc(out_stored, 16)
                    sp.wait_ge(out_stored, 16 * T)

        def finish():
            stored = sem("stored")
            with nc.Block() as block:
                @block.sync
                def _(sp):
                    sp.dma_start(out.rearrange("(t p) d -> p t d", p=P), X[:, :, :]).then_inc(stored, 16)
                    sp.wait_ge(stored, 16)

        setup()
        with ExitStack() as tmp:
            xs = sb("pool_xs", [P, T, D], where=tmp)
            bands = sb("pool_bands", [P, BAND_WIDTH], where=tmp)
            scale_row = sb("pool_scale_row", [P, D], where=tmp)
            normalize("n0", xs, None, (0, 1))
            pool_stage(xs, bands, scale_row, rows[0:1, :].broadcast_to([P, D]))
        if stop == 1:
            return finish()

        def norm_turn(tag, gain_name, units):
            with ExitStack() as tmp:
                xs = sb(tag + "xs", [P, T, D], where=tmp)
                normalize(tag, xs, gain_name, units)

        norm_turn("n1", "ffn0", (U_FFN0 + 1,))
        swiglu("f0", U_FFN0)
        if stop == 2:
            return finish()

        with ExitStack() as held:
            QN = sb("QN", [P, H, S], where=held)
            KN = sb("KN", [P, H, S], where=held)
            QR = sb("QR", [P, H // 2, S], where=held)
            KR = sb("KR", [P, S], where=held)
            V = sb("V", [P, T, D], where=held)
            norm_turn("n2", "mix1", (U_MLA, U_MLA + 1))
            with ExitStack() as tmp:
                CTH = sb("CTH", [P, 4, S], F32R, tmp)
                CTL = sb("CTL", [P, 4, S], F32R, tmp)
                rot = sb("rot", [P, 2, T, 32], where=tmp)
                mla_down(CTH, CTL, KR, rot)
                mla_up(CTH, CTL, rot, QN, QR, KN, V)
            O = sb("mla_O", [P, T, D], where=held)

            def mla_scores(pe, h, q, m, acc):
                keys = slice(0, (q + 1) * P)
                mine = slice(q * P, (q + 1) * P)
                half = slice((h % 2) * 64, (h % 2) * 64 + 64)
                pe.matmul(acc, QN[:, h, mine], KN[:, h, keys], start=True, stop=False)
                pe.matmul(acc, QR[half, h // 2, mine], KR[half, keys], start=False, stop=False)
                return pe.matmul(acc[:, q * P:(q + 1) * P], identr[:, :], causalr[:, :], start=False, stop=True)

            attend("m", 1, mla_scores, V, O, (U_MLA + 8,))
            attention_out("mo", O, U_MLA_OUT, None, U_FFN1 + 2)
        if stop == 3:
            return finish()
        recycle()
        norm_turn("n3", "ffn1", (U_FFN1, U_FFN1 + 1))
        swiglu("f1", U_FFN1)
        if stop == 4:
            return finish()
        final_norm()
        if stop == 5:
            return finish()
        with ExitStack() as held:
            V = sb("da_V", [P, T, D], where=held)
            with ExitStack() as tmp:
                norm_turn("n4", "mix2", (U_DA, U_DA + 1))
                QT = sb("QT", [P, H, S], where=held)
                KT = sb("KT", [P, H, S], where=held)
                QK = sb("QK", [P, T, 2 * D], where=tmp)
                da_in(QK, V)
                da_turn(QK, QT, KT)
            O = sb("da_O", [P, T, D], where=held)
            slopes = sb("slopes", [P, H, P], F32R, held)
            alibir = sb("alibir", [P, S], F32R, held)

            def prepare(tmp, block, ready):
                lam_here = sem("lam_here")
                lam_step = sem("lam_step")
                lam_exp = sem("lam_exp")
                lam = sb("lam", [P, 4, 64], where=tmp)
                ls = sb("lam_s", [P, 8], where=tmp)

                @block.sync
                def _(sp):
                    sp.dma_start(lam[:, :, :].rearrange("p a n -> p (a n)"),
                                 lams.broadcast_to([P, 256])).then_inc(lam_here, 16)

                @block.scalar
                def _(act):
                    act.wait_ge(lam_step, 2)
                    act.activation(ls[:, 2:4], ls[:, 0:2], ACT.Exp).then_inc(lam_exp, 1)

                @block.vector
                def _(dve):
                    for h in range(H):
                        dve.tensor_scalar(slopes[:, h, :], ident, 2.0 ** (-8.0 * (h + 1) / H), None,
                                          ALU.mult).then_inc(ready, 1)
                    dve.tensor_copy(alibir[:, :], const("alibi")).then_inc(ready, 1)
                    dve.wait_ge(lam_here, 16)
                    for k in range(2):
                        dve.tensor_tensor_reduce(lam[:, 2 * k, :], lam[:, 2 * k, :], lam[:, 2 * k + 1, :], 1.0, 0.0,
                                                 ALU.mult, ALU.add, ls[:, k:k + 1]).then_inc(lam_step, 1)
                    dve.wait_ge(lam_exp, 1)
                    dve.tensor_tensor(ls[:, 4:5], ls[:, 3:4], ls[:, 2:3], ALU.subtract).then_inc(lam_step, 1)
                    dve.wait_ge(lam_step, 3)
                    dve.tensor_scalar(ls[:, 5:6], ls[:, 4:5], -LAMBDA_INIT, None, ALU.add).then_inc(lam_step, 1)
                    dve.wait_ge(lam_step, 4)

                return ls[:, 5:6], H + 1

            def da_scores(pe, h, q, m, acc):
                half = slice(m * 64, m * 64 + 64)
                pe.matmul(acc, QT[half, h, q * P:(q + 1) * P], KT[half, h, 0:(q + 1) * P], start=True, stop=False)
                return pe.matmul(acc, slopes[:, h, :], alibir[:, S - (q + 1) * P:S], start=False, stop=True)

            attend("d", 2, da_scores, V, O, (U_DA_OUT, U_DA_OUT + 1), prepare)
            attention_out("do", O, U_DA_OUT, gain_col("da_sub"), U_END, True)
        if stop == 6:
            return finish()
        recycle()
        wctx.close()
        place = sb("place", [P, T, ROUNDS * E])
        weight = sb("weight", [P, 2, T])
        code = sb("code", [P, T, ROUNDS * E])
        counts = sb("counts", [P, 1], I32)
        landed = [sem(f"expert_landed{j}") for j in range(EU)]
        with ExitStack() as tmp:
            eraw = sb("eraw", [P, EU, UNIT], where=tmp)
            with ExitStack() as tmp2:
                xs = sb("moe_xs", [P, T, D], where=tmp2)
                normalize("n5", xs, "moe", (), moe_prefetch(eraw, landed))
                route(xs, place, weight, code, counts)
            run_experts(eraw, landed, place, code, counts)
        combine(weight)


def lay_out(a):
    units = np.zeros((U_END, P, UNIT), np.float32)

    def chunks(w):
        return w.reshape(w.shape[0] // P, P, w.shape[1]).transpose(1, 0, 2)

    units[U_POOL] = a["pool_w"][0].reshape(4, 2, P, 256).transpose(2, 0, 1, 3).reshape(P, UNIT)
    for layer, u0 in ((0, U_FFN0), (1, U_FFN1)):
        for part, w in ((0, a["ffn_w_gate"][layer]), (1, a["ffn_w_up"][layer])):
            v = chunks(w).reshape(P, C, FC // 2, 256)
            units[u0 + part:u0 + FC:2] = v.transpose(2, 0, 1, 3).reshape(FC // 2, P, UNIT)
        v = chunks(a["ffn_w_down"][layer]).reshape(P, FC // 2, UNIT)
        units[u0 + FC:u0 + FFN_UNITS] = v.transpose(1, 0, 2)
    w = chunks(a["mla_w_down"][0])
    units[U_MLA] = w[:, 0:4, 0:512].reshape(P, UNIT)
    units[U_MLA + 1] = w[:, 4:8, 0:512].reshape(P, UNIT)
    units[U_MLA + 2, :, 0:512] = w[:, :, 512:576].reshape(P, 512)
    w = chunks(a["mla_w_uq"][0]).reshape(P, 3, H, 192)
    units[U_MLA + 3, :, 0:1536] = w[:, :, :, 128:192].reshape(P, 1536)
    units[U_MLA + 4, :, 0:1536] = w[:, :, 0:4, 0:128].reshape(P, 1536)
    units[U_MLA + 5, :, 0:1536] = w[:, :, 4:8, 0:128].reshape(P, 1536)
    units[U_MLA + 6] = a["mla_w_ukv"][0].reshape(P, H, 2, P).transpose(0, 2, 1, 3).reshape(P, UNIT)
    units[U_MLA_OUT:U_MLA_OUT + 4] = chunks(a["mla_w_o"][0]).reshape(P, 4, UNIT).transpose(1, 0, 2)
    v = chunks(a["da_w_in_2"][0]).reshape(P, 2, 4, 6, 512)
    units[U_DA:U_DA + 12] = v.transpose(3, 1, 0, 2, 4).reshape(12, P, UNIT)
    units[U_DA_OUT:U_DA_OUT + 4] = chunks(a["da_w_out_2"][0]).reshape(P, 4, UNIT).transpose(1, 0, 2)
    experts = np.zeros((E, EU, P, UNIT), np.float32)
    for part, name in ((0, "moe_w_gate_2"), (2, "moe_w_up_2")):
        v = a[name][0].reshape(E, 2, 4, P, DE)
        experts[:, part:part + 2] = v.transpose(0, 1, 3, 2, 4).reshape(E, 2, P, UNIT)
    v = a["moe_w_down_2"][0].reshape(E, 2, 2, P, D)
    experts[:, 4:6] = v.transpose(0, 1, 3, 2, 4).reshape(E, 2, P, UNIT)
    gains = np.zeros((P, GAIN_WIDTH), np.float32)
    for name, v in (("mix0", a["norm_mix"][0]), ("ffn0", a["norm_ffn"][0]), ("mix1", a["norm_mix"][1]),
                    ("ffn1", a["norm_ffn"][1]), ("mix2", a["norm_mix_2"][0]), ("moe", a["norm_ffn_2"][0]),
                    ("q_lora", a["mla_q_norm"][0]), ("kv_lora", a["mla_kv_norm"][0]),
                    ("da_q", np.concatenate([a["da_q_norm_2"][0]] * 2)),
                    ("da_k", np.concatenate([a["da_k_norm_2"][0]] * 2)), ("da_sub", a["da_subln_2"][0])):
        c, w = GAIN_COLS[name]
        gains[:, c:c + w] = v.reshape(w, P).T
    rows = np.stack([a["pool_scale"][0], a["norm_final"], a["norm_ffn_2"][0]])
    router = np.zeros((P + 1, C, 20), np.float32)
    router[0:P, :, 0:4] = chunks(a["moe_w_group_2"][0])
    router[0:P, :, 4:20] = chunks(a["moe_w_router_2"][0])
    router[P, 0, 0:4] = a["moe_b_group_2"][0]
    router[P, 0, 4:20] = a["moe_b_router_2"][0]
    lams = np.stack([a["da_lambda_q1_2"][0], a["da_lambda_k1_2"][0], a["da_lambda_q2_2"][0], a["da_lambda_k2_2"][0]])
    consts, band = constants()
    return {
        "stream": units, "experts": experts, "x": a["x"][0], "positions": a["positions"][0].reshape(T, P).T,
        "gains": gains, "rows": rows, "lams": lams.reshape(1, 4 * 64), "router": router.reshape(P + 1, C * 20),
        "consts": consts, "band": band,
    }


def kernel(**inputs):
    import concourse.bacc as bacc
    from concourse.bass_utils import run_bass_kernel_spmd

    arrays = {k: np.ascontiguousarray(v) for k, v in lay_out({k: np.asarray(v) for k, v in inputs.items()}).items()}
    nc = bacc.Bacc("TRN2", target_bir_lowering=False, num_devices=1)
    aps = {k: nc.dram_tensor(k, v.shape, mybir.dt.from_np(v.dtype), kind="ExternalInput").ap()
           for k, v in arrays.items()}
    aps["out"] = nc.dram_tensor("out", (S, D), F32, kind="ExternalOutput").ap()
    aps["scratch"] = nc.dram_tensor("scratch", (2 * S, D), F32, kind="Internal").ap()
    build_program(nc, **aps)
    r = run_bass_kernel_spmd(nc, [arrays], core_ids=[0])
    return r.results[0]["out"].reshape(1, S, D)
```

```python
from contextlib import ExitStack

import numpy as np
import concourse.bass as bass
from concourse import mybir

F32 = mybir.dt.float32
F32R = mybir.dt.float32r
I32 = mybir.dt.int32
U32 = mybir.dt.uint32
ALU = mybir.AluOpType
ACT = mybir.ActivationFunctionType
AX_X = mybir.AxisListType.X

P = 128
S = 512
T = S // P
D = 1024
C = D // P
F = 2816
FC = F // P
EPS = 1e-6
UNIT = 2048
SLOTS = 2
POOL_WINDOWS = (2, 4, 8, 16)
H = 8
ROPE = 64
Q_LORA = 384
KV_LORA = 128
MLA_SCALE = 192.0 ** -0.5
ROPE_THETA = 10000.0
NEG = -1e30
LAMBDA_INIT = 0.2
G = 4
E = 16
DE = 512
EU = 6
ESLOTS = 3
ROUNDS = S // P

U_POOL = 0
U_FFN0 = 1
FFN_UNITS = 3 * FC // 2
U_MLA = U_FFN0 + FFN_UNITS
U_MLA_OUT = U_MLA + 7
U_FFN1 = U_MLA + 11
U_DA = U_FFN1 + FFN_UNITS
U_DA_OUT = U_DA + 12
U_END = U_DA + 16

CONST_COLS = {}
_at = 0
for _name, _width in (("ident", P), ("causal", P), ("alibi", S), ("before", P), ("iota", P),
                      ("inv_freq", ROPE // 2), ("token1", T), ("priority", G)):
    CONST_COLS[_name] = (_at, _width)
    _at += _width
CONST_WIDTH = _at
BAND_WIDTH = 4 * (P + P + 16)

GAIN_COLS = {}
_at = 0
for _name, _width in (("mix0", C), ("ffn0", C), ("mix1", C), ("ffn1", C), ("mix2", C), ("moe", C),
                      ("q_lora", 3), ("kv_lora", 1), ("da_q", 1), ("da_k", 1), ("da_sub", 1)):
    GAIN_COLS[_name] = (_at, _width)
    _at += _width
GAIN_WIDTH = _at


def constants():
    p = np.arange(P)
    out = np.zeros((P, CONST_WIDTH), np.float32)

    def put(name, value):
        a, w = CONST_COLS[name]
        out[:, a:a + w] = value

    put("ident", np.eye(P))
    put("causal", np.where(p[None, :] <= p[:, None], 0.0, NEG))
    dist = p[:, None] + (S - P) - np.arange(S)[None, :]
    put("alibi", np.where(dist >= 0, -dist, NEG))
    put("before", p[:, None] < p[None, :])
    put("iota", np.broadcast_to(p[None, :], (P, P)))
    inv = np.float32(1.0) / np.float32(ROPE_THETA) ** (np.arange(0, ROPE, 2, dtype=np.float32) / np.float32(ROPE))
    put("inv_freq", inv[None, :])
    put("token1", p[:, None] + P * np.arange(T)[None, :] + 1)
    put("priority", (G - np.arange(G))[None, :])
    band = np.zeros((P, BAND_WIDTH), np.float32)
    for g, win in enumerate(POOL_WINDOWS):
        t, s = p[:, None], p[None, :]
        inside = (s - win < t) & (t <= s)
        first = np.where(inside, 1.0 / np.minimum(s + 1, win), 0.0) - (s == t)
        rest = np.where(inside, 1.0 / win, 0.0) - (s == t)
        s = np.arange(16)[None, :]
        prev = np.where(s + P - win < t, 1.0 / win, 0.0)
        band[:, g * P:(g + 1) * P] = first
        band[:, (4 + g) * P:(5 + g) * P] = rest
        band[:, 8 * P + 16 * g:8 * P + 16 * (g + 1)] = prev
    return out, band


def build_program(nc, stream, experts, x, positions, gains, rows, lams, router, consts, band, out, scratch):
    ctx = ExitStack()
    with ctx:
        def sb(name, shape, dt=F32, where=None):
            return (where or ctx).enter_context(nc.sbuf_tensor(name, shape, dt))

        stage_sems = []

        def lasting(name):
            return nc.alloc_semaphore(name)

        def sem(name):
            stage_sems.append(nc.alloc_semaphore(name))
            return stage_sems[-1]

        def recycle():
            nc.clear_and_free_semaphores(list(stage_sems))
            stage_sems.clear()
            nc.all_engine_barrier()

        PS = ctx.enter_context(nc.psum_tensor("PS", [P, 8, 512], F32))
        X = sb("X", [P, T, D])
        cst = sb("cst", [P, CONST_WIDTH])
        gain = sb("gain", [P, GAIN_WIDTH])
        identr = sb("identr", [P, P], F32R)
        causalr = sb("causalr", [P, P], F32R)
        rstd = sb("rstd", [P, 8])
        spare = sb("spare", [P, 8])
        final_row = sb("final_row", [P, D])
        AH = sb("AH", [P, C, S], F32R)
        AL = sb("AL", [P, C, S], F32R)
        wctx = ctx.enter_context(ExitStack())
        raw = sb("raw", [P, SLOTS, UNIT], where=wctx)
        WH = sb("WH", [P, SLOTS, UNIT], F32R, where=wctx)
        WL = sb("WL", [P, SLOTS, UNIT], F32R, where=wctx)

        def const(name):
            a, w = CONST_COLS[name]
            return cst[:, a:a + w]

        def gain_col(name, c=0):
            a, _ = GAIN_COLS[name]
            return gain[:, a + c:a + c + 1]

        ident = const("ident")

        final_row_here = lasting("final_row_here")
        unit_landed = [lasting(f"unit_landed{k}") for k in range(SLOTS)]
        unit_hi = lasting("unit_hi")
        unit_lo = lasting("unit_lo")
        unit_used = lasting("unit_used")

        def load_unit(sp, u, turn=0):
            v = u + SLOTS * turn
            if u >= SLOTS:
                sp.wait_ge(unit_lo, v - SLOTS + 1)
            src = stream[u, :, :] if isinstance(turn, int) else stream[bass.ds(v, 1), :, :].rearrange("a p n -> p (a n)")
            sp.dma_start(raw[:, u % SLOTS, :], src).then_inc(unit_landed[u % SLOTS], 16)

        def split_hi(act, u, turn=0):
            act.wait_ge(unit_landed[u % SLOTS], 16 * (u // SLOTS + 1) + 16 * turn)
            if u >= SLOTS:
                act.wait_ge(unit_used, u - SLOTS + 1 + SLOTS * turn)
            act.activation(WH[:, u % SLOTS, :], raw[:, u % SLOTS, :], ACT.Copy).then_inc(unit_hi, 1)

        def split_lo(dve, u, turn=0):
            dve.wait_ge(unit_hi, u + 1 + SLOTS * turn)
            dve.tensor_tensor(WL[:, u % SLOTS, :], raw[:, u % SLOTS, :], WH[:, u % SLOTS, :].bitcast(F32),
                              ALU.subtract).then_inc(unit_lo, 1)

        def product(pe, acc, lhs_hi, lhs_lo, rhs_hi, rhs_lo, start, stop):
            pe.matmul(acc, lhs_lo, rhs_hi, start=start, stop=False)
            pe.matmul(acc, lhs_hi, rhs_lo, start=False, stop=False)
            return pe.matmul(acc, lhs_hi, rhs_hi, start=False, stop=stop)

        def setup(block, bands, scale_row):
            tile_here = [sem(f"x_tile{t}_here") for t in range(T)]
            gains_here = sem("gains_here")
            consts_here = sem("consts_here")
            tables_here = sem("pool_tables_here")
            row_here = sem("pool_row_here")
            copied = sem("constants_copied")

            @block.sync
            def _(sp):
                for t in range(T):
                    sp.dma_start(X[:, t, :], x[t * P:(t + 1) * P, :]).then_inc(tile_here[t], 16)
                sp.dma_start(bands[:, :], band[:, :]).then_inc(tables_here, 16)
                load_unit(sp, 0)
                sp.dma_start(scale_row[:, :], rows[0:1, :].broadcast_to([P, D])).then_inc(row_here, 16)
                sp.dma_start(cst[:, :], consts[:, :]).then_inc(consts_here, 16)
                load_unit(sp, 1)
                sp.dma_start(final_row[:, :], rows[1:2, :].broadcast_to([P, D])).then_inc(final_row_here, 16)
                load_unit(sp, 2)

            @block.scalar
            def _(act):
                act.dma_start(gain[:, :], gains[:, :]).then_inc(gains_here, 16)
                act.wait_ge(gains_here, 16)
                act.activation(spare[:, 0:1], gain[:, 0:1], ACT.Square).then_inc(copied, 1)
                act.wait_ge(copied, 1)
                act.activation(spare[:, 1:2], spare[:, 0:1], ACT.Sqrt).then_inc(copied, 1)

            def derive(dve):
                dve.wait_ge(consts_here, 16)
                dve.tensor_copy(identr[:, :], ident).then_inc(copied, 1)
                dve.tensor_copy(causalr[:, :], const("causal")).then_inc(copied, 1)
                a = GAIN_COLS["da_q"][0]
                dve.tensor_scalar(gain[:, a:a + 1], gain[:, a:a + 1], 0.125, None, ALU.mult).then_inc(copied, 1)
                a = GAIN_COLS["da_sub"][0]
                dve.tensor_scalar(gain[:, a:a + 1], gain[:, a:a + 1], 1.0 - LAMBDA_INIT, None,
                                  ALU.mult).then_inc(copied, 1)

            return tile_here, tables_here, row_here, derive

        def invert_root(block, tag, before_act, before_dve):
            meaned = sem(tag + "meaned")
            rooted = sem(tag + "rooted")
            inverted = sem(tag + "inverted")

            @block.scalar
            def _(act):
                before_act(act)
                act.wait_ge(meaned, 1)
                act.activation(rstd[:, 4:8], rstd[:, 0:4], ACT.Sqrt).then_inc(rooted, 1)

            @block.vector
            def _(dve):
                before_dve(dve)
                dve.tensor_scalar(rstd[:, 0:4], rstd[:, 0:4], 1.0 / D, EPS, ALU.mult, ALU.add).then_inc(meaned, 1)
                dve.wait_ge(rooted, 1)
                dve.reciprocal(rstd[:, 0:4], rstd[:, 4:8]).then_inc(inverted, 1)
                dve.wait_ge(inverted, 1)

        def normalize(block, tag, xs, gain_name=None, split=(), junk=None, tile_here=None,
                      halves=(AH, AL), act_tiles=range(0, T, 2), meanwhile=None):
            out_hi, out_lo = halves
            dve_tiles = [t for t in range(T) if t not in act_tiles]
            squared_a = sem(tag + "squared_act")
            squared_v = sem(tag + "squared_dve")
            scaled = sem(tag + "scaled")
            turned = sem(tag + "turned")
            hi = sem(tag + "hi")
            lo = sem(tag + "lo")

            def squares_act(act):
                if junk is not None:
                    for n, t in enumerate(act_tiles):
                        tile_here(act, t)
                        if n >= 2:
                            act.wait_ge(squared_a, n - 1)
                        act.activation(junk[:, n % 2, :], X[:, t, :], ACT.Square,
                                       accum_out=rstd[:, t:t + 1]).then_inc(squared_a, 1)

            def squares_dve(dve):
                if junk is not None:
                    for t in dve_tiles:
                        tile_here(dve, t)
                        dve.tensor_tensor_reduce(xs[:, t, :], X[:, t, :], X[:, t, :], 1.0, 0.0, ALU.mult, ALU.add,
                                                 rstd[:, t:t + 1]).then_inc(squared_v, 1)
                    dve.wait_ge(squared_a, len(act_tiles))
                    if dve_tiles:
                        dve.wait_ge(squared_v, len(dve_tiles))

            invert_root(block, tag, squares_act, squares_dve)

            @block.scalar
            def _(act):
                if meanwhile:
                    meanwhile[0](act)
                for u in split:
                    split_hi(act, u)
                if gain_name:
                    for c in range(C):
                        act.wait_ge(turned, c + 1)
                        act.activation(out_hi[:, c, :], PS[:, c, :], ACT.Copy,
                                       scale=gain_col(gain_name, c)).then_inc(hi, 1)

            @block.vector
            def _(dve):
                for t in range(T):
                    dve.tensor_scalar(xs[:, t, :], X[:, t, :], rstd[:, t:t + 1], None, ALU.mult).then_inc(scaled, 1)
                if meanwhile:
                    meanwhile[1](dve)
                for u in split:
                    split_lo(dve, u)
                if gain_name:
                    for c in range(C):
                        dve.wait_ge(hi, c + 1)
                        dve.scalar_tensor_tensor(out_lo[:, c, :], PS[:, c, :], gain_col(gain_name, c),
                                                 out_hi[:, c, :].bitcast(F32), ALU.mult, ALU.subtract).then_inc(lo, 1)

            @block.tensor
            def _(pe):
                if gain_name:
                    for t in range(T):
                        pe.wait_ge(scaled, t + 1)
                        for c in range(C):
                            mm = pe.transpose(PS[:, c, t * P:(t + 1) * P], xs[:, t, c * P:(c + 1) * P], ident)
                            if t == T - 1:
                                mm.then_inc(turned, 1)

            return scaled, turned, lo

        def pool_stage():
            pooled = sem("pooled")
            hi = sem("pooled_hi")
            lo = sem("pooled_lo")
            mixed = sem("pool_mixed")
            weighed = sem("pool_weighed")
            added = sem("pool_added")
            with ExitStack() as tmp, nc.Block() as block:
                xs = sb("pool_xs", [P, T, D], where=tmp)
                junk = sb("pool_junk", [P, 2, D], where=tmp)
                bands = sb("pool_bands", [P, BAND_WIDTH], where=tmp)
                scale_row = sb("pool_scale_row", [P, D], where=tmp)
                tile_here, tables_here, row_here, derive = setup(block, bands, scale_row)
                scaled, _, _ = normalize(block, "n0", xs, None, (0,), junk,
                                      lambda engine, t: engine.wait_ge(tile_here[t], 16))

                @block.tensor
                def _(pe):
                    pe.wait_ge(tables_here, 16)
                    for c in range(C):
                        g = c // 2
                        for t in range(T):
                            if c == 0:
                                pe.wait_ge(scaled, t + 1)
                            here = bands[:, (g if t == 0 else 4 + g) * P:(g + 1 if t == 0 else 5 + g) * P]
                            mm = pe.matmul(PS[:, c, t * P:(t + 1) * P], xs[:, t, c * P:(c + 1) * P], here,
                                           start=True, stop=(t == 0))
                            if t:
                                mm = pe.matmul(PS[:, c, t * P:t * P + 16], xs[:, t - 1, c * P:(c + 1) * P],
                                               bands[:, 8 * P + 16 * g:8 * P + 16 * (g + 1)], start=False, stop=True)
                        mm.then_inc(pooled, 1)
                    pe.wait_ge(unit_lo, U_POOL + 1)
                    for t in range(T):
                        for g in range(4):
                            for k in range(2):
                                c = 2 * g + k
                                if t == 0:
                                    pe.wait_ge(lo, c + 1)
                                w = slice(c * 256, (c + 1) * 256)
                                mm = product(pe, PS[:, 2 * t + g // 2, (g % 2) * 256:(g % 2 + 1) * 256],
                                             AH[:, c, t * P:(t + 1) * P], AL[:, c, t * P:(t + 1) * P],
                                             WH[:, 0, w], WL[:, 0, w], k == 0, k == 1)
                        mm.then_inc(mixed, 1)
                    pe.wait_ge(mixed, T)
                    pe.sem_inc(unit_used, 1)

                @block.scalar
                def _(act):
                    for c in range(C):
                        act.wait_ge(pooled, c + 1)
                        act.activation(AH[:, c, :], PS[:, c, :], ACT.Copy,
                                       scale=gain_col("mix0", c)).then_inc(hi, 1)
                    split_hi(act, U_FFN0)
                    square_sums(act, added, sem("n0_next_summed"), junk, range(T))

                @block.vector
                def _(dve):
                    for c in range(C):
                        dve.wait_ge(hi, c + 1)
                        dve.scalar_tensor_tensor(AL[:, c, :], PS[:, c, :], gain_col("mix0", c),
                                                 AH[:, c, :].bitcast(F32), ALU.mult, ALU.subtract).then_inc(lo, 1)
                    split_lo(dve, U_FFN0)
                    derive(dve)
                    dve.wait_ge(row_here, 16)
                    for t in range(T):
                        dve.wait_ge(mixed, t + 1)
                        dve.tensor_tensor(xs[:, t, :], PS[:, 2 * t:2 * t + 2, :].rearrange("p a n -> p (a n)"),
                                          scale_row[:, :], ALU.mult).then_inc(weighed, 1)
                        dve.wait_ge(weighed, t + 1)
                        dve.tensor_tensor(X[:, t, :], X[:, t, :], xs[:, t, :], ALU.add).then_inc(added, 1)

        def square_sums(act, added, summed, junk, tiles):
            for n, t in enumerate(tiles):
                act.wait_ge(added, n + 1)
                if n >= 2:
                    act.wait_ge(summed, n - 1)
                act.activation(junk[:, n % 2, :], X[:, t, :], ACT.Square,
                               accum_out=rstd[:, t:t + 1]).then_inc(summed, 1)

        def project_pe(pe, u0, n, lhs_hi, lhs_lo, done, tiles=range(T), ready=None, first=None):
            for d in range(n):
                u = u0 + d
                pe.wait_ge(unit_lo, u + 1)
                if ready:
                    ready(d)
                for t in tiles:
                    if first and d == 0:
                        first(t)
                    for f in range(2):
                        for half in range(2):
                            w = slice(f * D + half * 512, f * D + half * 512 + 512)
                            j = 2 * d + f
                            mm = product(pe, PS[:, 2 * t + half, :], lhs_hi[:, j, t * P:(t + 1) * P],
                                         lhs_lo[:, j, t * P:(t + 1) * P], WH[:, u % SLOTS, w], WL[:, u % SLOTS, w],
                                         j == 0, j == 2 * n - 1)
                    if d == n - 1:
                        mm.then_inc(done, 1)
                if d < n - 1:
                    mm.then_inc(unit_used, 1)
            pe.wait_ge(done, T)
            pe.sem_inc(unit_used, 1)

        def project_add(dve, done, added, tiles=range(T)):
            for n, t in enumerate(tiles):
                dve.wait_ge(done, n + 1)
                dve.tensor_tensor(X[:, t, :], X[:, t, :], PS[:, 2 * t:2 * t + 2, :].rearrange("p a n -> p (a n)"),
                                  ALU.add).then_inc(added, 1)

        def swiglu(tag, u0, gain_name, split):
            n = FC // 2
            gate_made = sem(tag + "gate_made")
            up_made = sem(tag + "up_made")
            gate_free = sem(tag + "gate_free")
            up_free = sem(tag + "up_free")
            table_loaded = sem(tag + "table_loaded")
            h_hi = sem(tag + "h_hi")
            h_lo = sem(tag + "h_lo")
            down_made = sem(tag + "down_made")
            added = sem(tag + "added")
            with ExitStack() as tmp, nc.Block() as block:
                silu = sb(tag + "silu", [P, 2, S], F32, tmp)

                @block.scalar
                def _(act):
                    act.sem_inc(gate_free, 2)

                @block.vector
                def _(dve):
                    dve.sem_inc(up_free, 2)
                    dve.sem_inc(h_lo, 1)

                with ExitStack() as early:
                    xs = sb(tag + "xs", [P, T, D], where=early)
                    _, _, turned_lo = normalize(block, tag + "n", xs, gain_name, split)
                FH = sb(tag + "FH", [P, FC, S], F32R, tmp)
                FL = sb(tag + "FL", [P, FC, S], F32R, tmp)

                @block.sync
                def _(sp):
                    with nc.sync.Fori(0, n) as i:
                        for k in range(2):
                            load_unit(sp, u0 + 2 + k, i)
                    for u in range(u0 + 2 * n + 2, u0 + FFN_UNITS + 2):
                        load_unit(sp, u)

                @block.tensor
                def _(pe):
                    with nc.Fori(0, n, engines=(mybir.EngineType.PE,), hint_back_edge=True) as i:
                        for part, made, free in ((0, gate_made, gate_free), (1, up_made, up_free)):
                            slot = (u0 + part) % SLOTS
                            pe.wait_ge(unit_lo, u0 + part + 1 + 2 * i)
                            for k in range(2):
                                pe.wait_ge(free, 2 * i + k + 1)
                                for c in range(C):
                                    if part == 0 and k == 0:
                                        pe.wait_ge(turned_lo, c + 1)
                                    w = slice(c * 256 + k * P, c * 256 + k * P + P)
                                    mm = product(pe, PS[:, 2 * part + k, :], WH[:, slot, w], WL[:, slot, w],
                                                 AH[:, c, :], AL[:, c, :], c == 0, c == C - 1)
                                mm.then_inc(unit_used if k else made, 1)

                    def halves_ready(d):
                        pe.wait_ge(h_lo, 2 * d + 3)

                    def banks_free(t):
                        if t < 2:
                            pe.wait_ge((gate_free, up_free)[t], FC + 2)

                    project_pe(pe, u0 + 2 * n, n, FH, FL, down_made, (2, 3, 0, 1), halves_ready, banks_free)

                @block.scalar
                def _(act):
                    act.activation(silu[:, 0, 0:1], ident[:, 0:1], ACT.Silu).then_inc(table_loaded, 1)
                    act.wait_ge(table_loaded, 1)
                    with nc.scalar.Fori(0, n) as i:
                        for k in range(2):
                            if k:
                                act.wait_ge(unit_used, u0 + 1 + 2 * i)
                            else:
                                act.wait_ge(gate_made, i + 1)
                            act.wait_ge(h_lo, 2 * i + 1)
                            act.activation(silu[:, k, :], PS[:, k, :], ACT.Silu).then_inc(gate_free, 1)
                        split_hi(act, u0 + 2, i)
                        for k in range(2):
                            act.wait_ge(up_free, 2 * i + k + 3)
                            act.activation(FH[:, bass.ds(2 * i + k, 1), :].rearrange("p a s -> p (a s)"),
                                           silu[:, k, :], ACT.Copy).then_inc(h_hi, 1)
                        split_hi(act, u0 + 3, i)
                    for u in range(u0 + 2 * n + 2, u0 + FFN_UNITS):
                        split_hi(act, u)
                    act.activation(spare[:, 2:3], ident[:, 0:1], ACT.Sqrt).then_inc(table_loaded, 1)
                    square_sums(act, added, sem(tag + "next_summed"), AH[:, 0:4, :].rearrange("p (a b) s -> p a (b s)", a=2), (2, 3, 0, 1))

                @block.vector
                def _(dve):
                    with nc.vector.Fori(0, n) as i:
                        split_lo(dve, u0 + 2, i)
                        for k in range(2):
                            dve.wait_ge(gate_free, 2 * i + k + 3)
                            if k:
                                dve.wait_ge(unit_used, u0 + 2 + 2 * i)
                            else:
                                dve.wait_ge(up_made, i + 1)
                            dve.tensor_tensor(silu[:, k, :], silu[:, k, :], PS[:, 2 + k, :],
                                              ALU.mult).then_inc(up_free, 1)
                        for k in range(2):
                            dve.wait_ge(h_hi, 2 * i + k + 1)
                            j = bass.ds(2 * i + k, 1)
                            dve.tensor_tensor(FL[:, j, :].rearrange("p a s -> p (a s)"), silu[:, k, :],
                                              FH[:, j, :].rearrange("p a s -> p (a s)").bitcast(F32),
                                              ALU.subtract).then_inc(h_lo, 1)
                        split_lo(dve, u0 + 3, i)
                    for u in range(u0 + 2 * n + 2, u0 + FFN_UNITS):
                        split_lo(dve, u)
                    project_add(dve, down_made, added, (2, 3, 0, 1))


        def mla_down(CTH, CTL, KR, rot, xs):
            rope_in = sem("rope_in")
            angle = sem("angle")
            sines = sem("sines")
            main_made = sem("mla_main_made")
            rope_made = sem("mla_rope_made")
            squared = sem("mla_squared")
            meaned = sem("mla_meaned")
            rooted = sem("mla_rooted")
            inverted = sem("mla_inverted")
            scaled = sem("mla_scaled")
            kr_copied = sem("mla_kr_copied")
            rotated = sem("mla_kr_rotated")
            turned = sem("mla_turned")
            hi = sem("mla_ct_hi")
            lo = sem("mla_ct_lo")
            kr_out = sem("mla_kr_out")
            two_pi = 2.0 * np.pi
            c1 = 6.28125
            c2 = float(np.float32(int((two_pi - c1) * 2 ** 21) / 2 ** 21))
            c3 = float(two_pi - c1 - c2)
            magic = 1.5 * 2.0 ** 23
            edge = 3.1415925
            with ExitStack() as tmp, nc.Block() as block:
                dn = sb("mla_dn", [P, T, 512], where=tmp)
                krt = sb("mla_krt", [ROPE, S], where=tmp)
                kr = sb("mla_kr", [P, T, 2, 32], where=tmp)
                krot = sb("mla_krot", [P, T, 2, 2, 32], where=tmp)
                krm = sb("mla_krm", [P, 2, T, 2, 32], where=tmp)
                pos = sb("rope_pos", [P, T], I32, tmp)
                posf = sb("rope_posf", [P, T], where=tmp)
                ang = sb("rope_ang", [P, 2, T, 32], where=tmp)
                turns = sb("rope_turns", [P, 2, T, 32], where=tmp)
                sc = sb("mla_sc", [P, 16], where=tmp)
                _, _, turned_lo = normalize(block, "n2", xs, "mix1", (U_MLA, U_MLA + 1))

                @block.sync
                def _(sp):
                    sp.dma_start(pos[:, :], positions[:, :]).then_inc(rope_in, 16)
                    for u in range(U_MLA + 2, U_MLA + 5):
                        load_unit(sp, u)

                @block.tensor
                def _(pe):
                    for part in range(2):
                        u = U_MLA + part
                        pe.wait_ge(unit_lo, u + 1)
                        for t in range(T):
                            for k in range(4):
                                c = 4 * part + k
                                if t == 0:
                                    pe.wait_ge(turned_lo, c + 1)
                                w = slice(k * 512, (k + 1) * 512)
                                mm = product(pe, PS[:, t, :], AH[:, c, t * P:(t + 1) * P], AL[:, c, t * P:(t + 1) * P],
                                             WH[:, u % SLOTS, w], WL[:, u % SLOTS, w], c == 0, c == C - 1)
                            if part:
                                mm.then_inc(main_made, 1)
                        if part:
                            pe.wait_ge(main_made, T)
                            pe.sem_inc(unit_used, 1)
                        else:
                            mm.then_inc(unit_used, 1)
                    u = U_MLA + 2
                    pe.wait_ge(unit_lo, u + 1)
                    for c in range(C):
                        w = slice(c * ROPE, (c + 1) * ROPE)
                        mm = product(pe, PS[0:ROPE, 4, :], WH[:, u % SLOTS, w], WL[:, u % SLOTS, w], AH[:, c, :],
                                     AL[:, c, :], c == 0, c == C - 1)
                    mm.then_inc(unit_used, 1)
                    pe.wait_ge(rope_made, 1)
                    for t in range(T):
                        mm = pe.transpose(PS[:, 5, t * ROPE:(t + 1) * ROPE], krt[0:ROPE, t * P:(t + 1) * P],
                                          ident[0:ROPE, 0:ROPE])
                    mm.then_inc(rope_made, 1)
                    pe.wait_ge(kr_copied, 1)
                    for t in range(T):
                        pe.wait_ge(scaled, 2 * (t + 1))
                        for c in range(4):
                            mm = pe.transpose(PS[:, 4 + c, t * P:(t + 1) * P], dn[:, t, c * P:(c + 1) * P], ident)
                            if t == T - 1:
                                mm.then_inc(turned, 1)
                    pe.wait_ge(rotated, 1)
                    for t in range(T):
                        mm = pe.transpose(PS[:, 0, t * P:(t + 1) * P],
                                          krot[:, t, :, :, :].rearrange("p a b n -> p (a b n)"), ident)
                    mm.then_inc(turned, 1)

                @block.scalar
                def _(act):
                    split_hi(act, U_MLA + 2)
                    act.wait_ge(angle, 14)
                    act.activation(rot[:, :, :, :], ang[:, :, :, :], ACT.Sin).then_inc(sines, 1)
                    for t in range(T):
                        act.wait_ge(main_made, t + 1)
                        act.activation(dn[:, t, 0:Q_LORA], PS[:, t, 0:Q_LORA], ACT.Square,
                                       accum_out=sc[:, t:t + 1]).then_inc(squared, 1)
                        act.activation(dn[:, t, Q_LORA:512], PS[:, t, Q_LORA:512], ACT.Square,
                                       accum_out=sc[:, 4 + t:5 + t]).then_inc(squared, 1)
                    act.wait_ge(meaned, 2)
                    act.activation(sc[:, 8:16], sc[:, 0:8], ACT.Sqrt).then_inc(rooted, 1)
                    act.wait_ge(unit_used, U_MLA + 3)
                    act.activation(krt[0:ROPE, :], PS[0:ROPE, 4, :], ACT.Copy).then_inc(rope_made, 1)
                    act.wait_ge(rope_made, 2)
                    act.activation(kr[:, :, :, :].rearrange("p t a n -> p (t a n)"), PS[:, 5, 0:T * ROPE],
                                   ACT.Copy).then_inc(kr_copied, 1)
                    split_hi(act, U_MLA + 3)
                    for c in range(4):
                        act.wait_ge(turned, c + 1)
                        act.activation(CTH[:, c, :], PS[:, 4 + c, :], ACT.Copy,
                                       scale=gain_col("q_lora", c)).then_inc(hi, 1)
                    act.wait_ge(turned, 5)
                    act.activation(KR[:, :], PS[:, 0, :], ACT.Copy).then_inc(kr_out, 1)

                @block.vector
                def _(dve):
                    split_lo(dve, U_MLA + 2)
                    dve.wait_ge(rope_in, 16)
                    dve.tensor_copy(posf[:, :], pos[:, :]).then_inc(angle, 1)
                    dve.wait_ge(angle, 1)
                    for w in range(2):
                        for t in range(T):
                            ins = dve.tensor_scalar(ang[:, w, t, :], const("inv_freq"), posf[:, t:t + 1], None, ALU.mult)
                    ins.then_inc(angle, 1)
                    dve.wait_ge(angle, 2)
                    for w, quarter in ((0, 0.0), (1, 0.25)):
                        dve.tensor_scalar(turns[:, w, :, :], ang[:, w, :, :], 1.0 / two_pi, quarter, ALU.mult,
                                          ALU.add).then_inc(angle, 1)
                    dve.wait_ge(angle, 4)
                    dve.tensor_scalar(turns[:, :, :, :], turns[:, :, :, :], magic, None, ALU.add).then_inc(angle, 1)
                    dve.wait_ge(angle, 5)
                    dve.tensor_scalar(turns[:, :, :, :], turns[:, :, :, :], magic, None, ALU.subtract).then_inc(angle, 1)
                    dve.wait_ge(angle, 6)
                    flat = "p a t n -> p (a t n)"
                    for n, part in enumerate((c1, c2, c3)):
                        dve.scalar_tensor_tensor(ang[:, :, :, :].rearrange(flat), turns[:, :, :, :].rearrange(flat),
                                                 -part, ang[:, :, :, :].rearrange(flat), ALU.mult,
                                                 ALU.add).then_inc(angle, 1)
                        dve.wait_ge(angle, 7 + n)
                    dve.tensor_scalar(ang[:, 1, :, :], ang[:, 1, :, :], 0.5 * np.pi, None, ALU.add).then_inc(angle, 1)
                    dve.wait_ge(angle, 10)
                    dve.tensor_scalar(ang[:, :, :, :], ang[:, :, :, :], edge, None, ALU.min).then_inc(angle, 1)
                    dve.wait_ge(angle, 11)
                    dve.tensor_scalar(ang[:, :, :, :], ang[:, :, :, :], -edge, None, ALU.max).then_inc(angle, 3)
                    dve.wait_ge(squared, 2 * T)
                    dve.tensor_scalar(sc[:, 0:4], sc[:, 0:4], 1.0 / Q_LORA, EPS, ALU.mult, ALU.add).then_inc(meaned, 1)
                    dve.tensor_scalar(sc[:, 4:8], sc[:, 4:8], 1.0 / KV_LORA, EPS, ALU.mult, ALU.add).then_inc(meaned, 1)
                    dve.wait_ge(rooted, 1)
                    dve.reciprocal(sc[:, 0:8], sc[:, 8:16]).then_inc(inverted, 1)
                    dve.wait_ge(inverted, 1)
                    for t in range(T):
                        dve.tensor_scalar(dn[:, t, 0:Q_LORA], PS[:, t, 0:Q_LORA], sc[:, t:t + 1], None,
                                          ALU.mult).then_inc(scaled, 1)
                        dve.tensor_scalar(dn[:, t, Q_LORA:512], PS[:, t, Q_LORA:512], sc[:, 4 + t:5 + t], None,
                                          ALU.mult).then_inc(scaled, 1)
                    dve.wait_ge(kr_copied, 1)
                    dve.wait_ge(sines, 1)
                    for w in range(2):
                        for a in range(2):
                            ins = dve.tensor_tensor(krm[:, w, :, a, :], kr[:, :, a, :], rot[:, w, :, :], ALU.mult)
                    ins.then_inc(scaled, 1)
                    dve.wait_ge(scaled, 2 * T + 1)
                    for twice in range(2):
                        dve.tensor_tensor(krot[:, :, twice, 0, :], krm[:, 1, :, 0, :], krm[:, 0, :, 1, :], ALU.subtract)
                        ins = dve.tensor_tensor(krot[:, :, twice, 1, :], krm[:, 1, :, 1, :], krm[:, 0, :, 0, :], ALU.add)
                    ins.then_inc(rotated, 1)
                    split_lo(dve, U_MLA + 3)
                    for c in range(4):
                        dve.wait_ge(hi, c + 1)
                        dve.scalar_tensor_tensor(CTL[:, c, :], PS[:, 4 + c, :], gain_col("q_lora", c),
                                                 CTH[:, c, :].bitcast(F32), ALU.mult, ALU.subtract).then_inc(lo, 1)

        def mla_up(CTH, CTL, rot, QN, QR, KN, V):
            made = sem("mla_up_made")
            emptied = [sem("mla_up_emptied_act"), sem("mla_up_emptied_dve")]
            rotated = sem("mla_q_rotated")
            n_plain = 4 + 8 + 8 + 8
            with ExitStack() as tmp, nc.Block() as block:
                qr = sb("mla_qr", [P, T, 512], where=tmp)
                qrot = sb("mla_qrot", [P, T, H, 2, 32], where=tmp)
                qrm = sb("mla_qrm", [P, 2, 2, 512], where=tmp)

                def home(n):
                    if n < 4:
                        return qr[:, n, :], 1.0
                    if n < 12:
                        return QN[:, n - 4, :], MLA_SCALE
                    if n < 20:
                        return KN[:, n - 12, :], 1.0
                    if n < 28:
                        return V[:, (n - 20) // 2, (n % 2) * 512:(n % 2 + 1) * 512], 1.0
                    return QR[:, n - 28, :], MLA_SCALE

                @block.sync
                def _(sp):
                    for u in range(U_MLA + 5, U_MLA + 9):
                        load_unit(sp, u)

                @block.tensor
                def _(pe):
                    for n in range(n_plain + 4):
                        if n >= 8:
                            pe.wait_ge(emptied[n % 2], (n - 8) // 2 + 1)
                        acc = PS[:, n % 8, :]
                        u = U_MLA + (3 if n < 4 else 4 if n < 8 else 5 if n < 12 else 6)
                        if n in (0, 4, 8, 12):
                            pe.wait_ge(unit_lo, u + 1)
                        wh, wl = WH[:, u % SLOTS, :], WL[:, u % SLOTS, :]
                        if n < 4:
                            for c in range(3):
                                w = slice(c * 512, (c + 1) * 512)
                                mm = product(pe, acc, CTH[:, c, n * P:(n + 1) * P], CTL[:, c, n * P:(n + 1) * P],
                                             wh[:, w], wl[:, w], c == 0, c == 2)
                        elif n < 12:
                            for c in range(3):
                                w = slice(c * 512 + (n % 4) * P, c * 512 + (n % 4) * P + P)
                                mm = product(pe, acc, wh[:, w], wl[:, w], CTH[:, c, :], CTL[:, c, :], c == 0, c == 2)
                        elif n < 20:
                            w = slice((n - 12) * P, (n - 11) * P)
                            mm = product(pe, acc, wh[:, w], wl[:, w], CTH[:, 3, :], CTL[:, 3, :], True, True)
                        elif n < 28:
                            t = (n - 20) // 2
                            w = slice(D + (n % 2) * 512, D + (n % 2) * 512 + 512)
                            mm = product(pe, acc, CTH[:, 3, t * P:(t + 1) * P], CTL[:, 3, t * P:(t + 1) * P],
                                         wh[:, w], wl[:, w], True, True)
                        else:
                            for t in range(T):
                                pe.wait_ge(rotated, 4 * (t + 1))
                                src = qrot[:, t, 2 * (n - 28):2 * (n - 28) + 2, :, :]
                                mm = pe.transpose(PS[:, n % 8, t * P:(t + 1) * P],
                                                  src.rearrange("p h a n -> p (h a n)"), ident)
                        mm.then_inc(made, 1)
                        if n in (3, 7, 11, 27):
                            pe.wait_ge(made, n + 1)
                            pe.sem_inc(unit_used, 1)

                @block.scalar
                def _(act):
                    split_hi(act, U_MLA + 4)
                    for n in range(0, n_plain + 4, 2):
                        act.wait_ge(made, n + 1)
                        dst, scale = home(n)
                        act.activation(dst, PS[:, n % 8, :], ACT.Copy, scale=scale).then_inc(emptied[0], 1)
                        if n in (4, 8, 12):
                            split_hi(act, U_MLA + 5 + (n - 4) // 4)

                @block.vector
                def _(dve):
                    split_lo(dve, U_MLA + 4)
                    for n in range(1, n_plain + 4, 2):
                        dve.wait_ge(made, n + 1)
                        dst, scale = home(n)
                        dve.tensor_scalar(dst, PS[:, n % 8, :], scale, None, ALU.mult).then_inc(emptied[1], 1)
                        if n in (5, 9, 13):
                            split_lo(dve, U_MLA + 5 + (n - 5) // 4)
                        if n in (5, 7, 9, 11):
                            t = (n - 5) // 2
                            dve.wait_ge(emptied[0], t // 2 + 1)
                            dve.wait_ge(emptied[1], t // 2 + 1)
                            if t >= 2:
                                dve.wait_ge(rotated, 4 * (t - 1))
                            for w in range(2):
                                dve.tensor_tensor(qrm[:, t % 2, w, :].rearrange("p (a n) -> p a n", n=32),
                                                  qr[:, t, :].rearrange("p (a n) -> p a n", n=32),
                                                  rot[:, w, t:t + 1, :].broadcast_to([P, 2 * H, 32]),
                                                  ALU.mult).then_inc(rotated, 1)
                            dve.wait_ge(rotated, 4 * t + 2)
                            by_sin, by_cos = (qrm[:, t % 2, w, :].rearrange("p (h a n) -> p h a n", a=2, n=32)
                                              for w in range(2))
                            dve.tensor_tensor(qrot[:, t, :, 0, :], by_cos[:, :, 0, :], by_sin[:, :, 1, :],
                                              ALU.subtract).then_inc(rotated, 1)
                            dve.tensor_tensor(qrot[:, t, :, 1, :], by_cos[:, :, 1, :], by_sin[:, :, 0, :],
                                              ALU.add).then_inc(rotated, 1)

        def attend(tag, maps, scores, V, O, units, prepare=None, head_squares=None):
            scored = sem(tag + "scored")
            maxed = sem(tag + "maxed")
            exped = sem(tag + "exped")
            factored = sem(tag + "factored")
            combined = sem(tag + "combined")
            turned = sem(tag + "turned")
            copied = sem(tag + "copied")
            weighed = sem(tag + "weighed")
            emptied = sem(tag + "emptied")
            ready = sem(tag + "ready")
            squared = sem(tag + "squared")
            N = H * T
            ahead = 4 // maps
            with ExitStack() as tmp, nc.Block() as block:
                probs = sb(tag + "probs", [P, 2, maps, S], where=tmp)
                mixed = sb(tag + "mixed", [P, 2, S], where=tmp) if maps == 2 else None
                turned_probs = sb(tag + "turned_probs", [P, 2, S], where=tmp)
                neg_max = sb(tag + "neg_max", [P, N * maps], where=tmp)
                total = sb(tag + "total", [P, N * maps], where=tmp)
                factor = sb(tag + "factor", [P, N * maps], where=tmp)
                junk = sb(tag + "junk", [P, 4, P], where=tmp) if head_squares is not None else None
                neg_lambda, extra = prepare(tmp, block, ready) if prepare else (None, 0)

                @block.tensor
                def _(pe):
                    for i in range(N + 3):
                        if i < N:
                            h, q = divmod(i, T)
                            if i >= ahead:
                                pe.wait_ge(exped, maps * (i - ahead + 1))
                            if i == 0 and extra:
                                pe.wait_ge(ready, extra)
                            for m in range(maps):
                                scores(pe, h, q, m, PS[:, maps * (i % ahead) + m, 0:(q + 1) * P]).then_inc(scored, 1)
                        j = i - 2
                        if 0 <= j < N:
                            q = j % T
                            pe.wait_ge(combined if maps == 2 else exped, j + 1)
                            if j >= 2:
                                pe.wait_ge(copied, j - 1)
                            src = mixed[:, j % 2, :] if maps == 2 else probs[:, j % 2, 0, :]
                            for k in range(q + 1):
                                mm = pe.transpose(PS[:, 4 + j % 2, k * P:(k + 1) * P], src[:, k * P:(k + 1) * P], ident)
                            mm.then_inc(turned, 1)
                        j = i - 3
                        if 0 <= j < N:
                            h, q = divmod(j, T)
                            pe.wait_ge(copied, j + 1)
                            if j >= 2:
                                pe.wait_ge(emptied, j - 1)
                            for k in range(q + 1):
                                mm = pe.matmul(PS[:, 6 + j % 2, 0:P], turned_probs[:, j % 2, k * P:(k + 1) * P],
                                               V[:, k, h * P:(h + 1) * P], start=(k == 0), stop=(k == q))
                            mm.then_inc(weighed, 1)

                @block.scalar
                def _(act):
                    for i in range(N + 4):
                        if i < N:
                            w = (i % T + 1) * P
                            for m in range(maps):
                                n = maps * i + m
                                act.wait_ge(maxed, n + 1)
                                if i >= 2:
                                    act.wait_ge(combined if maps == 2 else turned, i - 1)
                                act.activation(probs[:, i % 2, m, 0:w], PS[:, maps * (i % ahead) + m, 0:w], ACT.Exp,
                                               bias=neg_max[:, n:n + 1],
                                               accum_out=total[:, n:n + 1]).then_inc(exped, 1)
                        j = i - 2
                        if 0 <= j < N:
                            w = (j % T + 1) * P
                            act.wait_ge(turned, j + 1)
                            if j >= 2:
                                act.wait_ge(weighed, j - 1)
                            act.activation(turned_probs[:, j % 2, 0:w], PS[:, 4 + j % 2, 0:w],
                                           ACT.Copy).then_inc(copied, 1)
                        j = i - 4
                        if 0 <= j < N and head_squares is not None:
                            h, q = divmod(j, T)
                            act.wait_ge(emptied, j + 1)
                            if j >= 4:
                                act.wait_ge(squared, j - 3)
                            act.activation(junk[:, j % 4, :], O[:, q, h * P:(h + 1) * P], ACT.Square,
                                           accum_out=head_squares[:, q, h:h + 1]).then_inc(squared, 1)
                        if i == 1:
                            for u in units:
                                split_hi(act, u)

                @block.vector
                def _(dve):
                    for i in range(N + 3):
                        if i < N:
                            w = (i % T + 1) * P
                            for m in range(maps):
                                n = maps * i + m
                                dve.wait_ge(scored, n + 1)
                                dve.tensor_reduce(neg_max[:, n:n + 1], PS[:, maps * (i % ahead) + m, 0:w], AX_X,
                                                  ALU.max, negate=True).then_inc(maxed, 1)
                        j = i - 1
                        if 0 <= j < N:
                            n = maps * j
                            w = (j % T + 1) * P
                            dve.wait_ge(exped, maps * (j + 1))
                            dve.reciprocal(factor[:, n:n + maps], total[:, n:n + maps]).then_inc(factored, 1)
                            if maps == 2:
                                dve.wait_ge(factored, 2 * j + 1)
                                dve.scalar_tensor_tensor(factor[:, n + 1:n + 2], total[:, n:n + 1], neg_lambda,
                                                         factor[:, n + 1:n + 2], ALU.mult,
                                                         ALU.mult).then_inc(factored, 1)
                                dve.wait_ge(factored, 2 * j + 2)
                                if j >= 2:
                                    dve.wait_ge(turned, j - 1)
                                dve.scalar_tensor_tensor(mixed[:, j % 2, 0:w], probs[:, j % 2, 1, 0:w],
                                                         factor[:, n + 1:n + 2], probs[:, j % 2, 0, 0:w], ALU.mult,
                                                         ALU.add).then_inc(combined, 1)
                        j = i - 3
                        if 0 <= j < N:
                            h, q = divmod(j, T)
                            n = maps * j
                            dve.wait_ge(weighed, j + 1)
                            dve.wait_ge(factored, maps * (j + 1))
                            dve.tensor_scalar(O[:, q, h * P:(h + 1) * P], PS[:, 6 + j % 2, 0:P], factor[:, n:n + 1],
                                              None, ALU.mult).then_inc(emptied, 1)
                        if i == 1:
                            for u in units:
                                split_lo(dve, u)

        def attention_out(tag, O, u0, column, last_load, stat=None):
            turned = sem(tag + "turned")
            hi = sem(tag + "hi")
            lo = sem(tag + "lo")
            made = sem(tag + "made")
            added = sem(tag + "added")
            meaned = sem(tag + "meaned")
            rooted = sem(tag + "rooted")
            normal = sem(tag + "normal")
            normed = stat is not None
            with nc.Block() as block:

                @block.sync
                def _(sp):
                    for u in range(u0 + 2, last_load):
                        load_unit(sp, u)

                @block.tensor
                def _(pe):
                    for t in range(T):
                        if normed:
                            pe.wait_ge(normal, t + 1)
                        for c in range(C):
                            mm = pe.transpose(PS[:, c, t * P:(t + 1) * P], O[:, t, c * P:(c + 1) * P], ident)
                            if t == T - 1:
                                mm.then_inc(turned, 1)

                    def halves_ready(d):
                        pe.wait_ge(lo, 2 * d + 2)

                    def banks_free(t):
                        pe.wait_ge(lo, 2 * t + 2)

                    project_pe(pe, u0, 4, AH, AL, made, range(T), halves_ready, banks_free)

                @block.scalar
                def _(act):
                    if normed:
                        act.wait_ge(meaned, 1)
                        act.activation(stat[:, :, H:2 * H], stat[:, :, 0:H], ACT.Sqrt).then_inc(rooted, 1)
                    for c in range(C):
                        act.wait_ge(turned, c + 1)
                        scale = column if column is not None else 1.0
                        act.activation(AH[:, c, :], PS[:, c, :], ACT.Copy, scale=scale).then_inc(hi, 1)
                    for u in range(u0 + 2, u0 + 4):
                        split_hi(act, u)
                    act.activation(spare[:, 3:4], ident[:, 0:1], ACT.Sqrt).then_inc(hi, 1)
                    square_sums(act, added, sem(tag + "next_summed"), O, range(T))

                @block.vector
                def _(dve):
                    if normed:
                        dve.tensor_scalar(stat[:, :, 0:H], stat[:, :, 0:H], 1.0 / P, EPS, ALU.mult,
                                          ALU.add).then_inc(meaned, 1)
                        dve.wait_ge(rooted, 1)
                        dve.reciprocal(stat[:, :, 0:H], stat[:, :, H:2 * H]).then_inc(rooted, 1)
                        dve.wait_ge(rooted, 2)
                        for t in range(T):
                            o = O[:, t, :].rearrange("p (h d) -> p h d", h=H)
                            dve.tensor_tensor(o, o, stat[:, t, 0:H].unsqueeze(2).broadcast_to([P, H, P]),
                                              ALU.mult).then_inc(normal, 1)
                    for c in range(C):
                        dve.wait_ge(hi, c + 1)
                        scale = column if column is not None else 1.0
                        dve.scalar_tensor_tensor(AL[:, c, :], PS[:, c, :], scale, AH[:, c, :].bitcast(F32),
                                                 ALU.mult, ALU.subtract).then_inc(lo, 1)
                    for u in range(u0 + 2, u0 + 4):
                        split_lo(dve, u)
                    project_add(dve, made, added)

        def final_norm(block):
            gained = sem("final_gained")

            invert_root(block, "nf", lambda act: None, lambda dve: None)

            @block.vector
            def _(dve):
                dve.wait_ge(final_row_here, 16)
                for t in range(T):
                    dve.scalar_tensor_tensor(X[:, t, :], X[:, t, :], rstd[:, t:t + 1], final_row[:, :], ALU.mult,
                                             ALU.mult).then_inc(gained, 1)
            return gained

        def da_in(QK, V):
            made = sem("da_made")
            squared = sem("da_squared")
            emptied = sem("da_emptied")
            summed = sem("da_summed")
            rooted = sem("da_rooted")
            normal = sem("da_normal")
            with ExitStack() as tmp, nc.Block() as block:
                square = sb("da_square", [P, 2, 512], where=tmp)
                stat = sb("da_stat", [P, T, 32], where=tmp)
                root = sb("da_root", [P, T, 32], where=tmp)
                gained = final_norm(block)
                _, _, turned_lo = normalize(block, "n4", QK[:, :, 0:D], "mix2", (U_DA, U_DA + 1), QK[:, 0:2, D:2 * D],
                                         lambda engine, t: engine.wait_ge(gained, t + 1), act_tiles=range(T))

                @block.sync
                def _(sp):
                    for u in range(U_DA + 2, U_DA_OUT + 2):
                        load_unit(sp, u)

                @block.tensor
                def _(pe):
                    for b in range(6):
                        for part in range(2):
                            u = U_DA + 2 * b + part
                            pe.wait_ge(unit_lo, u + 1)
                            for t in range(T):
                                bank = 4 * (b % 2) + t
                                if b >= 2 and part == 0:
                                    pe.wait_ge(emptied, 4 * (b - 2) + t + 1)
                                for k in range(4):
                                    c = 4 * part + k
                                    if b == 0 and t == 0:
                                        pe.wait_ge(turned_lo, c + 1)
                                    w = slice(k * 512, (k + 1) * 512)
                                    mm = product(pe, PS[:, bank, :], AH[:, c, t * P:(t + 1) * P],
                                                 AL[:, c, t * P:(t + 1) * P], WH[:, u % SLOTS, w], WL[:, u % SLOTS, w],
                                                 c == 0, c == C - 1)
                                if part and t < T - 1:
                                    mm.then_inc(made, 1)
                            mm.then_inc(unit_used, 1)

                @block.scalar
                def _(act):
                    for b in range(6):
                        if b < 5:
                            split_hi(act, U_DA + 2 * b + 2)
                        for t in range(T):
                            bank = 4 * (b % 2) + t
                            n = 4 * b + t
                            if t < T - 1:
                                act.wait_ge(made, 3 * b + t + 1)
                            else:
                                act.wait_ge(unit_used, U_DA + 2 * b + 2)
                            if b < 4:
                                if n >= 2:
                                    act.wait_ge(summed, n - 1)
                                act.activation(square[:, n % 2, :], PS[:, bank, :], ACT.Square).then_inc(squared, 1)
                                act.activation(QK[:, t, b * 512:(b + 1) * 512], PS[:, bank, :],
                                               ACT.Copy).then_inc(emptied, 1)
                            else:
                                act.activation(V[:, t, (b - 4) * 512:(b - 3) * 512], PS[:, bank, :],
                                               ACT.Copy).then_inc(emptied, 1)
                        if b < 5:
                            split_hi(act, U_DA + 2 * b + 3)
                        if b == 3:
                            act.wait_ge(summed, 17)
                            act.activation(root[:, :, :], stat[:, :, :], ACT.Sqrt).then_inc(rooted, 1)

                @block.vector
                def _(dve):
                    for b in range(6):
                        if b < 5:
                            split_lo(dve, U_DA + 2 * b + 2)
                        if b < 4:
                            for t in range(T):
                                n = 4 * b + t
                                dve.wait_ge(squared, n + 1)
                                dve.tensor_reduce(stat[:, t, 8 * b:8 * b + 8],
                                                  square[:, n % 2, :].rearrange("p (g d) -> p g d", d=64), AX_X,
                                                  ALU.add).then_inc(summed, 1)
                        if b == 3:
                            dve.wait_ge(summed, 16)
                            dve.tensor_scalar(stat[:, :, :], stat[:, :, :], 1.0 / 64, EPS, ALU.mult,
                                              ALU.add).then_inc(summed, 1)
                        if b < 5:
                            split_lo(dve, U_DA + 2 * b + 3)
                        if b == 3:
                            dve.wait_ge(rooted, 1)
                            dve.reciprocal(stat[:, :, :], root[:, :, :]).then_inc(rooted, 1)
                            dve.wait_ge(rooted, 2)
                            dve.wait_ge(emptied, 16)
                        if b >= 4:
                            for t in range(2 * (b - 4), 2 * (b - 4) + 2):
                                qk = QK[:, t, :].rearrange("p (g d) -> p g d", d=64)
                                dve.tensor_tensor(qk, qk, stat[:, t, :].unsqueeze(2).broadcast_to([P, 32, 64]),
                                                  ALU.mult).then_inc(normal, 1)

        def da_turn(QK, QT, KT):
            turned = sem("da_turned")
            emptied = [sem("da_emptied_act"), sem("da_emptied_dve")]
            with nc.Block() as block:
                def home(n):
                    return (QT[:, n, :], gain_col("da_q")) if n < 8 else (KT[:, n - 8, :], gain_col("da_k"))

                @block.tensor
                def _(pe):
                    for n in range(16):
                        if n >= 8:
                            pe.wait_ge(emptied[n % 2], (n - 8) // 2 + 1)
                        for t in range(T):
                            mm = pe.transpose(PS[:, n % 8, t * P:(t + 1) * P], QK[:, t, n * P:(n + 1) * P], ident)
                        mm.then_inc(turned, 1)

                @block.scalar
                def _(act):
                    for n in range(0, 16, 2):
                        act.wait_ge(turned, n + 1)
                        dst, scale = home(n)
                        act.activation(dst, PS[:, n % 8, :], ACT.Copy, scale=scale).then_inc(emptied[0], 1)

                @block.vector
                def _(dve):
                    for n in range(1, 16, 2):
                        dve.wait_ge(turned, n + 1)
                        dst, scale = home(n)
                        dve.tensor_scalar(dst, PS[:, n % 8, :], scale, None, ALU.mult).then_inc(emptied[1], 1)

        def route(block, tmp, early, turned_halves, place, weight, code, counts, prefetch):
            TH, TL = turned_halves
            here = sem("router_here")
            logits_made = sem("logits_made")
            step = sem("route_step")
            exped = sem("route_exped")
            selected = sem("route_selected")
            ranked = sem("route_ranked")
            gained = sem("moe_gained")
            hi = sem("moe_rows_hi")
            lo = sem("moe_rows_lo")
            wr = sb("wr", [P, C, 20], where=tmp)
            wr_hi = sb("wr_hi", [P, C, 20], F32R, tmp)
            wr_lo = sb("wr_lo", [P, C, 20], F32R, tmp)
            LT = sb("logits_turned", [20, S], where=tmp)
            earlier_r = sb("route_earlier", [P, T + 1, E], F32R, tmp)
            chosen_r = sb("route_chosen", [P, T, E], F32R, tmp)
            before_r = sb("route_before", [P, P], F32R, tmp)
            bias = sb("router_bias", [P, 20], where=tmp)
            row = sb("moe_gain_row", [P, D], where=tmp)
            ones = sb("ones", [P, P], where=tmp)
            ones_r = sb("ones_r", [P, P], F32R, tmp)
            L = sb("logits", [P, T, 20], where=tmp)
            small = sb("route_small", [P, 12, T, 1], where=tmp)
            four = sb("route_four", [P, 8, T, G], where=tmp)
            wide = sb("route_wide", [P, 6, T, G, G], where=tmp)
            rank = sb("route_rank", [P, T + 1, E], where=tmp)
            xs = sb("moe_xs", [P, T, D], where=early)
            gained_rows = sb("moe_gained_rows", [P, T, D], where=early)

            split = sem("router_split")
            counted = sem("route_counted")
            tables = sem("route_tables")

            def tables_act(act):
                act.wait_ge(here, 48)
                act.activation(wr_hi[:, :, :], wr[:, :, :], ACT.Copy).then_inc(split, 1)
                act.activation(before_r[:, :], const("before"), ACT.Copy).then_inc(tables, 1)
                act.wait_ge(tables, 2)
                act.activation(ones_r[:, :], ones[:, :], ACT.Copy).then_inc(tables, 1)

            def tables_dve(dve):
                dve.memset(ones[:, :], 1.0).then_inc(tables, 1)
                dve.wait_ge(split, 1)
                dve.tensor_tensor(wr_lo[:, :, :], wr[:, :, :], wr_hi[:, :, :].bitcast(F32),
                                  ALU.subtract).then_inc(split, 1)

            scaled, turned, turned_lo = normalize(block, "n5", xs, "moe", halves=turned_halves,
                                                  meanwhile=(tables_act, tables_dve))

            @block.sync
            def _(sp):
                sp.dma_start(wr[:, :, :].rearrange("p c n -> p (c n)"), router[0:P, :]).then_inc(here, 16)
                sp.dma_start(bias[:, :], router[P:P + 1, 0:20].broadcast_to([P, 20])).then_inc(here, 16)
                sp.dma_start(row[:, :], rows[2:3, :].broadcast_to([P, D])).then_inc(here, 16)
                prefetch(sp)

            @block.tensor
            def _(pe):
                pe.wait_ge(split, 2)
                for c in range(C):
                    pe.wait_ge(turned_lo, c + 1)
                    mm = product(pe, PS[0:20, 0, :], wr_hi[:, c, :], wr_lo[:, c, :], TH[:, c, :], TL[:, c, :],
                                 c == 0, c == C - 1)
                mm.then_inc(logits_made, 1)
                pe.wait_ge(logits_made, 2)
                for t in range(T):
                    mm = pe.transpose(PS[:, 1, t * 32:t * 32 + 20], LT[0:20, t * P:(t + 1) * P], ident[0:20, 0:20])
                mm.then_inc(logits_made, 1)
                pe.wait_ge(tables, 3)
                pe.wait_ge(selected, T + 2)
                pe.matmul(PS[:, 2, 0:(T + 1) * E], ones_r[:, :], earlier_r[:, :, :].rearrange("p t e -> p (t e)"),
                          start=True, stop=False)
                mm = pe.matmul(PS[:, 2, 0:T * E], before_r[:, :], chosen_r[:, :, :].rearrange("p t e -> p (t e)"),
                               start=False, stop=True)
                mm.then_inc(ranked, 1)

            @block.scalar
            def _(act):
                def rows_hi(t):
                    act.wait_ge(gained, t + 1)
                    act.activation(AH[:, 2 * t:2 * t + 2, :].rearrange("p a n -> p (a n)"), gained_rows[:, t, :],
                                   ACT.Copy).then_inc(hi, 1)

                act.activation(spare[:, 4:5], ident[:, 0:1], ACT.Exp).then_inc(tables, 1)
                for t in range(3):
                    rows_hi(t)
                act.wait_ge(step, 3)
                act.activation(four[:, 1, :, :], four[:, 0, :, :], ACT.Exp).then_inc(exped, 1)
                rows_hi(3)
                act.wait_ge(step, 12)
                act.activation(four[:, 4, :, :], four[:, 3, :, :], ACT.Exp).then_inc(exped, 1)

            @block.gpsimd
            def _(pool):
                pool.wait_ge(here, 48)
                for t in range(T):
                    pool.wait_ge(scaled, t + 1)
                    pool.tensor_tensor(gained_rows[:, t, :], xs[:, t, :], row[:, :], ALU.mult).then_inc(gained, 1)
                for t in range(T):
                    pool.wait_ge(hi, t + 1)
                    pool.tensor_tensor(AL[:, 2 * t:2 * t + 2, :].rearrange("p a n -> p (a n)"), gained_rows[:, t, :],
                                       AH[:, 2 * t:2 * t + 2, :].rearrange("p a n -> p (a n)").bitcast(F32),
                                       ALU.subtract).then_inc(lo, 1)

            @block.vector
            def _(dve):
                n = [0]

                def then(ins):
                    ins.then_inc(step, 1)
                    n[0] += 1
                    dve.wait_ge(step, n[0])

                def s(k):
                    return small[:, k, :, :]

                def s4(k):
                    return small[:, k, :, :].broadcast_to([P, T, G])

                def first_of_equal(out, values, most):
                    then(dve.tensor_tensor(out, values, most, ALU.is_equal))
                    then(dve.tensor_tensor(out, out, const("priority").unsqueeze(1).broadcast_to([P, T, G]),
                                           ALU.mult))
                    then(dve.tensor_reduce(s(11), out, AX_X, ALU.max))
                    then(dve.tensor_tensor(out, out, s4(11), ALU.is_equal))

                dve.wait_ge(logits_made, 1)
                dve.tensor_copy(LT[:, :], PS[0:20, 0, :]).then_inc(logits_made, 1)
                dve.wait_ge(logits_made, 3)
                then(dve.tensor_tensor(L[:, :, :], PS[:, 1, 0:T * 32].rearrange("p (t n) -> p t n", n=32)[:, :, 0:20],
                                       bias[:, :].unsqueeze(1).broadcast_to([P, T, 20]), ALU.add))
                then(dve.tensor_reduce(s(0), L[:, :, 0:G], AX_X, ALU.max))
                then(dve.tensor_tensor(four[:, 0, :, :], L[:, :, 0:G], s4(0), ALU.subtract))
                first_of_equal(four[:, 2, :, :], L[:, :, 0:G], s4(0))
                for t in range(T):
                    ins = dve.tensor_tensor(wide[:, 0, t, :, :], L[:, t, G:G + E].rearrange("p (g e) -> p g e", e=G),
                                            four[:, 2, t, :].unsqueeze(2).broadcast_to([P, G, G]), ALU.mult)
                then(ins)
                for t in range(T):
                    ins = dve.tensor_reduce(four[:, 3, t, :], wide[:, 0, t, :, :].rearrange("p g e -> p e g"),
                                            AX_X, ALU.add)
                then(ins)
                then(dve.tensor_reduce(s(1), four[:, 3, :, :], AX_X, ALU.max))
                then(dve.tensor_tensor(four[:, 3, :, :], four[:, 3, :, :], s4(1), ALU.subtract))
                dve.wait_ge(exped, 1)
                then(dve.tensor_reduce(s(2), four[:, 1, :, :], AX_X, ALU.add))
                assert n[0] == 12
                then(dve.reciprocal(s(3), s(2)))
                dve.wait_ge(exped, 2)
                then(dve.tensor_reduce(s(4), four[:, 4, :, :], AX_X, ALU.add))
                then(dve.reciprocal(s(5), s(4)))
                then(dve.tensor_tensor(four[:, 4, :, :], four[:, 4, :, :], s4(5), ALU.mult))
                then(dve.tensor_reduce(s(6), four[:, 4, :, :], AX_X, ALU.max))
                first_of_equal(four[:, 5, :, :], four[:, 4, :, :], s4(6))
                then(dve.tensor_scalar(four[:, 6, :, :], four[:, 5, :, :], -2.0, None, ALU.mult))
                then(dve.tensor_tensor(four[:, 4, :, :], four[:, 4, :, :], four[:, 6, :, :], ALU.add))
                then(dve.tensor_reduce(s(7), four[:, 4, :, :], AX_X, ALU.max))
                first_of_equal(four[:, 6, :, :], four[:, 4, :, :], s4(7))
                for k in range(2):
                    for t in range(T):
                        ins = dve.tensor_tensor(wide[:, 2 + k, t, :, :],
                                                four[:, 2, t, :].unsqueeze(2).broadcast_to([P, G, G]),
                                                four[:, 5 + k, t, :].unsqueeze(1).broadcast_to([P, G, G]), ALU.mult)
                then(ins)
                for both in (wide[:, 4, :, :, :].rearrange("p t g e -> p (t g e)"),
                             chosen_r[:, :, :].rearrange("p t e -> p (t e)")):
                    ins = dve.tensor_tensor(both, wide[:, 2, :, :, :].rearrange("p t g e -> p (t g e)"),
                                            wide[:, 3, :, :, :].rearrange("p t g e -> p (t g e)"), ALU.add)
                    ins.then_inc(selected, 1)
                dve.wait_ge(selected, 1)
                both = [wide[:, 4, t, :, :].rearrange("p g e -> p (g e)") for t in range(T)]
                dve.tensor_scalar(earlier_r[:, 0, :], both[0], 0.0, None, ALU.mult)
                dve.tensor_scalar(earlier_r[:, 1, :], both[0], 1.0, None, ALU.mult).then_inc(selected, 1)
                for t in range(1, T):
                    dve.wait_ge(selected, t + 2)
                    dve.tensor_tensor(earlier_r[:, t + 1, :], earlier_r[:, t, :].bitcast(F32), both[t],
                                      ALU.add).then_inc(selected, 1)
                then(dve.tensor_tensor(s(8), s(6), s(7), ALU.add))
                then(dve.reciprocal(s(9), s(8)))
                then(dve.tensor_tensor(s(9), s(9), s(3), ALU.mult))
                dve.tensor_tensor(weight[:, 0, :], small[:, 6, :, 0], small[:, 9, :, 0], ALU.mult)
                then(dve.tensor_tensor(weight[:, 1, :], small[:, 7, :, 0], small[:, 9, :, 0], ALU.mult))
                dve.wait_ge(ranked, 1)
                then(dve.tensor_copy(rank[:, :, :], PS[:, 2, 0:(T + 1) * E].rearrange("p (t e) -> p t e", e=E)))
                dve.wait_ge(selected, 2)
                chosen = wide[:, 4, :, :, :].rearrange("p t g e -> p t (g e)")
                for r in range(ROUNDS):
                    ins = dve.scalar_tensor_tensor(place[:, :, r * E:(r + 1) * E], rank[:, 0:T, :], 1.0 - P * r,
                                                   chosen, ALU.add, ALU.mult)
                then(ins)
                then(dve.tensor_scalar(place[:, :, :], place[:, :, :], -1.0, None, ALU.add))
                acc = wide[:, 0, :, :, :].rearrange("p t g e -> p t (g e)")
                then(dve.tensor_tensor(acc, chosen, const("token1").unsqueeze(2).broadcast_to([P, T, E]), ALU.mult))
                second = wide[:, 3, :, :, :].rearrange("p t g e -> p t (g e)")
                for r in range(ROUNDS):
                    ins = dve.scalar_tensor_tensor(code[:, :, r * E:(r + 1) * E, :],
                                                   second.unsqueeze(3).broadcast_to([P, T, E, 2]), float(S),
                                                   acc.unsqueeze(3).broadcast_to([P, T, E, 2]), ALU.mult, ALU.add)
                then(ins)
                then(dve.tensor_reduce(small[:, 0, 0, :], rank[:, T, :], AX_X, ALU.max))
                for r in range(1, ROUNDS):
                    ins = dve.tensor_scalar(small[:, r, 0, :], small[:, 0, 0, :], float(P * r), None, ALU.is_gt)
                then(ins)
                then(dve.tensor_tensor(small[:, 1, 0, :], small[:, 1, 0, :], small[:, 2, 0, :], ALU.add))
                then(dve.tensor_tensor(small[:, 1, 0, :], small[:, 1, 0, :], small[:, 3, 0, :], ALU.add))
                then(dve.tensor_scalar(small[:, 2, 0, :], small[:, 1, 0, :], float(E), float(E - 1), ALU.mult,
                                       ALU.add))
                dve.tensor_copy(counts[:, 0:1], small[:, 2, 0, :]).then_inc(counted, 1)

            return counted, logits_made, lo

        def moe_prefetch(eraw, landed):
            def issue(sp):
                for j in range(EU):
                    sp.dma_start(eraw[:, j, :], experts[0, j, :, :]).then_inc(landed[j], 16)
            return issue

        def run_experts(eraw, landed, place, weight, code, counts):
            unit_hi = sem("expert_unit_hi")
            unit_lo = sem("expert_unit_lo")
            unit_used = sem("expert_unit_used")
            dispatch_made = sem("dispatch_made")
            gathered = sem("gathered")
            gathered_copied = sem("gathered_copied")
            gathered_turned = sem("gathered_turned")
            gathered_hi = sem("gathered_hi")
            gathered_lo = sem("gathered_lo")
            silued = sem("expert_silued")
            h_made = sem("expert_h_made")
            h_turned = sem("expert_h_turned")
            h_hi = sem("expert_h_hi")
            h_lo = sem("expert_h_lo")
            y_act = sem("expert_y_act")
            y_dve = sem("expert_y_dve")
            stored = sem("expert_stored")
            index_found = sem("index_found")
            index_step = sem("index_step")
            index_ready = sem("index_ready")
            store_allowed = sem("store_allowed")
            y_free = sem("expert_y_free")
            table_loaded = sem("expert_table_loaded")
            with ExitStack() as tmp, nc.Block() as block:
                WEH = sb("WEH", [P, ESLOTS, UNIT], F32R, tmp)
                WEL = sb("WEL", [P, ESLOTS, UNIT], F32R, tmp)
                with ExitStack() as early:
                    counted, logits_made, rows_lo_made = route(
                        block, tmp, early, [w[:, 0:2, :].rearrange("p a (b s) -> p (a b) s", s=S) for w in (WEH, WEL)],
                        place, weight, code, counts, moe_prefetch(eraw, landed))
                dispatch = sb("dispatch", [P, T, P], F32R, tmp)
                chosen_rows = sb("chosen_rows", [P, D], where=tmp)
                GH = sb("GH", [P, C, P], F32R, tmp)
                GL = sb("GL", [P, C, P], F32R, tmp)
                h = sb("expert_h", [P, DE], where=tmp)
                HH = sb("HH", [P, DE // P, P], F32R, tmp)
                HL = sb("HL", [P, DE // P, P], F32R, tmp)
                y = sb("expert_y", [P, D], where=tmp)
                absent = sb("absent", [P, 1], where=tmp)
                index_next = sb("index_next", [P, 1], U32, tmp)
                index = sb("index", [P, 1], U32, tmp)
                rows_hi = AH[:, :, :].rearrange("p (t a) n -> p t (a n)", t=T)
                rows_lo = AL[:, :, :].rearrange("p (t a) n -> p t (a n)", t=T)

                @block.sync
                def _(sp):
                    sp.wait_ge(counted, 1)
                    final = sp.value_load(counts[0:1, 0:1], min_val=E - 1, max_val=E * ROUNDS - 1)
                    with nc.sync.Fori(0, final) as n:
                        following = (n + 1) % E
                        for j in range(EU):
                            sp.wait_ge(unit_lo, EU * n + j + 7)
                            sp.dma_start(eraw[:, j, :],
                                         experts[bass.ds(following, 1), j, :, :].rearrange("a p n -> p (a n)")
                                         ).then_inc(landed[j], 16)

                def gather(pe, n, a):
                    if a == 0:
                        pe.wait_ge(dispatch_made, n + 1)
                        pe.wait_ge(index_step, 2 * n + 1)
                        for t in range(T):
                            col = code[:, t, n, :] if isinstance(n, int) else \
                                code[:, t, bass.ds(n, 1), :].rearrange("p a b -> p (a b)")
                            mm = pe.matmul(PS[:, 7, 0:2], dispatch[:, t, :], col, start=(t == 0), stop=(t == T - 1))
                        mm.then_inc(index_found, 1)
                    for t in range(T):
                        for half in (rows_lo, rows_hi):
                            mm = pe.matmul(PS[:, 2 + a, :], dispatch[:, t, :], half[:, t, a * 512:(a + 1) * 512],
                                           start=(t == 0 and half is rows_lo), stop=(t == T - 1 and half is rows_hi))
                    mm.then_inc(gathered, 1)

                def turn_gathered(pe, n, a):
                    pe.wait_ge(gathered_copied, 2 * n + a + 1)
                    for c in range(4):
                        mm = pe.transpose(PS[:, 2 + a, c * P:(c + 1) * P],
                                          chosen_rows[:, (4 * a + c) * P:(4 * a + c + 1) * P], ident)
                    mm.then_inc(gathered_turned, 1)

                @block.tensor
                def _(pe):
                    pe.wait_ge(counted, 1)
                    final = pe.value_load(counts[0:1, 0:1], min_val=E - 1, max_val=E * ROUNDS - 1)

                    def turn(n, last):
                        pe.wait_ge(gathered_lo, 2 * n + 2)
                        for part, acc in ((0, PS[:, 0, :]), (1, PS[:, 1, :])):
                            pe.wait_ge(silued if part == 0 else h_made, n + 1)
                            for c in range(C):
                                j = 2 * part + c // 4
                                w = slice((c % 4) * DE, (c % 4 + 1) * DE)
                                if c % 4 == 0:
                                    pe.wait_ge(unit_lo, EU * n + j + 7)
                                mm = product(pe, acc, GH[:, c, :], GL[:, c, :], WEH[:, j % ESLOTS, w],
                                             WEL[:, j % ESLOTS, w], c == 0, c == C - 1)
                                if c % 4 == 3:
                                    mm.then_inc(unit_used, 1)
                        if not last:
                            gather(pe, n + 1, 0)
                        pe.wait_ge(h_made, n + 2)
                        for k in range(DE // P):
                            mm = pe.transpose(PS[:, 4, k * P:(k + 1) * P], h[:, k * P:(k + 1) * P], ident)
                        mm.then_inc(h_turned, 1)
                        if not last:
                            gather(pe, n + 1, 1)
                            turn_gathered(pe, n + 1, 0)
                        pe.wait_ge(h_lo, n + 1)
                        pe.wait_ge(y_act, n + 1)
                        pe.wait_ge(y_dve, n + 1)
                        for k in range(DE // P):
                            j = 4 + k // 2
                            if k % 2 == 0:
                                pe.wait_ge(unit_lo, EU * n + j + 7)
                            for half in range(2):
                                w = slice((k % 2) * D + half * 512, (k % 2) * D + half * 512 + 512)
                                mm = product(pe, PS[:, 5 + half, :], HH[:, k, :], HL[:, k, :], WEH[:, j % ESLOTS, w],
                                             WEL[:, j % ESLOTS, w], k == 0, k == DE // P - 1)
                            if k % 2:
                                mm.then_inc(unit_used, 1)
                            if k == 1 and not last:
                                turn_gathered(pe, n + 1, 1)

                    pe.wait_ge(rows_lo_made, T)
                    for a in range(2):
                        gather(pe, 0, a)
                    for a in range(2):
                        turn_gathered(pe, 0, a)
                    with nc.Fori(0, final, engines=(mybir.EngineType.PE,), hint_back_edge=True) as n:
                        turn(n, False)
                    turn(final, True)

                @block.scalar
                def _(act):
                    act.wait_ge(logits_made, 1)
                    for j in range(3):
                        act.wait_ge(landed[j], 16)
                        act.activation(WEH[:, j, :], eraw[:, j, :], ACT.Copy).then_inc(unit_hi, 1)
                    act.wait_ge(counted, 1)
                    final = act.value_load(counts[0:1, 0:1], min_val=E - 1, max_val=E * ROUNDS - 1)

                    def hi(n, j):
                        act.wait_ge(landed[j], 16 * n + 16)
                        act.wait_ge(unit_used, EU * n + j + 1)
                        act.activation(WEH[:, j % ESLOTS, :], eraw[:, j, :], ACT.Copy).then_inc(unit_hi, 1)

                    def copy_gathered(n, a):
                        act.wait_ge(gathered, 2 * n + a + 1)
                        act.activation(chosen_rows[:, a * 512:(a + 1) * 512], PS[:, 2 + a, :],
                                       ACT.Copy).then_inc(gathered_copied, 1)

                    def gathered_out(n, a):
                        act.wait_ge(gathered_turned, 2 * n + a + 1)
                        act.activation(GH[:, 4 * a:4 * a + 4, :], PS[:, 2 + a, :].rearrange("p (c s) -> p c s", s=P),
                                       ACT.Copy).then_inc(gathered_hi, 1)

                    def turn(n, last):
                        hi(n, 3)
                        act.wait_ge(unit_used, EU * n + 5)
                        act.wait_ge(h_turned, n + 1)
                        act.activation(h[:, :], PS[:, 0, :], ACT.Silu).then_inc(silued, 1)
                        hi(n, 4)
                        hi(n, 5)
                        if not last:
                            hi(n + 1, 0)
                            copy_gathered(n + 1, 0)
                        act.wait_ge(h_turned, n + 2)
                        act.wait_ge(unit_used, EU * n + 3)
                        act.activation(HH[:, :, :], PS[:, 4, :].rearrange("p (k s) -> p k s", s=P),
                                       ACT.Copy).then_inc(h_hi, 1)
                        if not last:
                            copy_gathered(n + 1, 1)
                            gathered_out(n + 1, 0)
                            gathered_out(n + 1, 1)
                            hi(n + 1, 1)
                            hi(n + 1, 2)
                        act.wait_ge(unit_used, EU * n + 9)
                        act.wait_ge(y_free, n + 1)
                        act.activation(y[:, 0:512], PS[:, 5, :], ACT.Copy).then_inc(y_act, 1)

                    act.wait_ge(rows_lo_made, T)
                    act.activation(h[:, 0:1], ident[:, 0:1], ACT.Silu).then_inc(table_loaded, 1)
                    act.wait_ge(table_loaded, 1)
                    for a in range(2):
                        copy_gathered(0, a)
                    for a in range(2):
                        gathered_out(0, a)
                    with nc.scalar.Fori(0, final) as n:
                        turn(n, False)
                    turn(final, True)

                @block.vector
                def _(dve):
                    dve.wait_ge(counted, 1)
                    final = dve.value_load(counts[0:1, 0:1], min_val=E - 1, max_val=E * ROUNDS - 1)

                    def lo(n, j):
                        dve.wait_ge(unit_hi, EU * n + j + 1)
                        dve.tensor_tensor(WEL[:, j % ESLOTS, :], eraw[:, j, :], WEH[:, j % ESLOTS, :].bitcast(F32),
                                          ALU.subtract).then_inc(unit_lo, 1)

                    def build_dispatch(n):
                        for t in range(T):
                            col = place[:, t, n:n + 1] if isinstance(n, int) else place[:, t, bass.ds(n, 1)]
                            ins = dve.tensor_scalar(dispatch[:, t, :], const("iota"), col, None, ALU.is_equal)
                        ins.then_inc(dispatch_made, 1)

                    def gathered_out(n, a):
                        dve.wait_ge(gathered_hi, 2 * n + a + 1)
                        dve.tensor_tensor(GL[:, 4 * a:4 * a + 4, :], PS[:, 2 + a, :].rearrange("p (c s) -> p c s", s=P),
                                          GH[:, 4 * a:4 * a + 4, :].bitcast(F32), ALU.subtract).then_inc(gathered_lo, 1)

                    def find_index(n):
                        dve.wait_ge(index_found, n + 1)
                        dve.tensor_scalar(absent[:, :], PS[:, 7, 0:1], 0.0, 2.0 * S + 1.0, ALU.is_equal,
                                          ALU.mult).then_inc(index_step, 1)
                        dve.wait_ge(index_step, 2 * n + 2)
                        dve.wait_ge(index_ready, n + 1)
                        dve.scalar_tensor_tensor(index_next[:, :], PS[:, 7, 0:1], -1.0, absent[:, :], ALU.add,
                                                 ALU.add).then_inc(index_step, 1)

                    def turn(n, last):
                        if not last:
                            dve.wait_ge(gathered, 2 * n + 2)
                            build_dispatch(n + 1)
                        lo(n, 3)
                        lo(n, 4)
                        dve.wait_ge(index_step, 2 * n + 3)
                        dve.wait_ge(y_free, n + 1)
                        dve.tensor_copy(index[:, :], index_next[:, :]).then_inc(index_ready, 1)
                        dve.wait_ge(silued, n + 2)
                        dve.wait_ge(unit_used, EU * n + 7)
                        dve.tensor_tensor(h[:, :], h[:, :], PS[:, 1, :], ALU.mult).then_inc(h_made, 1)
                        lo(n, 5)
                        dve.wait_ge(h_hi, n + 1)
                        dve.tensor_tensor(HL[:, :, :], PS[:, 4, :].rearrange("p (k s) -> p k s", s=P),
                                          HH[:, :, :].bitcast(F32), ALU.subtract).then_inc(h_lo, 1)
                        if not last:
                            lo(n + 1, 0)
                            find_index(n + 1)
                            gathered_out(n + 1, 0)
                            gathered_out(n + 1, 1)
                            lo(n + 1, 1)
                            lo(n + 1, 2)
                        dve.wait_ge(unit_used, EU * n + 9)
                        dve.wait_ge(y_free, n + 1)
                        dve.tensor_copy(y[:, 512:1024], PS[:, 6, :]).then_inc(y_dve, 1)

                    dve.wait_ge(rows_lo_made, T)
                    build_dispatch(0)
                    find_index(0)
                    dve.wait_ge(unit_lo, 7)
                    lo(0, 1)
                    gathered_out(0, 0)
                    gathered_out(0, 1)
                    lo(0, 2)
                    with nc.vector.Fori(0, final) as n:
                        turn(n, False)
                    turn(final, True)

                @block.gpsimd
                def _(pool):
                    pool.sem_inc(unit_used, 3)
                    pool.sem_inc(unit_lo, 6)
                    for one_turn_back in (y_free, silued, h_made, h_turned, y_act, y_dve, index_step, index_ready):
                        pool.sem_inc(one_turn_back, 1)
                    pool.wait_ge(unit_hi, 1)
                    pool.tensor_tensor(WEL[:, 0, :], eraw[:, 0, :], WEH[:, 0, :].bitcast(F32),
                                       ALU.subtract).then_inc(unit_lo, 1)
                    pool.wait_ge(counted, 1)
                    final = pool.value_load(counts[0:1, 0:1], min_val=E - 1, max_val=E * ROUNDS - 1)
                    bound = pool.to_reg(2 * S - 1)
                    with nc.gpsimd.Fori(0, final + 1) as n:
                        pool.wait_ge(index_ready, n + 2)
                        pool.wait_ge(y_act, n + 2)
                        pool.wait_ge(y_dve, n + 2)
                        pool.sem_inc(store_allowed, 1)
                        pool.indirect_dma_start(scratch[:, :], bass.IndirectOffsetOnAxis(index[:, 0:1], 0), y[:, :],
                                                None, bounds_check=bound, oob_is_err=False).then_inc(stored, 16)
                        pool.wait_ge(stored, 16 * n + 16)
                        pool.sem_inc(y_free, 1)

        def combine(weight):
            fetched = [sem(f"fetched{n}") for n in range(2 * T)]
            summed = sem("summed")
            out_stored = sem("out_stored")
            with ExitStack() as tmp, nc.Block() as block:
                got = sb("got", [P, T, 2, D], where=tmp)

                @block.vector
                def _(dve):
                    for t in range(T):
                        for k in range(2):
                            dve.wait_ge(fetched[2 * t + k], 16)
                            if k:
                                dve.wait_ge(summed, 2 * t + 1)
                            dve.scalar_tensor_tensor(X[:, t, :], got[:, t, k, :], weight[:, k, t:t + 1], X[:, t, :],
                                                     ALU.mult, ALU.add).then_inc(summed, 1)

                @block.sync
                def _(sp):
                    for t in range(T):
                        for k in range(2):
                            sp.dma_start(got[:, t, k, :], scratch[k * S + t * P:k * S + (t + 1) * P, :]
                                         ).then_inc(fetched[2 * t + k], 16)
                    for t in range(T):
                        sp.wait_ge(summed, 2 * t + 2)
                        sp.dma_start(out[t * P:(t + 1) * P, :], X[:, t, :]).then_inc(out_stored, 16)
                    sp.wait_ge(out_stored, 16 * T)

        pool_stage()

        swiglu("f0", U_FFN0, "ffn0", (U_FFN0 + 1,))

        with ExitStack() as held:
            QN = sb("QN", [P, H, S], where=held)
            KN = sb("KN", [P, H, S], where=held)
            QR = sb("QR", [P, H // 2, S], where=held)
            KR = sb("KR", [P, S], where=held)
            V = sb("V", [P, T, D], where=held)
            with ExitStack() as tmp:
                CTH = sb("CTH", [P, 4, S], F32R, tmp)
                CTL = sb("CTL", [P, 4, S], F32R, tmp)
                rot = sb("rot", [P, 2, T, 32], where=tmp)
                mla_down(CTH, CTL, KR, rot, QN[:, :, :].rearrange("p (t a) s -> p t (a s)", t=T))
                mla_up(CTH, CTL, rot, QN, QR, KN, V)
            O = sb("mla_O", [P, T, D], where=held)

            def mla_scores(pe, h, q, m, acc):
                keys = slice(0, (q + 1) * P)
                mine = slice(q * P, (q + 1) * P)
                half = slice((h % 2) * 64, (h % 2) * 64 + 64)
                pe.matmul(acc, QN[:, h, mine], KN[:, h, keys], start=True, stop=False)
                pe.matmul(acc, QR[half, h // 2, mine], KR[half, keys], start=False, stop=False)
                return pe.matmul(acc[:, q * P:(q + 1) * P], identr[:, :], causalr[:, :], start=False, stop=True)

            attend("m", 1, mla_scores, V, O, (U_MLA + 8,))
            attention_out("mo", O, U_MLA_OUT, None, U_FFN1 + 2)
        recycle()
        swiglu("f1", U_FFN1, "ffn1", (U_FFN1, U_FFN1 + 1))
        with ExitStack() as held:
            V = sb("da_V", [P, T, D], where=held)
            with ExitStack() as tmp:
                QT = sb("QT", [P, H, S], where=held)
                KT = sb("KT", [P, H, S], where=held)
                QK = sb("QK", [P, T, 2 * D], where=tmp)
                da_in(QK, V)
                da_turn(QK, QT, KT)
            O = sb("da_O", [P, T, D], where=held)
            stat = sb("da_head_stat", [P, T, 2 * H], where=held)
            slopes = sb("slopes", [P, H, P], F32R, held)
            alibir = sb("alibir", [P, S], F32R, held)

            def prepare(tmp, block, ready):
                lam_here = sem("lam_here")
                lam_step = sem("lam_step")
                lam_exp = sem("lam_exp")
                lam = sb("lam", [P, 4, 64], where=tmp)
                ls = sb("lam_s", [P, 8], where=tmp)

                @block.sync
                def _(sp):
                    sp.dma_start(lam[:, :, :].rearrange("p a n -> p (a n)"),
                                 lams.broadcast_to([P, 256])).then_inc(lam_here, 16)

                @block.scalar
                def _(act):
                    act.wait_ge(lam_step, 2)
                    act.activation(ls[:, 2:4], ls[:, 0:2], ACT.Exp).then_inc(lam_exp, 1)

                @block.vector
                def _(dve):
                    for h in range(H):
                        dve.tensor_scalar(slopes[:, h, :], ident, 2.0 ** (-8.0 * (h + 1) / H), None,
                                          ALU.mult).then_inc(ready, 1)
                    dve.tensor_copy(alibir[:, :], const("alibi")).then_inc(ready, 1)
                    dve.wait_ge(lam_here, 16)
                    for k in range(2):
                        dve.tensor_tensor_reduce(lam[:, 2 * k, :], lam[:, 2 * k, :], lam[:, 2 * k + 1, :], 1.0, 0.0,
                                                 ALU.mult, ALU.add, ls[:, k:k + 1]).then_inc(lam_step, 1)
                    dve.wait_ge(lam_exp, 1)
                    dve.tensor_tensor(ls[:, 4:5], ls[:, 3:4], ls[:, 2:3], ALU.subtract).then_inc(lam_step, 1)
                    dve.wait_ge(lam_step, 3)
                    dve.tensor_scalar(ls[:, 5:6], ls[:, 4:5], -LAMBDA_INIT, None, ALU.add).then_inc(lam_step, 1)
                    dve.wait_ge(lam_step, 4)

                return ls[:, 5:6], H + 1

            def da_scores(pe, h, q, m, acc):
                half = slice(m * 64, m * 64 + 64)
                pe.matmul(acc, QT[half, h, q * P:(q + 1) * P], KT[half, h, 0:(q + 1) * P], start=True, stop=False)
                return pe.matmul(acc, slopes[:, h, :], alibir[:, S - (q + 1) * P:S], start=False, stop=True)

            attend("d", 2, da_scores, V, O, (U_DA_OUT, U_DA_OUT + 1), prepare, stat)
            attention_out("do", O, U_DA_OUT, gain_col("da_sub"), U_END, stat)
        recycle()
        wctx.close()
        place = sb("place", [P, T, ROUNDS * E])
        weight = sb("weight", [P, 2, T])
        code = sb("code", [P, T, ROUNDS * E, 2], F32R)
        counts = sb("counts", [P, 1], I32)
        landed = [sem(f"expert_landed{j}") for j in range(EU)]
        with ExitStack() as tmp:
            eraw = sb("eraw", [P, EU, UNIT], where=tmp)
            run_experts(eraw, landed, place, weight, code, counts)
        combine(weight)


def lay_out(a):
    units = np.zeros((U_END, P, UNIT), np.float32)

    def chunks(w):
        return w.reshape(w.shape[0] // P, P, w.shape[1]).transpose(1, 0, 2)

    units[U_POOL] = a["pool_w"][0].reshape(4, 2, P, 256).transpose(2, 0, 1, 3).reshape(P, UNIT)
    for layer, u0 in ((0, U_FFN0), (1, U_FFN1)):
        for part, w in ((0, a["ffn_w_gate"][layer]), (1, a["ffn_w_up"][layer])):
            v = chunks(w).reshape(P, C, FC // 2, 256)
            units[u0 + part:u0 + FC:2] = v.transpose(2, 0, 1, 3).reshape(FC // 2, P, UNIT)
        v = chunks(a["ffn_w_down"][layer]).reshape(P, FC // 2, UNIT)
        units[u0 + FC:u0 + FFN_UNITS] = v.transpose(1, 0, 2)
    w = chunks(a["mla_w_down"][0])
    units[U_MLA] = w[:, 0:4, 0:512].reshape(P, UNIT)
    units[U_MLA + 1] = w[:, 4:8, 0:512].reshape(P, UNIT)
    units[U_MLA + 2, :, 0:512] = w[:, :, 512:576].reshape(P, 512)
    w = chunks(a["mla_w_uq"][0]).reshape(P, 3, H, 192)
    units[U_MLA + 3, :, 0:1536] = w[:, :, :, 128:192].reshape(P, 1536)
    units[U_MLA + 4, :, 0:1536] = w[:, :, 0:4, 0:128].reshape(P, 1536)
    units[U_MLA + 5, :, 0:1536] = w[:, :, 4:8, 0:128].reshape(P, 1536)
    units[U_MLA + 6] = a["mla_w_ukv"][0].reshape(P, H, 2, P).transpose(0, 2, 1, 3).reshape(P, UNIT)
    units[U_MLA_OUT:U_MLA_OUT + 4] = chunks(a["mla_w_o"][0]).reshape(P, 4, UNIT).transpose(1, 0, 2)
    v = chunks(a["da_w_in_2"][0]).reshape(P, 2, 4, 6, 512)
    units[U_DA:U_DA + 12] = v.transpose(3, 1, 0, 2, 4).reshape(12, P, UNIT)
    units[U_DA_OUT:U_DA_OUT + 4] = chunks(a["da_w_out_2"][0]).reshape(P, 4, UNIT).transpose(1, 0, 2)
    experts = np.zeros((E, EU, P, UNIT), np.float32)
    for part, name in ((0, "moe_w_gate_2"), (2, "moe_w_up_2")):
        v = a[name][0].reshape(E, 2, 4, P, DE)
        experts[:, part:part + 2] = v.transpose(0, 1, 3, 2, 4).reshape(E, 2, P, UNIT)
    v = a["moe_w_down_2"][0].reshape(E, 2, 2, P, D)
    experts[:, 4:6] = v.transpose(0, 1, 3, 2, 4).reshape(E, 2, P, UNIT)
    gains = np.zeros((P, GAIN_WIDTH), np.float32)
    for name, v in (("mix0", a["norm_mix"][0]), ("ffn0", a["norm_ffn"][0]), ("mix1", a["norm_mix"][1]),
                    ("ffn1", a["norm_ffn"][1]), ("mix2", a["norm_mix_2"][0]), ("moe", a["norm_ffn_2"][0]),
                    ("q_lora", a["mla_q_norm"][0]), ("kv_lora", a["mla_kv_norm"][0]),
                    ("da_q", np.concatenate([a["da_q_norm_2"][0]] * 2)),
                    ("da_k", np.concatenate([a["da_k_norm_2"][0]] * 2)), ("da_sub", a["da_subln_2"][0])):
        c, w = GAIN_COLS[name]
        gains[:, c:c + w] = v.reshape(w, P).T
    rows = np.stack([a["pool_scale"][0], a["norm_final"], a["norm_ffn_2"][0]])
    router = np.zeros((P + 1, C, 20), np.float32)
    router[0:P, :, 0:4] = chunks(a["moe_w_group_2"][0])
    router[0:P, :, 4:20] = chunks(a["moe_w_router_2"][0])
    router[P, 0, 0:4] = a["moe_b_group_2"][0]
    router[P, 0, 4:20] = a["moe_b_router_2"][0]
    lams = np.stack([a["da_lambda_q1_2"][0], a["da_lambda_k1_2"][0], a["da_lambda_q2_2"][0], a["da_lambda_k2_2"][0]])
    consts, band = constants()
    return {
        "stream": units, "experts": experts, "x": a["x"][0], "positions": a["positions"][0].reshape(T, P).T,
        "gains": gains, "rows": rows, "lams": lams.reshape(1, 4 * 64), "router": router.reshape(P + 1, C * 20),
        "consts": consts, "band": band,
    }


def kernel(**inputs):
    import concourse.bacc as bacc
    from concourse.bass_utils import run_bass_kernel_spmd

    arrays = {k: np.ascontiguousarray(v) for k, v in lay_out({k: np.asarray(v) for k, v in inputs.items()}).items()}
    nc = bacc.Bacc("TRN2", target_bir_lowering=False, num_devices=1)
    aps = {k: nc.dram_tensor(k, v.shape, mybir.dt.from_np(v.dtype), kind="ExternalInput").ap()
           for k, v in arrays.items()}
    aps["out"] = nc.dram_tensor("out", (S, D), F32, kind="ExternalOutput").ap()
    aps["scratch"] = nc.dram_tensor("scratch", (2 * S, D), F32, kind="Internal").ap()
    build_program(nc, **aps)
    r = run_bass_kernel_spmd(nc, [arrays], core_ids=[0])
    return r.results[0]["out"].reshape(1, S, D)
```
